# Optimizing a Trainium2 kernel written in Bass

```python
import math
import jax, jax.numpy as jnp
from jax import lax
import numpy as np

D_MODEL = 2048
BATCH = 1
SEQ = 256
DEPTH = 2

DIFF_HEADS = 6
DIFF_HD = 64
DIFF_VD = 2 * DIFF_HD
GLA_HEADS = 4
GLA_DK = 64
GLA_DV = 128
GLA_GATE_RANK = 16
GLA_TAU = 16.0
GLA_CHUNK = 64
MLA_HEADS = 6
MLA_Q_RANK = 512
MLA_KV_RANK = 256
MLA_NOPE = 128
MLA_ROPE = 64
MLA_VD = 128
ROPE_THETA = 10000.0
D_FF = 5632
Q_BLOCK = 128
EPS = 1e-6

IN_SPLIT_SIZES = (
    DIFF_HEADS * 2 * DIFF_HD,
    DIFF_HEADS * 2 * DIFF_HD,
    DIFF_HEADS * DIFF_VD,
    GLA_HEADS * GLA_DK,
    GLA_HEADS * GLA_DK,
    GLA_HEADS * GLA_DV,
    GLA_GATE_RANK,
    GLA_HEADS * GLA_DV,
    MLA_Q_RANK,
    MLA_KV_RANK,
    MLA_ROPE,
)
IN_COLS = sum(IN_SPLIT_SIZES)
MIX_WIDTH = DIFF_HEADS * DIFF_VD + GLA_HEADS * GLA_DV + MLA_HEADS * MLA_VD

kernel_name = "hybrid_diffattn_gla_mla_parallel_heads"

def _rmsnorm(x, w):
    xf = x.astype(jnp.float32)
    y = xf * lax.rsqrt(jnp.mean(xf * xf, axis=-1, keepdims=True) + EPS)
    return (y * w.astype(jnp.float32)).astype(x.dtype)

def _split_cols(t, sizes):
    out, off = [], 0
    for s in sizes:
        out.append(t[..., off:off + s])
        off += s
    return out

def _rope(t, positions):
    r = t.shape[-1]
    inv = 1.0 / (ROPE_THETA ** (jnp.arange(0, r, 2, dtype=jnp.float32) / r))
    ang = positions.astype(jnp.float32)[:, :, None, None] * inv
    cos, sin = jnp.cos(ang), jnp.sin(ang)
    tf = t.astype(jnp.float32)
    t1, t2 = tf[..., : r // 2], tf[..., r // 2:]
    return jnp.concatenate([t1 * cos - t2 * sin, t1 * sin + t2 * cos], axis=-1).astype(t.dtype)

def _to_blocks(t):
    b, h, s, d = t.shape
    return t.reshape(b, h, s // Q_BLOCK, Q_BLOCK, d).transpose(2, 0, 1, 3, 4)

def _from_blocks(o):
    nb, b, h, q, d = o.shape
    return o.transpose(1, 2, 0, 3, 4).reshape(b, h, nb * q, d)

def _causal_probs(q_blk, k, blk, scale):
    s = jnp.einsum('bhqd,bhkd->bhqk', q_blk.astype(jnp.float32), k.astype(jnp.float32)) * scale
    q_pos = blk * Q_BLOCK + jnp.arange(q_blk.shape[2])
    k_pos = jnp.arange(k.shape[2])
    s = jnp.where(k_pos[None, :] <= q_pos[:, None], s, -jnp.inf)
    return jax.nn.softmax(s, axis=-1)

def _diff_attention(q1, q2, k1, k2, v, lam):
    scale = DIFF_HD ** -0.5
    nb = q1.shape[2] // Q_BLOCK

    def block(args):
        idx, q1b, q2b = args
        p = _causal_probs(q1b, k1, idx, scale) - lam * _causal_probs(q2b, k2, idx, scale)
        return jnp.einsum('bhqk,bhkd->bhqd', p.astype(v.dtype), v)

    o = lax.map(block, (jnp.arange(nb), _to_blocks(q1), _to_blocks(q2)))
    return _from_blocks(o)

def _causal_attention(q, k, v, scale):
    nb = q.shape[2] // Q_BLOCK

    def block(args):
        idx, qb = args
        p = _causal_probs(qb, k, idx, scale)
        return jnp.einsum('bhqk,bhkd->bhqd', p.astype(v.dtype), v)

    o = lax.map(block, (jnp.arange(nb), _to_blocks(q)))
    return _from_blocks(o)

def _gla_chunked(q, k, v, log_a):
    b, h, s, dk = q.shape
    dv = v.shape[-1]
    c = GLA_CHUNK
    nc = s // c

    def chunks(t):
        return t.astype(jnp.float32).reshape(b, h, nc, c, t.shape[-1]).transpose(2, 0, 1, 3, 4)

    qc, kc, vc = chunks(q), chunks(k), chunks(v)
    bc = jnp.cumsum(chunks(log_a), axis=3)
    causal = jnp.tril(jnp.ones((c, c), dtype=bool))

    def step(state, inp):
        qi, ki, vi, bi = inp
        inter = jnp.einsum('bhcd,bhde->bhce', qi * jnp.exp(bi), state)
        rel = bi[:, :, :, None, :] - bi[:, :, None, :, :]
        decay = jnp.exp(jnp.where(causal[:, :, None], rel, -jnp.inf))
        attn = jnp.einsum('bhid,bhjd,bhijd->bhij', qi, ki, decay)
        intra = jnp.einsum('bhij,bhjd->bhid', attn, vi)
        b_end = bi[:, :, -1:, :]
        state = (jnp.exp(b_end[:, :, 0, :])[..., None] * state
                 + jnp.einsum('bhcd,bhce->bhde', ki * jnp.exp(b_end - bi), vi))
        return state, inter + intra

    state0 = jnp.zeros((b, h, dk, dv), jnp.float32)
    _, out = lax.scan(step, state0, (qc, kc, vc, bc))
    return out.transpose(1, 2, 0, 3, 4).reshape(b, h, s, dv).astype(v.dtype)

def setup_inputs(seed: int = 0) -> dict:
    key = jax.random.key(seed)
    ks = jax.random.split(key, 24)
    f32 = jnp.float32

    def w(k, shape, fan_in):
        return jax.random.normal(k, shape, f32) * (fan_in ** -0.5)

    def gain(k, shape):
        return 1.0 + 0.02 * jax.random.normal(k, shape, f32)

    return {
        "x": jax.random.normal(ks[0], (BATCH, SEQ, D_MODEL), f32),
        "positions": jnp.broadcast_to(jnp.arange(SEQ, dtype=jnp.int32), (BATCH, SEQ)),
        "attn_norm": gain(ks[1], (DEPTH, D_MODEL)),
        "w_in": w(ks[2], (DEPTH, D_MODEL, IN_COLS), D_MODEL),
        "diff_lambda_q1": 0.1 * jax.random.normal(ks[3], (DEPTH, DIFF_HD), f32),
        "diff_lambda_k1": 0.1 * jax.random.normal(ks[4], (DEPTH, DIFF_HD), f32),
        "diff_lambda_q2": 0.1 * jax.random.normal(ks[5], (DEPTH, DIFF_HD), f32),
        "diff_lambda_k2": 0.1 * jax.random.normal(ks[6], (DEPTH, DIFF_HD), f32),
        "diff_subln": gain(ks[7], (DEPTH, DIFF_VD)),
        "gla_gate_w": w(ks[8], (DEPTH, GLA_GATE_RANK, GLA_HEADS * GLA_DK), GLA_GATE_RANK),
        "gla_gate_b": 0.01 * jax.random.normal(ks[9], (DEPTH, GLA_HEADS * GLA_DK), f32),
        "gla_norm": gain(ks[10], (DEPTH, GLA_DV)),
        "mla_q_norm": gain(ks[11], (DEPTH, MLA_Q_RANK)),
        "mla_w_q_b": w(ks[12], (DEPTH, MLA_Q_RANK, MLA_HEADS * (MLA_NOPE + MLA_ROPE)), MLA_Q_RANK),
        "mla_kv_norm": gain(ks[13], (DEPTH, MLA_KV_RANK)),
        "mla_w_kv_b": w(ks[14], (DEPTH, MLA_KV_RANK, MLA_HEADS * (MLA_NOPE + MLA_VD)), MLA_KV_RANK),
        "w_out": w(ks[15], (DEPTH, MIX_WIDTH, D_MODEL), MIX_WIDTH),
        "ffn_norm": gain(ks[16], (DEPTH, D_MODEL)),
        "w_gate": w(ks[17], (DEPTH, D_MODEL, D_FF), D_MODEL),
        "w_up": w(ks[18], (DEPTH, D_MODEL, D_FF), D_MODEL),
        "w_down": w(ks[19], (DEPTH, D_FF, D_MODEL), D_FF),
        "final_norm": gain(ks[20], (D_MODEL,)),
    }

def reference(x, positions, attn_norm, w_in, diff_lambda_q1, diff_lambda_k1, diff_lambda_q2,
              diff_lambda_k2, diff_subln, gla_gate_w, gla_gate_b, gla_norm, mla_q_norm, mla_w_q_b,
              mla_kv_norm, mla_w_kv_b, w_out, ffn_norm, w_gate, w_up, w_down, final_norm):
    f32 = jnp.float32
    b, s, _ = x.shape
    for l in range(DEPTH):
        h = _rmsnorm(x, attn_norm[l])
        proj = jnp.einsum('bsd,de->bse', h, w_in[l])
        (d_q, d_k, d_v, g_q, g_k, g_v, g_r, g_o, m_qa, m_kva, m_kr) = _split_cols(proj, IN_SPLIT_SIZES)

        dq = d_q.reshape(b, s, DIFF_HEADS, 2, DIFF_HD).transpose(0, 2, 3, 1, 4)
        dk = d_k.reshape(b, s, DIFF_HEADS, 2, DIFF_HD).transpose(0, 2, 3, 1, 4)
        dv = d_v.reshape(b, s, DIFF_HEADS, DIFF_VD).transpose(0, 2, 1, 3)
        lam_init = 0.8 - 0.6 * math.exp(-0.3 * l)
        lam = (jnp.exp(jnp.sum(diff_lambda_q1[l].astype(f32) * diff_lambda_k1[l].astype(f32)))
               - jnp.exp(jnp.sum(diff_lambda_q2[l].astype(f32) * diff_lambda_k2[l].astype(f32)))
               + lam_init)
        o_diff = _diff_attention(dq[:, :, 0], dq[:, :, 1], dk[:, :, 0], dk[:, :, 1], dv, lam)
        o_diff = _rmsnorm(o_diff, diff_subln[l]) * (1.0 - lam_init)
        o_diff = o_diff.transpose(0, 2, 1, 3).reshape(b, s, DIFF_HEADS * DIFF_VD)

        gq = g_q.reshape(b, s, GLA_HEADS, GLA_DK).transpose(0, 2, 1, 3) * (GLA_DK ** -0.5)
        gk = g_k.reshape(b, s, GLA_HEADS, GLA_DK).transpose(0, 2, 1, 3)
        gv = g_v.reshape(b, s, GLA_HEADS, GLA_DV).transpose(0, 2, 1, 3)
        gate_logits = jnp.einsum('bsr,re->bse', g_r, gla_gate_w[l]) + gla_gate_b[l]
        log_a = jax.nn.log_sigmoid(gate_logits.astype(f32)) / GLA_TAU
        log_a = log_a.reshape(b, s, GLA_HEADS, GLA_DK).transpose(0, 2, 1, 3)
        o_gla = _rmsnorm(_gla_chunked(gq, gk, gv, log_a), gla_norm[l])
        o_gla = o_gla.transpose(0, 2, 1, 3).reshape(b, s, GLA_HEADS * GLA_DV) * jax.nn.silu(g_o)

        mq = jnp.einsum('bsr,re->bse', _rmsnorm(m_qa, mla_q_norm[l]), mla_w_q_b[l])
        mq = mq.reshape(b, s, MLA_HEADS, MLA_NOPE + MLA_ROPE)
        mq = jnp.concatenate([mq[..., :MLA_NOPE], _rope(mq[..., MLA_NOPE:], positions)], axis=-1)
        mkv = jnp.einsum('bsr,re->bse', _rmsnorm(m_kva, mla_kv_norm[l]), mla_w_kv_b[l])
        mkv = mkv.reshape(b, s, MLA_HEADS, MLA_NOPE + MLA_VD)
        k_rope = jnp.broadcast_to(_rope(m_kr[:, :, None, :], positions), (b, s, MLA_HEADS, MLA_ROPE))
        mk = jnp.concatenate([mkv[..., :MLA_NOPE], k_rope], axis=-1)
        mv = mkv[..., MLA_NOPE:]
        o_mla = _causal_attention(mq.transpose(0, 2, 1, 3), mk.transpose(0, 2, 1, 3),
                                  mv.transpose(0, 2, 1, 3), (MLA_NOPE + MLA_ROPE) ** -0.5)
        o_mla = o_mla.transpose(0, 2, 1, 3).reshape(b, s, MLA_HEADS * MLA_VD)

        mixed = jnp.concatenate([o_diff, o_gla, o_mla], axis=-1)
        x = x + jnp.einsum('bse,ed->bsd', mixed, w_out[l])

        h2 = _rmsnorm(x, ffn_norm[l])
        ff = jax.nn.silu(jnp.einsum('bsd,df->bsf', h2, w_gate[l])) * jnp.einsum('bsd,df->bsf', h2, w_up[l])
        x = x + jnp.einsum('bsf,fd->bsd', ff, w_down[l])
    return _rmsnorm(x, final_norm)


_drawn_inputs = setup_inputs


def setup_inputs(seed=0):
    import zlib

    import numpy as np

    out = dict(_drawn_inputs(seed))
    spreads = {}
    factors = {'diff_subln': 4.107,
     'gla_gate_b': 8.0,
     'gla_norm': 6.468,
     'mla_q_norm': 8.0,
     'mla_kv_norm': 8.0,
     'ffn_norm': 2.921,
     'final_norm': 2.873}
    for name, (base, spread) in spreads.items():
        noise = np.random.default_rng([zlib.crc32(name.encode()), seed]).standard_normal(out[name].shape)
        drawn = base * np.exp(spread * noise) if base else spread * noise
        out[name] = __import__('jax').numpy.asarray(drawn.astype(out[name].dtype))
    for name, factor in factors.items():
        out[name] = (out[name] * factor).astype(out[name].dtype)
    return out
```

```python
from contextlib import ExitStack

import numpy as np

import concourse.bass as bass
from concourse import mybir

F32 = mybir.dt.float32
F32R = mybir.dt.float32r
U8 = mybir.dt.uint8
I32 = mybir.dt.int32
ALU = mybir.AluOpType
ACT = mybir.ActivationFunctionType
AX = mybir.AxisListType

P = 128
D_MODEL, SEQ, DEPTH = 2048, 256, 2
DIFF_HEADS, DIFF_HD, DIFF_VD = 6, 64, 128
GLA_HEADS, GLA_DK, GLA_DV, GLA_RANK, GLA_TAU = 4, 64, 128, 16, 16.0
MLA_HEADS, MLA_Q_RANK, MLA_KV_RANK, MLA_NOPE, MLA_ROPE, MLA_VD = 6, 512, 256, 128, 64, 128
ROPE_THETA, D_FF, EPS = 10000.0, 5632, 1e-6

NT = SEQ // P
KT = D_MODEL // P
FT = D_FF // P
NCH = 512
FF_CHUNKS = D_FF // NCH

C_DV = 2 * DIFF_HEADS * 2 * DIFF_HD
C_GQ = C_DV + DIFF_HEADS * DIFF_VD
C_GK = C_GQ + GLA_HEADS * GLA_DK
C_GV = C_GK + GLA_HEADS * GLA_DK
C_GR = C_GV + GLA_HEADS * GLA_DV
C_GO = C_GR + GLA_RANK
C_QA = C_GO + GLA_HEADS * GLA_DV
C_KVA = C_QA + MLA_Q_RANK
C_KR = C_KVA + MLA_KV_RANK
IN_COLS = C_KR + MLA_ROPE
DIFF_QK = DIFF_HEADS * 2 * DIFF_HD
G3 = 3 * 2 * DIFF_HD

EARLY = [(C_QA, MLA_Q_RANK), (C_KVA, IN_COLS - C_KVA), (C_GQ, NCH), (C_GV, NCH), (C_GR, 272), (C_GR + 272, 256)]
LATE = [(part + g * G3, G3) for g in range(2) for part in (0, DIFF_QK, 2 * DIFF_QK)]

U_MLA = 4 * len(EARLY)
U_LATE = U_MLA + 2 * MLA_HEADS
U_OUT = U_LATE + 4 * len(LATE)
U_FF = U_OUT + 4 * (D_MODEL // NCH)
U_DOWN = U_FF + 8 * FF_CHUNKS
DOWN_KT = [range(4 * u, 4 * u + 4) for u in range(8)] + [range(32 + 3 * u, 35 + 3 * u) for u in range(4)]
UNITS = U_DOWN + len(DOWN_KT) * (D_MODEL // NCH)
QUADS = UNITS // 4
R_MLA = len(EARLY) // 2
R_LATE = R_MLA + MLA_HEADS
R_OUT = R_LATE + len(LATE) // 2
R_FF = R_OUT + 2
R_DOWN = R_FF + FF_CHUNKS
ROUNDS = R_DOWN + 2

OUT_KT = [[6, 7, 8, 9], [10, 11, 12, 13], [14, 15, 0, 1], [2, 3, 4, 5]]

LEVELS = [64, 32, 16, 8, 4, 2, 1, 0]
N_LEVELS = 1 + len(LEVELS)
HEADS = MLA_HEADS + DIFF_HEADS


def hooks():
    at = {}

    def put(n, *steps):
        at.setdefault(n, []).extend(steps)

    for c in range(len(EARLY)):
        put(4 * c + 3, ("evac", c))
    put(7, ("qa_rms", 0))
    put(8, ("qa_scale", 0))
    for b in range(3):
        put(9 + b, ("qa_turn", b))
    put(19, ("gla_turn", 0))
    put(20, ("gla_logits", 0))
    put(21, ("gla_decay", 0))
    put(23, ("gla_silu", 0))
    for i in range(N_LEVELS):
        put(24 + 2 * i + 2, ("level_mm", i))
        put(24 + 2 * i + 2, ("level_prep", i + 1) if i + 1 < N_LEVELS - 1 else ("none", 0))
    at[24] = [("level_prep", 0)] + at.get(24, [])
    for h in range(MLA_HEADS):
        put(U_MLA + 2 * h, ("mla_q", h))
        put(U_MLA + 2 * h + 1, ("mla_kv", h))
    for c in range(len(LATE)):
        put(U_LATE + 4 * c + 3, ("evac", len(EARLY) + c))
    put(36, ("rope", 0))
    put(38, ("rope_turn", 0))
    start = [39 + j for j in range(MLA_HEADS)] + [48, 49, 50, 58, 59, 60]
    for n in range(39, 64):
        for j in range(HEADS):
            if n == start[j] + 2:
                put(n, ("head_out", j))
        for j in range(HEADS):
            if n == start[j] + 1:
                put(n, ("head_turn", j))
        for j in range(HEADS):
            if n == start[j]:
                put(n, ("head_scores", j))
    put(44, ("gla_out", 0))
    put(45, ("gla_rms", 0))
    put(46, ("gla_gated", 0), ("diff_turn", 0))
    put(47, ("diff_turn", 1))
    put(53, ("diff_rms", 0))
    put(54, ("diff_scale", 0))
    at[56] = [("diff_turn", 2)] + at.get(56, [])
    at[57] = [("diff_turn", 3)] + at.get(57, [])
    put(59, ("mix_turn", 6), ("mix_turn", 8))
    put(60, ("mix_turn", 10))
    put(61, ("mix_turn", 12), ("mix_turn", 14))
    put(62, ("mix_turn", 0), ("diff_rms", 1))
    put(63, ("diff_scale", 1))
    put(64, ("mix_turn", 2), ("mix_turn", 4))
    return at


HOOKS = hooks()
BANKS_OF = {"qa_turn": lambda b: [4 + b], "gla_turn": lambda _: [4, 5, 6], "gla_logits": lambda _: [7],
            "level_mm": lambda _: [6, 7], "rope_turn": lambda _: [4, 5],
            "head_scores": lambda j: [6] if j < MLA_HEADS else [6, 7], "head_turn": lambda _: [4],
            "head_out": lambda _: [5], "gla_out": lambda _: [6, 7], "diff_turn": lambda _: [4, 5],
            "mix_turn": lambda kt: [4 + kt // 2 % 2]}


def chunk_round(c):
    return c % 2, c // 2 if c < len(EARLY) else R_LATE + (c - len(EARLY)) // 2


def bank_rounds():
    used = {b: 0 for b in (4, 5, 6, 7)}
    of = {}

    def take(key, banks):
        of[key] = {}
        for b in banks:
            of[key][b] = used[b]
            used[b] += 1

    for r in range(KT // 2):
        take(("norm1", r), [4 + r % 4])
    for n in sorted(HOOKS):
        for step in HOOKS[n]:
            if step[0] in BANKS_OF:
                take(step, BANKS_OF[step[0]](step[1]))
    for r in range(KT // 2):
        take(("norm2", r), [4 + r % 4])
    take(("ff_turn", 0), [4, 5])
    for b in (4, 5):
        used[b] += FF_CHUNKS - 1
    return of, used


ROUND, USES = bank_rounds()
POW = {"norm1": 0, "mla": 1, "gla": 2, "diff0": 3, "diff1": 4, "norm2": 5}

ARENA = 2 * FT * SEQ
A_PD = 0
A_P2 = A_PD + NT * C_GQ
P2 = IN_COLS - C_GQ
A_QNT = A_P2 + NT * P2
A_KNT = A_QNT + MLA_HEADS * SEQ
A_MV = A_KNT + MLA_HEADS * SEQ
A_QRT = A_MV + NT * MLA_HEADS * MLA_VD
A_QR = A_QRT + 4 * SEQ
A_GQT = A_QR + NT * 8 * MLA_ROPE
A_GKT = A_GQT + 2 * SEQ
A_B = A_GKT + 2 * SEQ
A_QL = A_B + 2 * SEQ
A_KL = A_QL + 2 * 2 * SEQ
A_ATT = A_KL + 2 * 2 * SEQ
A_CROSS = A_ATT + 2 * NT * 2 * P
A_E1 = A_CROSS + 2 * 2 * P
A_E2 = A_E1 + 3 * P
A_PT = A_E2 + 3 * P
A_END = A_PT + 3 * P
assert A_END <= ARENA

K_ID, K_INV, K_LAM, K_END = 0, P, P + MLA_ROPE // 2, P + MLA_ROPE // 2 + 2 * DEPTH
G_ATTN, G_FFN, G_QA, G_KVA, G_BIAS, G_END = 0, KT, 2 * KT, 2 * KT + 4, 2 * KT + 6, 2 * KT + 8
W_SUB, W_GLA, W_LAM, W_END = 0, P, 2 * P, 2 * P + 4 * DIFF_HD
NEG = -1e30
ACT_LINKS, VEC_LINKS = 1, 57
TWO_PI = [6.28125, 0.0019350051879882812, 3.0199159819e-07]
ROUNDER = 12582912.0


def program(nc, x, positions, w_in, w_q_b, w_kv_b, w_out, w_gate, w_up, w_down, gate_w, gains, rows,
            final_norm, consts, levels, causal, out):
    with ExitStack() as ctx:
        def sem(name):
            return ctx.enter_context(nc.semaphore(name))

        def sb(name, shape, dt):
            return ctx.enter_context(nc.sbuf_tensor(name, shape, dt))

        arena_at = nc.sbuf_base + (-nc.sbuf_base) % 64
        xt_at = arena_at + 4 * ARENA
        g_at = xt_at + 4 * 2 * KT * SEQ
        sb("slab", [P, (g_at - arena_at) // 4 + NT * NCH], F32)

        def place(name, shape, dt, offset):
            return nc.alloc_sbuf_tensor_at(name, shape, dt, offset=offset)

        def arena(name, shape, dt, word):
            return place(name, shape, dt, arena_at + 4 * word)

        pd = arena("pd", [P, NT, C_GQ], F32, A_PD)
        p2 = arena("p2", [P, NT, P2], F32, A_P2)
        qa_hi = arena("qa_hi", [P, 6, SEQ], F32R, A_PD)
        qa_lo = arena("qa_lo", [P, 6, SEQ], F32R, A_PD + 6 * SEQ)
        turn1, turn2, turn3, turn4 = (arena(f"rope_product{i}", [P, NT, 7, 32], F32, A_PD + 448 * i) for i in range(4))
        qnt = arena("qnt", [P, MLA_HEADS, SEQ], F32, A_QNT)
        knt = arena("knt", [P, MLA_HEADS, SEQ], F32, A_KNT)
        mv = arena("mv", [P, NT, MLA_HEADS, MLA_VD], F32, A_MV)
        levels_in = arena("levels_in", [P, len(LEVELS), P], F32, A_QNT)
        qrt = arena("qrt", [P, 4, SEQ], F32, A_QRT)
        qr = arena("qr", [P, NT, 8, MLA_ROPE], F32, A_QR)
        gqt = arena("gqt", [P, 2, SEQ], F32, A_GQT)
        gkt = arena("gkt", [P, 2, SEQ], F32, A_GKT)
        dqt = arena("dqt", [P, 3, SEQ], F32, A_QR)
        dkt = arena("dkt", [P, 3, SEQ], F32, A_QR + 3 * SEQ)
        logs = arena("logs", [P, 2, SEQ], F32, A_B)
        ql = arena("ql", [P, 2, 2, SEQ], F32, A_QL)
        kl = arena("kl", [P, 2, 2, SEQ], F32, A_KL)
        grt = arena("grt", [GLA_RANK, SEQ], F32, A_QL)
        squares = arena("squares", [P, NT, 4, P], F32, A_QL)
        att = arena("att", [P, 2, NT, 2, P], F32, A_ATT)
        cross = arena("cross", [P, 2, 2, P], F32, A_CROSS)
        gate_z = arena("gate_z", [P, 2, SEQ], F32, A_ATT)
        gate_e = arena("gate_e", [P, 2, SEQ], F32, A_ATT + 2 * SEQ)
        ones = arena("ones", [P, SEQ], F32, A_CROSS)
        e1 = arena("e1", [P, 3 * P], F32, A_E1)
        e2 = arena("e2", [P, 3 * P], F32, A_E2)
        pt = arena("pt", [P, 3 * P], F32, A_PT)
        xn = arena("xn", [P, NT, D_MODEL], F32, 0)
        f_hi = arena("f_hi", [P, FT, SEQ], F32R, 0)
        f_lo = arena("f_lo", [P, FT, SEQ], F32R, FT * SEQ)
        xt_hi = place("xt_hi", [P, KT, SEQ], F32R, xt_at)
        xt_lo = place("xt_lo", [P, KT, SEQ], F32R, xt_at + 4 * KT * SEQ)
        last_gain = place("last_gain", [P, D_MODEL], F32, xt_at)
        row_sb = place("row_sb", [P, W_END], F32, g_at)
        gw_sb = place("gw_sb", [GLA_RANK, GLA_HEADS * GLA_DK], F32, g_at + 4 * W_END)
        small_at = g_at + 4 * (W_END + GLA_HEADS * GLA_DK)
        m_ss = place("m_ss", [P, 4], F32, small_at)
        rsum = place("rsum", [P, 4], F32, small_at + 32)
        held = place("held", [P, 2 * MLA_HEADS], F32, small_at + 64)
        lam2 = place("lam2", [P, 2], F32, small_at + 128)
        lam2e = place("lam2e", [P, 2], F32, small_at + 160)
        lam = place("lam", [P, 1], F32, small_at + 192)
        junk = place("junk", [P, NCH], F32, g_at)
        act_sb = place("act_sb", [P, NT, NCH], F32, g_at)

        resid = sb("resid", [P, NT, D_MODEL], F32)
        stage = [sb(f"stage{i}", [P, 4 * NCH], F32) for i in range(4)]
        w_hi = [sb(f"w_hi{i}", [P, 4 * NCH], F32R) for i in range(2)]
        w_lo = [sb(f"w_lo{i}", [P, 4 * NCH], F32R) for i in range(2)]
        k_sb = sb("k_sb", [P, K_END], F32)
        gain_sb = sb("gain_sb", [P, DEPTH, G_END], F32)
        lev_sb = sb("lev_sb", [P, len(LEVELS), P], U8)
        caus_sb = sb("caus_sb", [P, 2 * P], F32)
        cos_sb = sb("cos_sb", [P, NT, 1, 32], F32)
        sin_sb = sb("sin_sb", [P, NT, 1, 32], F32)
        pos_i = sb("pos_i", [P, NT], I32)
        pos_f = sb("pos_f", [P, NT], F32)
        ssq = sb("ssq", [P, NT, 4], F32)
        ms = sb("ms", [P, 8], F32)
        rstd = sb("rstd", [P, 8], F32)
        halves = sb("halves", [P, 8], F32)
        mx = sb("mx", [P, 4], F32)
        nmx = sb("nmx", [P, 4], F32)
        esum = sb("esum", [P, 4], F32)

        ident = k_sb[:, K_ID:K_ID + P]
        bank = [ctx.enter_context(nc.psum_tensor(f"bank{i}", [P, NCH], F32)) for i in range(8)]

        full = [sem(f"full{s}") for s in range(4)]
        hi_made = [sem(f"hi_made{s}") for s in range(4)]
        lo_made = [sem(f"lo_made{s}") for s in range(4)]
        used = [sem(f"used{s}") for s in range(4)]
        acc_out_act = [sem(f"acc_out_act{p}") for p in range(2)]
        acc_out_vec = [sem(f"acc_out_vec{p}") for p in range(2)]
        bank_full = {b: sem(f"bank_full{b}") for b in USES}
        bank_free = {b: sem(f"bank_free{b}") for b in USES}
        setup_in, rows_in, halves_made = sem("setup_in"), sem("rows_in"), sem("halves_made")
        consts_in, x_in = sem("consts_in"), sem("x_in")
        squared = sem("squared")
        x_added = sem("x_added")
        ms_made, rstd_made = sem("ms_made"), sem("rstd_made")
        xn_act, xn_vec = sem("xn_act"), sem("xn_vec")
        xt_hi_made = sem("xt_hi_made")
        m_squared, qa_scaled = sem("m_squared"), sem("qa_scaled")
        qa_hi_made = sem("qa_hi_made")
        roped, rope_mul = sem("roped"), sem("rope_mul")
        kr_in = sem("kr_in")
        gate_neg, gate_ln, gate_silu = sem("gate_neg"), sem("gate_ln"), sem("gate_silu")
        span_made, decay_made, level_made = sem("span_made"), sem("decay_made"), sem("level_made")
        gla_mixed, diff_mixed = sem("gla_mixed"), sem("diff_mixed")
        masked, exped, probs_made = sem("masked"), sem("exped"), sem("probs_made")
        lam_dot, lam_exp = sem("lam_dot"), sem("lam_exp")
        silu_made, act_made, ft_hi_made = sem("silu_made"), sem("act_made"), sem("ft_hi_made")
        angles, waves, angles_chain = sem("angles"), sem("waves"), sem("angles_chain")
        act_chain, vec_chain = sem("act_chain"), sem("vec_chain")
        out_made, stored = sem("out_made"), sem("stored")

        def p2c(t, col, n):
            return p2[:, t, col - C_GQ:col - C_GQ + n]

        def projected(t, col, n):
            return pd[:, t, col:col + n] if col < C_GQ else p2c(t, col, n)

        def unit_shape(n):
            n %= UNITS
            if n < U_MLA:
                return 4, EARLY[n // 4][1]
            if n < U_LATE:
                return (4, MLA_NOPE + MLA_ROPE) if n % 2 == 0 else (2, MLA_NOPE + MLA_VD)
            if n < U_OUT:
                return 4, LATE[(n - U_LATE) // 4][1]
            if n < U_DOWN:
                return 4, NCH
            return len(DOWN_KT[(n - U_DOWN) % len(DOWN_KT)]), NCH

        block = ctx.enter_context(nc.Block())

        @block.sync
        def _(sp):
            sp.dma_start(k_sb[:, :], consts).then_inc(consts_in, 16)
            sp.dma_start(resid[:, :, :], x.rearrange("(t p) d -> p t d", p=P)).then_inc(x_in, 16)
            sp.dma_start(gain_sb[:, :, :], gains).then_inc(setup_in, 16)
            sp.dma_start(pos_i[:, :], positions).then_inc(setup_in, 16)
            sp.dma_start(levels_in[:, :, :], levels).then_inc(setup_in, 16)
            sp.dma_start(caus_sb[:, :], causal).then_inc(setup_in, 16)

            def load(quad, n, sources, second_first=False):
                s = n % 4
                kts, cols = unit_shape(n)
                view = stage[s][:, 0:kts * cols].rearrange("p (k n) -> p k n", k=kts)
                sp.wait_ge(lo_made[s], quad + 1)
                parts = []
                for src in sources:
                    at, m = sum(n_rows for _, n_rows, _ in parts), src.shape[0] // P
                    parts.append((at, m, src))
                for at, m, src in reversed(parts) if second_first else parts:
                    sp.dma_start(view[:, at:at + m, :], src.rearrange("(k p) n -> p k n", p=P)).then_inc(full[s], 16)

            def halves_of(w, layer, kts, col, cols):
                kts = list(kts)
                cut = (len(kts) + 1) // 2
                return [w[layer, part[0] * P:(part[-1] + 1) * P, bass.ds(col, cols)] for part in (kts[:cut], kts[cut:])]

            with sp.Fori(0, DEPTH) as layer:
                def quad(n):
                    return layer * QUADS + n // 4

                for n in range(U_MLA):
                    col, cols = EARLY[n // 4]
                    load(quad(n), n, halves_of(w_in, layer, range(4 * (n % 4), 4 * (n % 4) + 4), col, cols))
                    if n == 7:
                        sp.wait_ge(squared, layer * 16 + 8)
                        sp.dma_start(row_sb[:, :], rows[layer].to_broadcast([P, W_END])).then_inc(rows_in, 16)
                        sp.dma_start(gw_sb[:, :], gate_w[layer]).then_inc(rows_in, 16)
                for h in range(MLA_HEADS):
                    n = U_MLA + 2 * h
                    load(quad(n), n, halves_of(w_q_b, layer, range(4), 192 * h, 192))
                    load(quad(n + 1), n + 1, halves_of(w_kv_b, layer, range(2), 256 * h, 256))
                for n in range(U_LATE, U_OUT):
                    i = n - U_LATE
                    col, cols = LATE[i // 4]
                    load(quad(n), n, halves_of(w_in, layer, range(4 * (i % 4), 4 * (i % 4) + 4), col, cols), i == 0)
                for pair in range(2):
                    for i in range(8):
                        n = U_OUT + 8 * pair + i
                        load(quad(n), n, [part for kts in (OUT_KT[i // 2][:2], OUT_KT[i // 2][2:])
                                          for part in [w_out[layer, kts[0] * P:(kts[1] + 1) * P,
                                                             bass.ds((2 * pair + i % 2) * NCH, NCH)]]])
                with sp.Fori(0, FF_CHUNKS) as f:
                    for i in range(8):
                        w = w_gate if i < 4 else w_up
                        load(quad(U_FF + i) + 2 * f, U_FF + i,
                             halves_of(w, layer, range(4 * (i % 4), 4 * (i % 4) + 4), f * NCH, NCH))
                for c in range(4):
                    for i, kts in enumerate(DOWN_KT):
                        n = U_DOWN + len(DOWN_KT) * c + i
                        load(quad(n), n, halves_of(w_down, layer, kts, c * NCH, NCH))
            for n in range(2):
                load(DEPTH * QUADS, n, halves_of(w_in, 0, range(4 * n, 4 * n + 4), EARLY[0][0], EARLY[0][1]))
            sp.wait_ge(act_made, DEPTH * FF_CHUNKS * NT)
            sp.dma_start(last_gain[:, :], final_norm.to_broadcast([P, D_MODEL])).then_inc(setup_in, 16)
            for t in range(NT):
                sp.wait_ge(out_made, t + 1)
                sp.dma_start(out[t * P:(t + 1) * P, :], xn[:, t, :]).then_inc(stored, 16)
            sp.wait_ge(stored, 16 * NT)

        @block.tensor
        def _(pe):
            pe.wait_ge(consts_in, 16)
            with pe.Fori(0, DEPTH) as layer:
                def need(s, per_layer, k):
                    pe.wait_ge(s, layer * per_layer + k)

                def bank_taken(key, b):
                    need(bank_free[b], USES[b], ROUND[key][b] + 1)
                    return bank[b]

                def copied(key, b):
                    need(bank_free[b], USES[b], ROUND[key][b] + 2)

                def projected_by_now(chunks):
                    parity, r = chunk_round(chunks - 1)
                    need(acc_out_act[parity], R_OUT, r + 1)
                    need(acc_out_vec[parity], R_OUT, r + 1)

                def transpose(dst, src):
                    return pe.transpose(dst, src, ident)

                def unit(n, kts, parity, hi, lo, first, last, turn=0):
                    s = n % 4
                    _, cols = unit_shape(n)
                    pe.wait_ge(lo_made[s], layer * QUADS + n // 4 + 2 + turn)
                    wh = w_hi[s % 2][:, 0:len(kts) * cols].rearrange("p (k n) -> p k n", n=cols)
                    wl = w_lo[s % 2][:, 0:len(kts) * cols].rearrange("p (k n) -> p k n", n=cols)
                    for i, kt in enumerate(kts):
                        for t in range(NT):
                            acc = bank[2 * parity + t][:, 0:cols]
                            a = hi[:, kt, t * P:(t + 1) * P]
                            b = lo[:, kt, t * P:(t + 1) * P]
                            pe.matmul(acc, a, wh[:, i, :], start=first and i == 0, stop=False)
                            pe.matmul(acc, a, wl[:, i, :], start=False, stop=False)
                            mm = pe.matmul(acc, b, wh[:, i, :], start=False, stop=last and i == len(kts) - 1)
                    mm.then_inc(used[s], 1)

                def acc_taken(parity, r, in_loop=False, f=0):
                    if r == 0:
                        return
                    if r <= R_OUT:
                        need(acc_out_act[parity], R_OUT, r)
                        need(acc_out_vec[parity], R_OUT, r)
                    elif r < R_FF or r == R_FF and not in_loop:
                        need(x_added, 16, NT * (2 * (r - 1 - R_OUT) + parity + 1))
                    elif r == R_FF:
                        need((silu_made, act_made)[parity], FF_CHUNKS * NT, NT * f)
                    elif r == R_DOWN:
                        need((silu_made, act_made)[parity], FF_CHUNKS * NT, NT * FF_CHUNKS)
                    else:
                        need(x_added, 16, 8 + NT * (parity + 1))

                def norm_turn(which, seen):
                    for r in range(KT // 2):
                        need(xn_act, 8, seen * 4 + r // 2 + 1)
                        need(xn_vec, 8, seen * 4 + r // 2 + 1)
                        b = 4 + r % 4
                        ps = bank_taken((which, r), b)
                        for i in range(2):
                            for t in range(NT):
                                kt = 2 * r + i
                                mm = transpose(ps[:, i * SEQ + t * P:i * SEQ + (t + 1) * P], xn[:, t, kt * P:(kt + 1) * P])
                        mm.then_inc(bank_full[b], 1)

                def qa_turn(b):
                    need(qa_scaled, 1, 1)
                    ps = bank_taken(("qa_turn", b), 4 + b)
                    for i in range(2):
                        for t in range(NT):
                            mm = transpose(ps[:, i * SEQ + t * P:i * SEQ + (t + 1) * P],
                                           p2c(t, C_QA + (2 * b + i) * P, P))
                    mm.then_inc(bank_full[4 + b], 1)

                def mla_unit(h, kv):
                    n = U_MLA + 2 * h + kv
                    s, (kts, cols) = n % 4, unit_shape(n)
                    if h == 0:
                        for b in range(3):
                            copied(("qa_turn", b), 4 + b)
                    pe.wait_ge(lo_made[s], layer * QUADS + n // 4 + 2)
                    acc_taken(kv, R_MLA + h)
                    wh = w_hi[s % 2][:, 0:kts * cols].rearrange("p (k n) -> p k n", n=cols)
                    wl = w_lo[s % 2][:, 0:kts * cols].rearrange("p (k n) -> p k n", n=cols)
                    ps, k0 = bank[2 * kv], 4 * kv
                    for k in range(kts):
                        a, b = wh[:, k, 0:P], wl[:, k, 0:P]
                        pe.matmul(ps[:, 0:SEQ], a, qa_hi[:, k0 + k, :], start=k == 0, stop=False)
                        pe.matmul(ps[:, 0:SEQ], a, qa_lo[:, k0 + k, :], start=False, stop=False)
                        pe.matmul(ps[:, 0:SEQ], b, qa_hi[:, k0 + k, :], start=False, stop=k == kts - 1)
                    w = cols - P
                    for t in range(NT):
                        dst = ps[:, SEQ + t * w:SEQ + (t + 1) * w]
                        for k in range(kts):
                            a = qa_hi[:, k0 + k, t * P:(t + 1) * P]
                            b = qa_lo[:, k0 + k, t * P:(t + 1) * P]
                            pe.matmul(dst, a, wh[:, k, P:cols], start=k == 0, stop=False)
                            pe.matmul(dst, a, wl[:, k, P:cols], start=False, stop=False)
                            mm = pe.matmul(dst, b, wh[:, k, P:cols], start=False, stop=k == kts - 1)
                    mm.then_inc(used[s], 1)

                def gla_turn(_):
                    projected_by_now(5)
                    for b, col in ((4, C_GQ), (5, C_GK)):
                        ps = bank_taken(("gla_turn", 0), b)
                        for g in range(2):
                            for t in range(NT):
                                mm = transpose(ps[:, g * SEQ + t * P:g * SEQ + (t + 1) * P], p2c(t, col + g * P, P))
                        mm.then_inc(bank_full[b], 1)
                    ps = bank_taken(("gla_turn", 0), 6)
                    for t in range(NT):
                        mm = transpose(ps[:, t * P:(t + 1) * P], p2c(t, C_GR, P))
                    mm.then_inc(bank_full[6], 1)

                def gla_logits(_):
                    copied(("gla_turn", 0), 6)
                    need(rows_in, 32, 32)
                    ps = bank_taken(("gla_logits", 0), 7)
                    for g in range(2):
                        mm = pe.matmul(ps[:, g * SEQ:(g + 1) * SEQ], gw_sb[:, g * P:(g + 1) * P], grt[:, :],
                                       start=True, stop=True)
                    mm.then_inc(bank_full[7], 1)

                def level_mm(i):
                    if i == 0:
                        copied(("gla_turn", 0), 4)
                        copied(("gla_turn", 0), 5)
                    if i < N_LEVELS - 1:
                        need(level_made, N_LEVELS - 1, i + 1)
                    q, k = (gqt, gkt) if i == N_LEVELS - 1 else (ql[:, i % 2], kl[:, i % 2])
                    for par in range(2):
                        ps = bank_taken(("level_mm", i), 6 + par)
                        rows_ = slice(par * 64, par * 64 + 64)
                        for g in range(2):
                            if i == 0:
                                mm = pe.matmul(ps[:, g * P:(g + 1) * P], k[rows_, g, 0:P], q[rows_, g, P:SEQ],
                                               start=True, stop=True)
                                continue
                            for t in range(NT):
                                at = (t * 2 + g) * P
                                mm = pe.matmul(ps[:, at:at + P], k[rows_, g, t * P:(t + 1) * P],
                                               q[rows_, g, t * P:(t + 1) * P], start=True, stop=True)
                        mm.then_inc(bank_full[6 + par], 1)

                def gla_out(_):
                    copied(("level_mm", N_LEVELS - 1), 7)
                    for t in range(NT):
                        ps = bank_taken(("gla_out", 0), 6 + t)
                        for h in range(GLA_HEADS):
                            dst, par, g = ps[:, h * P:(h + 1) * P], h % 2, h // 2
                            if t == 1:
                                pe.matmul(dst, cross[:, par, g, :], p2c(0, C_GV + h * P, P), start=True, stop=False)
                            mm = pe.matmul(dst, att[:, par, t, g, :], p2c(t, C_GV + h * P, P), start=t == 0, stop=True)
                        mm.then_inc(bank_full[6 + t], 1)

                def rope_turn(_):
                    need(roped, 1, 1)
                    for b in range(2):
                        ps = bank_taken(("rope_turn", 0), 4 + b)
                        for i in range(2):
                            for t in range(NT):
                                pair = 2 * b + i
                                mm = transpose(ps[:, i * SEQ + t * P:i * SEQ + (t + 1) * P],
                                               qr[:, t, 2 * pair:2 * pair + 2, :].rearrange("p a b -> p (a b)"))
                        mm.then_inc(bank_full[4 + b], 1)

                def diff_turn(i):
                    g, part = i // 2, i % 2
                    projected_by_now(7 + 3 * g + part)
                    for b, heads in ((4, (0, 1)), (5, (2,))):
                        ps = bank_taken(("diff_turn", i), b)
                        for k, h in enumerate(heads):
                            for t in range(NT):
                                col = part * DIFF_QK + (3 * g + h) * P
                                mm = transpose(ps[:, k * SEQ + t * P:k * SEQ + (t + 1) * P], pd[:, t, col:col + P])
                        mm.then_inc(bank_full[b], 1)

                def head_scores(j):
                    key = ("head_scores", j)
                    if j < MLA_HEADS:
                        if j == 0:
                            copied(("rope_turn", 0), 4)
                            copied(("rope_turn", 0), 5)
                            for parity in range(2):
                                need(acc_out_act[parity], R_OUT, R_LATE)
                        ps = bank_taken(key, 6)
                        r = slice(64 * (j % 2), 64 * (j % 2) + 64)
                        for t in range(NT):
                            dst = ps[:, t * P:t * P + (t + 1) * P]
                            n = (t + 1) * P
                            pe.matmul(dst, qnt[:, j, t * P:n], knt[:, j, 0:n], start=True, stop=False)
                            mm = pe.matmul(dst, qrt[r, j // 2, t * P:n], qrt[r, 3, 0:n], start=False, stop=True)
                        mm.then_inc(bank_full[6], 1)
                        return
                    h = j - MLA_HEADS
                    copied(("diff_turn", 2 * (h // 3) + 1), 4)
                    copied(("diff_turn", 2 * (h // 3) + 1), 5)
                    for branch in range(2):
                        ps = bank_taken(key, 6 + branch)
                        r = slice(64 * branch, 64 * branch + 64)
                        for t in range(NT):
                            n = (t + 1) * P
                            mm = pe.matmul(ps[:, t * P:t * P + n], dqt[r, h % 3, t * P:n], dkt[r, h % 3, 0:n],
                                           start=True, stop=True)
                        mm.then_inc(bank_full[6 + branch], 1)

                def head_turn(j):
                    if j < MLA_HEADS:
                        need(exped, HEADS, j + 1)
                    else:
                        need(probs_made, DIFF_HEADS, j - MLA_HEADS + 1)
                    ps = bank_taken(("head_turn", j), 4)
                    for i in range(3):
                        mm = transpose(ps[:, i * P:(i + 1) * P], e1[:, i * P:(i + 1) * P])
                    mm.then_inc(bank_full[4], 1)

                def head_out(j):
                    copied(("head_turn", j), 4)
                    if j == 0:
                        need(acc_out_vec[1], R_OUT, R_LATE)
                    if j in (MLA_HEADS, MLA_HEADS + 3):
                        projected_by_now(9 + 3 * ((j - MLA_HEADS) // 3))

                    def v(t):
                        if j < MLA_HEADS:
                            return mv[:, t, j, :]
                        return pd[:, t, C_DV + (j - MLA_HEADS) * P:C_DV + (j - MLA_HEADS + 1) * P]

                    ps = bank_taken(("head_out", j), 5)
                    pe.matmul(ps[:, 0:P], pt[:, 0:P], v(0), start=True, stop=True)
                    pe.matmul(ps[:, P:2 * P], pt[:, P:2 * P], v(0), start=True, stop=False)
                    pe.matmul(ps[:, P:2 * P], pt[:, 2 * P:3 * P], v(1), start=False, stop=True).then_inc(bank_full[5], 1)

                def mix_turn(kt0):
                    b = 4 + kt0 // 2 % 2
                    if kt0 in (6, 8):
                        need(gla_mixed, 1, 1)
                    elif kt0 >= 10:
                        if b != 5:
                            copied(("head_out", kt0 - 10 + 1), 5)
                    else:
                        need(diff_mixed, 2, 2 if kt0 else 1)
                    ps = bank_taken(("mix_turn", kt0), b)
                    for i in range(2):
                        for t in range(NT):
                            kt = kt0 + i
                            src = (pd[:, t, C_DV + kt * P:C_DV + (kt + 1) * P] if kt < 6 else
                                   p2c(t, C_GV + (kt - 6) * P, P) if kt < 10 else mv[:, t, kt - 10, :])
                            mm = transpose(ps[:, i * SEQ + t * P:i * SEQ + (t + 1) * P], src)
                    mm.then_inc(bank_full[b], 1)

                steps = {"qa_turn": qa_turn, "gla_turn": gla_turn, "gla_logits": gla_logits, "level_mm": level_mm,
                         "gla_out": gla_out, "rope_turn": rope_turn, "diff_turn": diff_turn, "head_scores": head_scores,
                         "head_turn": head_turn, "head_out": head_out, "mix_turn": mix_turn}

                def hook(n):
                    for name, arg in HOOKS.get(n, []):
                        if name in steps:
                            steps[name](arg)

                norm_turn("norm1", 0)
                for c in range(len(EARLY)):
                    acc_taken(c % 2, c // 2)
                    for u in range(4):
                        if c == 0:
                            for r in (2 * u, 2 * u + 1):
                                copied(("norm1", r), 4 + r % 4)
                        n = 4 * c + u
                        unit(n, range(4 * u, 4 * u + 4), c % 2, xt_hi, xt_lo, u == 0, u == 3)
                        hook(n)
                for h in range(MLA_HEADS):
                    for kv in range(2):
                        mla_unit(h, kv)
                        hook(U_MLA + 2 * h + kv)
                for c in range(len(LATE)):
                    acc_taken(c % 2, R_LATE + c // 2)
                    for u in range(4):
                        n = U_LATE + 4 * c + u
                        unit(n, range(4 * u, 4 * u + 4), c % 2, xt_hi, xt_lo, u == 0, u == 3)
                        hook(n)
                for pair in range(2):
                    acc_taken(0, R_OUT + pair)
                    acc_taken(1, R_OUT + pair)
                    for i in range(8):
                        if pair == 0 and i % 2 == 0:
                            for kt0 in {kt - kt % 2 for kt in OUT_KT[i // 2]}:
                                copied(("mix_turn", kt0), 4 + kt0 // 2 % 2)
                        n = U_OUT + 8 * pair + i
                        unit(n, OUT_KT[i // 2], i % 2, xt_hi, xt_lo, i < 2, i >= 6)
                        hook(n)
                norm_turn("norm2", 1)

                def ff_turn(f):
                    pe.wait_ge(act_made, layer * (FF_CHUNKS * NT) + NT * f + NT)
                    for b in (4, 5):
                        pe.wait_ge(bank_free[b], layer * USES[b] + ROUND[("ff_turn", 0)][b] + f + 1)
                        for i in range(2):
                            for t in range(NT):
                                j = 2 * (b - 4) + i
                                mm = transpose(bank[b][:, i * SEQ + t * P:i * SEQ + (t + 1) * P],
                                               act_sb[:, t, j * P:(j + 1) * P])
                        mm.then_inc(bank_full[b], 1)

                def ff_chunk(f, first):
                    for half in range(2):
                        acc_taken(half, R_FF, not first, f)
                        for u in range(4):
                            if first and half == 0:
                                for r in (2 * u, 2 * u + 1):
                                    copied(("norm2", r), 4 + r % 4)
                            unit(U_FF + 4 * half + u, range(4 * u, 4 * u + 4), half, xt_hi, xt_lo, u == 0, u == 3,
                                 turn=2 * f)
                            if half == 0 and u == 1 and not first:
                                ff_turn(f - 1)

                ff_chunk(0, True)
                with pe.Fori(1, FF_CHUNKS) as f:
                    ff_chunk(f, False)
                for c in range(4):
                    acc_taken(c % 2, R_DOWN + c // 2)
                    for i, kts in enumerate(DOWN_KT):
                        if c == 0 and i in (0, 10):
                            for b in (4, 5):
                                need(bank_free[b], USES[b], USES[b] + (i != 0))
                        unit(U_DOWN + len(DOWN_KT) * c + i, kts, c % 2, f_hi, f_lo, i == 0, i == len(DOWN_KT) - 1)
                        if c == 0 and i == 1:
                            ff_turn(FF_CHUNKS - 1)

        @block.scalar
        def _(act):
            count = [0]

            def link(ins):
                count[0] += 1
                ins.then_inc(act_chain, 1)
                return count[0]

            act.wait_ge(x_in, 16)
            for t in range(NT):
                for c in range(4):
                    if t + c:
                        act.wait_ge(squared, 4 * t + c)
                    act.activation(junk[:, :], resid[:, t, c * NCH:(c + 1) * NCH], ACT.Square,
                                   accum_out=ssq[:, t, c:c + 1]).then_inc(squared, 1)
            act.wait_ge(angles, 1)
            act.activation(sin_sb[:, :, 0, :], sin_sb[:, :, 0, :], ACT.Sin).then_inc(waves, 1)
            act.activation(cos_sb[:, :, 0, :], cos_sb[:, :, 0, :], ACT.Sin).then_inc(waves, 1)

            def round_unit(quad, n):
                s = n % 4
                kts, cols = unit_shape(n)
                act.wait_ge(full[s], (quad + 1) * 32)
                act.wait_ge(used[(s + 2) % 4], quad + (1 if s >= 2 else 0))
                act.activation(w_hi[s % 2][:, 0:kts * cols], stage[s][:, 0:kts * cols], ACT.Copy).then_inc(hi_made[s], 1)

            round_unit(0, 0)
            round_unit(0, 1)
            act.wait_ge(setup_in, 64)

            with act.Fori(0, DEPTH) as layer:
                def need(s, per_layer, k):
                    act.wait_ge(s, layer * per_layer + k)

                def bank_in(key, b):
                    need(bank_full[b], USES[b], ROUND[key][b] + 1)
                    return bank[b]

                def complete(n):
                    need(used[n % 4], QUADS, n // 4 + 1)

                def gain(i):
                    return gain_sb[:, bass.ds(layer, 1), i:i + 1].rearrange("p a b -> p (a b)")

                def norm(which, seen):
                    need(rstd_made, len(POW), POW[which] + 1)
                    for q in range(4):
                        act.activation(xn[:, 1, q * NCH:(q + 1) * NCH], resid[:, 1, q * NCH:(q + 1) * NCH], ACT.Copy,
                                       scale=rstd[:, 1:2]).then_inc(xn_act, 1)
                    g0 = G_ATTN if which == "norm1" else G_FFN
                    for r in range(KT // 2):
                        ps = bank_in((which, r), 4 + r % 4)
                        for i in range(2):
                            act.activation(xt_hi[:, 2 * r + i, :], ps[:, i * SEQ:(i + 1) * SEQ], ACT.Copy,
                                           scale=gain(g0 + 2 * r + i)).then_inc(xt_hi_made, 1)

                def evac(c):
                    col, cols = (EARLY + LATE)[c]
                    complete(4 * c + 3 if c < len(EARLY) else U_LATE + 4 * (c - len(EARLY)) + 3)
                    act.activation(projected(0, col, cols), bank[2 * (c % 2)][:, 0:cols], ACT.Copy)\
                       .then_inc(acc_out_act[c % 2], 1)

                def qa_rms(_):
                    need(acc_out_vec[1], R_OUT, 1)
                    need(acc_out_act[1], R_OUT, 1)
                    for t in range(NT):
                        for i, (col, n) in enumerate(((C_QA, MLA_Q_RANK), (C_KVA, MLA_KV_RANK))):
                            at, m = 4 * i + t * n // SEQ, n // SEQ
                            act.activation(qnt[:, at:at + m, :].rearrange("p a b -> p (a b)"), p2c(t, col, n), ACT.Square,
                                           accum_out=m_ss[:, 2 * i + t:2 * i + t + 1]).then_inc(m_squared, 1)

                def qa_turn(b):
                    ps = bank_in(("qa_turn", b), 4 + b)
                    for i in range(2):
                        act.activation(qa_hi[:, 2 * b + i, :], ps[:, i * SEQ:(i + 1) * SEQ], ACT.Copy,
                                       scale=gain(G_QA + 2 * b + i)).then_inc(qa_hi_made, 1)

                def mla_q(h):
                    complete(U_MLA + 2 * h)
                    act.activation(qnt[:, h, :], bank[0][:, 0:SEQ], ACT.Copy).then_inc(acc_out_act[0], 1)

                def mla_kv(h):
                    complete(U_MLA + 2 * h + 1)
                    act.activation(knt[:, h, :], bank[2][:, 0:SEQ], ACT.Copy).then_inc(acc_out_act[1], 1)

                def gla_turn(_):
                    ps = bank_in(("gla_turn", 0), 6)
                    act.activation(grt[:, :], ps[0:GLA_RANK, 0:SEQ], ACT.Copy).then_inc(bank_free[6], 1)
                    ps = bank_in(("gla_turn", 0), 4)
                    act.activation(gqt[:, :, :].rearrange("p a b -> p (a b)"), ps[:, :], ACT.Copy,
                                   scale=GLA_DK ** -0.5).then_inc(bank_free[4], 1)

                def gla_decay(_):
                    need(gate_neg, 1, 1)
                    link(act.activation(gate_e[:, :, :], gate_e[:, :, :], ACT.Exp))
                    need(act_chain, ACT_LINKS, count[0])
                    act.activation(gate_e[:, :, :], gate_e[:, :, :], ACT.Ln, bias=1.0).then_inc(gate_ln, 1)

                def gla_silu(_):
                    need(acc_out_vec[1], R_OUT, 3)
                    need(acc_out_act[1], R_OUT, 3)
                    for t in range(NT):
                        act.activation(p2c(t, C_GO, NCH), p2c(t, C_GO, NCH), ACT.Silu).then_inc(gate_silu, 1)

                def level_prep(i):
                    need(span_made, N_LEVELS - 1, i + 1)
                    act.activation(p2[:, :, 0:SEQ], p2[:, :, 0:SEQ], ACT.Exp, scale=1.0 / GLA_TAU).then_inc(decay_made, 1)

                def rope_turn(_):
                    ps = bank_in(("rope_turn", 0), 4)
                    act.activation(qrt[:, 0:2, :].rearrange("p a b -> p (a b)"), ps[:, :], ACT.Copy)\
                       .then_inc(bank_free[4], 1)

                def diff_turn(i):
                    dst = dkt if i % 2 else dqt
                    ps = bank_in(("diff_turn", i), 4)
                    act.activation(dst[:, 0:2, :].rearrange("p a b -> p (a b)"), ps[:, :], ACT.Copy)\
                       .then_inc(bank_free[4], 1)

                def head_scores(j):
                    scale = (MLA_NOPE + MLA_ROPE) ** -0.5 if j < MLA_HEADS else DIFF_HD ** -0.5
                    if j == MLA_HEADS:
                        need(lam_dot, 1, 1)
                        act.activation(lam2e[:, :], lam2[:, :], ACT.Exp).then_inc(lam_exp, 1)
                    need(masked, HEADS, j + 1)
                    for branch in range(1 if j < MLA_HEADS else 2):
                        e = (e1, e2)[branch]
                        for t in range(NT):
                            k = 2 * branch + t
                            part = e[:, t * P:t * P + (t + 1) * P]
                            last = act.activation(part, part, ACT.Exp, bias=nmx[:, k:k + 1], scale=scale,
                                                  accum_out=esum[:, k:k + 1])
                    last.then_inc(exped, 1)

                def head_turn(j):
                    ps = bank_in(("head_turn", j), 4)
                    act.activation(pt[:, :], ps[:, 0:3 * P], ACT.Copy).then_inc(bank_free[4], 1)

                def mix_turn(kt0):
                    ps = bank_in(("mix_turn", kt0), 4 + kt0 // 2 % 2)
                    act.activation(xt_hi[:, kt0:kt0 + 2, :].rearrange("p a b -> p (a b)"), ps[:, :], ACT.Copy)\
                       .then_inc(xt_hi_made, 2)

                steps = {"evac": evac, "qa_rms": qa_rms, "qa_turn": qa_turn, "mla_q": mla_q, "mla_kv": mla_kv,
                         "gla_turn": gla_turn, "gla_decay": gla_decay, "gla_silu": gla_silu, "level_prep": level_prep,
                         "rope_turn": rope_turn, "diff_turn": diff_turn, "head_scores": head_scores,
                         "head_turn": head_turn, "mix_turn": mix_turn}

                def squares_of(c, seen):
                    for t in range(NT):
                        done = 8 * seen + NT * c + t
                        need(x_added, 16, done + 1)
                        need(squared, 16, 8 + done)
                        act.activation(junk[:, :], resid[:, t, c * NCH:(c + 1) * NCH], ACT.Square,
                                       accum_out=ssq[:, t, c:c + 1]).then_inc(squared, 1)

                norm("norm1", 0)
                for n in range(U_FF):
                    round_unit(layer * QUADS + (n + 2) // 4, n + 2)
                    for name, arg in HOOKS.get(n, []):
                        if name in steps:
                            steps[name](arg)
                    if n >= U_OUT and (n - U_OUT) % 8 >= 6:
                        squares_of(2 * ((n - U_OUT) // 8) + (n - U_OUT) % 2, 0)
                norm("norm2", 1)

                def ff_turn(f):
                    for b in (4, 5):
                        act.wait_ge(bank_full[b], layer * USES[b] + ROUND[("ff_turn", 0)][b] + f + 1)
                        dst = f_hi[:, bass.ds(f * 4 + 2 * (b - 4), 2), :].rearrange("p a b -> p (a b)")
                        act.activation(dst, bank[b][:, :], ACT.Copy).then_inc(ft_hi_made, 1)

                def ff_chunk(f, first):
                    for i in range(8):
                        round_unit(layer * QUADS + (U_FF + i + 2) // 4 + 2 * f, U_FF + i + 2)
                        if i == 1 and not first:
                            ff_turn(f - 1)
                        if i == 3:
                            act.wait_ge(used[3], layer * QUADS + (U_FF + 3) // 4 + 1 + 2 * f)
                            for t in range(NT):
                                act.activation(act_sb[:, t, :], bank[t][:, :], ACT.Silu).then_inc(silu_made, 1)

                ff_chunk(0, True)
                with act.Fori(1, FF_CHUNKS) as f:
                    ff_chunk(f, False)
                for n in range(U_DOWN, UNITS):
                    i = n - U_DOWN
                    round_unit(layer * QUADS + (n + 2) // 4, n + 2)
                    if i == 1:
                        ff_turn(FF_CHUNKS - 1)
                    if i % len(DOWN_KT) == len(DOWN_KT) - 1:
                        squares_of(i // len(DOWN_KT), 1)
            act.wait_ge(rstd_made, DEPTH * len(POW) + 1)
            act.activation(xn[:, 1, :], resid[:, 1, :], ACT.Copy, scale=rstd[:, 1:2]).then_inc(xn_act, 1)
            assert count[0] == ACT_LINKS, count[0]

        @block.gpsimd
        def _(pool):
            pool.memset(halves[:, :], -0.5).then_inc(halves_made, 1)
            pool.wait_ge(halves_made, 1)
            with pool.Fori(0, DEPTH) as layer:
                def need(s, per_layer, k):
                    pool.wait_ge(s, layer * per_layer + k)

                def power(name, n):
                    need(ms_made, len(POW), POW[name] + 1)
                    pool.tensor_tensor(rstd[:, 0:n], ms[:, 0:n], halves[:, 0:n], ALU.pow).then_inc(rstd_made, 1)

                power("norm1", 2)
                for n in range(U_FF):
                    for name, arg in HOOKS.get(n, []):
                        if name == "qa_rms":
                            power("mla", 4)
                        if name == "gla_rms":
                            power("gla", 8)
                        if name == "diff_rms":
                            power(f"diff{arg}", 6)
                        if name == "level_prep":
                            need(decay_made, N_LEVELS - 1, arg + 1)
                            if arg == 0:
                                for b in (4, 5):
                                    need(bank_free[b], USES[b], ROUND[("gla_turn", 0)][b] + 2)
                            if arg >= 2:
                                need(bank_full[7], USES[7], ROUND[("level_mm", arg - 2)][7] + 1)
                            pool.tensor_tensor(ql[:, arg % 2], gqt[:, :, :], p2[:, :, 0:SEQ], ALU.mult)
                            pool.tensor_tensor(kl[:, arg % 2], gkt[:, :, :], p2[:, :, 0:SEQ], ALU.mult)\
                                .then_inc(level_made, 1)
                        if name == "rope":
                            need(kr_in, 1, 1)
                            pool.wait_ge(waves, 2)
                            cos = cos_sb[:, :, :, :].to_broadcast([P, NT, 7, 32])
                            sin = sin_sb[:, :, :, :].to_broadcast([P, NT, 7, 32])
                            a, b = qr[:, :, 0:7, 0:32], qr[:, :, 0:7, 32:64]
                            pool.tensor_tensor(turn1[:, :, :, :], a, cos, ALU.mult)
                            pool.tensor_tensor(turn2[:, :, :, :], b, sin, ALU.mult)
                            pool.tensor_tensor(turn3[:, :, :, :], a, sin, ALU.mult)
                            pool.tensor_tensor(turn4[:, :, :, :], b, cos, ALU.mult).then_inc(rope_mul, 1)
                power("norm2", 2)
            pool.wait_ge(ms_made, DEPTH * len(POW) + 1)
            pool.tensor_tensor(rstd[:, 0:2], ms[:, 0:2], halves[:, 0:2], ALU.pow).then_inc(rstd_made, 1)

        @block.vector
        def _(vec):
            count = [0]

            def rest_of_unit(quad, n):
                s = n % 4
                kts, cols = unit_shape(n)
                vec.wait_ge(hi_made[s], quad + 1)
                vec.tensor_tensor(w_lo[s % 2][:, 0:kts * cols], stage[s][:, 0:kts * cols],
                                  w_hi[s % 2][:, 0:kts * cols].bitcast(F32), ALU.subtract).then_inc(lo_made[s], 1)

            first_links = [0]

            def first(ins):
                first_links[0] += 1
                ins.then_inc(angles_chain, 1)
                vec.wait_ge(angles_chain, first_links[0])

            for i, free in enumerate([*lo_made, *bank_free.values()]):
                vec.memset((mx, nmx)[i // 4][:, i % 4:i % 4 + 1], 0.0).then_inc(free, 1)

            vec.wait_ge(consts_in, 16)
            vec.wait_ge(setup_in, 64)
            inv = k_sb[:, K_INV:K_INV + 32]
            vec.tensor_copy(lev_sb[:, :, :], levels_in[:, :, :])
            first(vec.tensor_copy(pos_f[:, :], pos_i[:, :]))
            for t in range(NT):
                ang, turns = sin_sb[:, t, 0, :], cos_sb[:, t, 0, :]
                first(vec.tensor_scalar(ang, inv, pos_f[:, t:t + 1], None, ALU.mult))
                first(vec.tensor_scalar(turns, ang, 1.0 / (2 * np.pi), ROUNDER, ALU.mult, ALU.add))
                first(vec.tensor_scalar(turns, turns, ROUNDER, None, ALU.subtract))
                for part in TWO_PI:
                    first(vec.scalar_tensor_tensor(ang, turns, -part, ang, ALU.mult, ALU.add))
                first(vec.tensor_scalar(ang, ang, 3.1415925, -3.1415925, ALU.min, ALU.max))
                first(vec.scalar_tensor_tensor(turns, ang, -1.0, ang, ALU.mult, ALU.min))
                first(vec.tensor_scalar(turns, turns, float(np.pi / 2), None, ALU.add))
            vec.memset(esum[:, 0:1], 1.0).then_inc(angles, 1)
            rest_of_unit(0, 0)
            rest_of_unit(0, 1)

            with vec.Fori(0, DEPTH) as layer:
                def need(s, per_layer, k):
                    vec.wait_ge(s, layer * per_layer + k)

                def link(ins):
                    count[0] += 1
                    ins.then_inc(vec_chain, 1)
                    need(vec_chain, VEC_LINKS, count[0])

                def bank_in(key, b):
                    need(bank_full[b], USES[b], ROUND[key][b] + 1)
                    return bank[b]

                def masked_bank_in(key, b):
                    turn = vec.to_reg(layer * USES[b] + (ROUND[key][b] + 1))
                    vec.wait_ge(setup_in, 64)
                    vec.wait_ge(bank_full[b], turn)
                    return bank[b]

                def complete(n):
                    need(used[n % 4], QUADS, n // 4 + 1)

                def copied(key, b):
                    need(bank_free[b], USES[b], ROUND[key][b] + 2)

                def gain(i):
                    return gain_sb[:, bass.ds(layer, 1), i:i + 1].rearrange("p a b -> p (a b)")

                def scaled(n, width, of):
                    vec.tensor_scalar(ms[:, 0:n], of, 1.0 / width, EPS, ALU.mult, ALU.add).then_inc(ms_made, 1)

                def norm(which, seen):
                    vec.wait_ge(squared, layer * 16 + 8 * seen + 8)
                    link(vec.tensor_reduce(ms[:, 0:NT], ssq[:, :, :], AX.X, ALU.add))
                    scaled(NT, D_MODEL, ms[:, 0:NT])
                    need(rstd_made, len(POW), POW[which] + 1)
                    for q in range(4):
                        vec.tensor_scalar(xn[:, 0, q * NCH:(q + 1) * NCH], resid[:, 0, q * NCH:(q + 1) * NCH],
                                          rstd[:, 0:1], None, ALU.mult).then_inc(xn_vec, 1)
                    g0 = G_ATTN if which == "norm1" else G_FFN
                    for r in range(KT // 2):
                        ps = bank_in((which, r), 4 + r % 4)
                        need(xt_hi_made, 48, 32 * seen + 2 * r + 2)
                        for i in range(2):
                            kt = 2 * r + i
                            ins = vec.scalar_tensor_tensor(xt_lo[:, kt, :], ps[:, i * SEQ:(i + 1) * SEQ], gain(g0 + kt),
                                                           xt_hi[:, kt, :].bitcast(F32), ALU.mult, ALU.subtract)
                        ins.then_inc(bank_free[4 + r % 4], 1)

                def evac(c):
                    col, cols = (EARLY + LATE)[c]
                    complete(4 * c + 3 if c < len(EARLY) else U_LATE + 4 * (c - len(EARLY)) + 3)
                    vec.tensor_copy(projected(1, col, cols), bank[2 * (c % 2) + 1][:, 0:cols])\
                       .then_inc(acc_out_vec[c % 2], 1)

                def qa_rms(_):
                    need(m_squared, 4, 4)
                    vec.tensor_scalar(ms[:, 0:2], m_ss[:, 0:2], 1.0 / MLA_Q_RANK, EPS, ALU.mult, ALU.add)
                    vec.tensor_scalar(ms[:, 2:4], m_ss[:, 2:4], 1.0 / MLA_KV_RANK, EPS, ALU.mult, ALU.add)\
                       .then_inc(ms_made, 1)

                def qa_scale(_):
                    need(rstd_made, len(POW), POW["mla"] + 1)
                    need(acc_out_act[1], R_OUT, 1)
                    need(acc_out_vec[1], R_OUT, 1)
                    for t in range(NT):
                        for i, (col, n) in enumerate(((C_QA, MLA_Q_RANK), (C_KVA, MLA_KV_RANK))):
                            ins = vec.tensor_scalar(p2c(t, col, n), p2c(t, col, n), rstd[:, 2 * i + t:2 * i + t + 1], None,
                                                    ALU.mult)
                    ins.then_inc(qa_scaled, 1)

                def qa_turn(b):
                    ps = bank_in(("qa_turn", b), 4 + b)
                    need(qa_hi_made, 6, 2 * b + 2)
                    for i in range(2):
                        k = 2 * b + i
                        ins = vec.scalar_tensor_tensor(qa_lo[:, k, :], ps[:, i * SEQ:(i + 1) * SEQ], gain(G_QA + k),
                                                       qa_hi[:, k, :].bitcast(F32), ALU.mult, ALU.subtract)
                    ins.then_inc(bank_free[4 + b], 1)

                def mla_q(h):
                    need(acc_out_act[0], R_OUT, R_MLA + h + 1)
                    vec.tensor_copy(qr[:, :, h, :], bank[0][:, SEQ:SEQ + NT * 64].rearrange("p (t d) -> p t d", t=NT))\
                       .then_inc(acc_out_vec[0], 1)

                def mla_kv(h):
                    need(acc_out_act[1], R_OUT, R_MLA + h + 1)
                    vec.tensor_copy(mv[:, :, h, :], bank[2][:, SEQ:2 * SEQ].rearrange("p (t d) -> p t d", t=NT))\
                       .then_inc(acc_out_vec[1], 1)

                def gla_turn(_):
                    ps = bank_in(("gla_turn", 0), 5)
                    vec.tensor_copy(gkt[:, :, :].rearrange("p a b -> p (a b)"), ps[:, :]).then_inc(bank_free[5], 1)

                def gla_logits(_):
                    ps = bank_in(("gla_logits", 0), 7)
                    for g in range(2):
                        ins = vec.tensor_scalar(gate_z[:, g, :], ps[:, g * SEQ:(g + 1) * SEQ], gain(G_BIAS + g), None, ALU.add)
                    ins.then_inc(bank_free[7], 1)
                    copied(("gla_logits", 0), 7)
                    vec.scalar_tensor_tensor(gate_e[:, :, :], gate_z[:, :, :], -1.0, gate_z[:, :, :], ALU.mult, ALU.min)\
                       .then_inc(gate_neg, 1)
                    link(vec.memset(ones[:, :], 1.0))

                def gla_decay(_):
                    need(gate_ln, 1, 1)
                    link(vec.scalar_tensor_tensor(gate_z[:, :, :], gate_z[:, :, :], 0.0, gate_e[:, :, :], ALU.min,
                                                  ALU.subtract))
                    for g in range(2):
                        ins = vec.tensor_tensor_scan(logs[:, g, :], ones[:, :], gate_z[:, g, :], 0.0, ALU.mult, ALU.add)
                    link(ins)
                    link(vec.memset(att[:, :, :, :, :].rearrange("p a b c d -> p (a b c d)"), 0.0))

                def level_prep(i):
                    size = SEQ // 2 if i == 0 else LEVELS[i - 1]
                    b = logs[:, :, :].rearrange("p g (n w) -> p g n w", w=2 * size)
                    o = p2[:, :, 0:SEQ].rearrange("p g (n w) -> p g n w", w=2 * size)
                    if i:
                        need(level_made, N_LEVELS - 1, i)
                    nb = SEQ // (2 * size)
                    mid = b[:, :, :, size - 1:size].to_broadcast([P, 2, nb, 2 * size])
                    link(vec.tensor_tensor(o, b, mid, ALU.subtract))
                    vec.scalar_tensor_tensor(p2[:, :, 0:SEQ], p2[:, :, 0:SEQ], -1.0, p2[:, :, 0:SEQ], ALU.mult, ALU.min)\
                       .then_inc(span_made, 1)

                def level_mm(i):
                    for par in range(2):
                        ps = masked_bank_in(("level_mm", i), 6 + par)
                        if i == 0:
                            ins = vec.tensor_copy(cross[:, par, :, :].rearrange("p g n -> p (g n)"), ps[:, 0:2 * P])
                        else:
                            mask = lev_sb[:, i - 1:i, :].to_broadcast([P, 4, P])
                            ins = vec.copy_predicated(att[:, par, :, :, :].rearrange("p t g n -> p (t g) n"), mask,
                                                      ps[:, :].rearrange("p (a n) -> p a n", a=4))
                        ins.then_inc(bank_free[6 + par], 1)

                def gla_out(_):
                    bank_in(("gla_out", 0), 7)
                    for t in range(NT):
                        ps = bank_in(("gla_out", 0), 6 + t)
                        ins = vec.tensor_copy(p2c(t, C_GV, NCH), ps[:, :])
                        ins.then_inc(bank_free[6 + t], 1)
                    copied(("gla_out", 0), 7)

                def gla_rms(_):
                    o = p2[:, :, C_GV - C_GQ:C_GV - C_GQ + NCH]
                    link(vec.tensor_tensor(squares[:, :, :, :].rearrange("p t h d -> p t (h d)"), o, o, ALU.mult))
                    link(vec.tensor_reduce(ms[:, 0:8], squares[:, :, :, :].rearrange("p t h d -> p (t h) d"), AX.X, ALU.add))
                    scaled(8, GLA_DV, ms[:, 0:8])

                def gla_gated(_):
                    need(rstd_made, len(POW), POW["gla"] + 1)
                    need(gate_silu, 2, 2)
                    need(rows_in, 32, 32)
                    for t in range(NT):
                        o = p2c(t, C_GV, NCH).rearrange("p (h d) -> p h d", h=4)
                        r = rstd[:, 4 * t:4 * t + 4].rearrange("p (h o) -> p h o", o=1).to_broadcast([P, 4, P])
                        w = row_sb[:, W_GLA:W_GLA + P].rearrange("p (o d) -> p o d", o=1).to_broadcast([P, 4, P])
                        link(vec.tensor_tensor(o, o, r, ALU.mult))
                        link(vec.tensor_tensor(o, o, w, ALU.mult))
                        ins = vec.tensor_tensor(p2c(t, C_GV, NCH), p2c(t, C_GV, NCH), p2c(t, C_GO, NCH), ALU.mult)
                    ins.then_inc(gla_mixed, 1)

                def rope(_):
                    need(acc_out_vec[0], R_OUT, R_LATE)
                    vec.tensor_copy(qr[:, :, 6, :], p2[:, :, C_KR - C_GQ:C_KR - C_GQ + 64]).then_inc(kr_in, 1)
                    need(rope_mul, 1, 1)
                    vec.tensor_tensor(qr[:, :, 0:7, 0:32], turn1[:, :, :, :], turn2[:, :, :, :], ALU.subtract)
                    link(vec.tensor_tensor(qr[:, :, 0:7, 32:64], turn3[:, :, :, :], turn4[:, :, :, :], ALU.add))
                    vec.tensor_copy(qr[:, :, 7, :], qr[:, :, 6, :]).then_inc(roped, 1)

                def rope_turn(_):
                    ps = bank_in(("rope_turn", 0), 5)
                    vec.tensor_copy(qrt[:, 2:4, :].rearrange("p a b -> p (a b)"), ps[:, :])\
                       .then_inc(bank_free[5], 1)

                def diff_turn(i):
                    if i == 0:
                        need(rows_in, 32, 32)
                        prod = squares[:, 0, 0, :]
                        link(vec.tensor_tensor(prod, row_sb[:, W_LAM:W_LAM + P], row_sb[:, W_LAM + P:W_LAM + 2 * P],
                                               ALU.mult))
                        vec.tensor_reduce(lam2[:, :], prod.rearrange("p (a b) -> p a b", a=2), AX.X, ALU.add)\
                           .then_inc(lam_dot, 1)
                    ps = bank_in(("diff_turn", i), 5)
                    vec.tensor_copy((dkt if i % 2 else dqt)[:, 2, :], ps[:, 0:SEQ]).then_inc(bank_free[5], 1)

                def head_scores(j):
                    mla = j < MLA_HEADS
                    if j == MLA_HEADS:
                        need(lam_exp, 1, 1)
                        link(vec.tensor_tensor(lam[:, :], lam2e[:, 0:1], lam2e[:, 1:2], ALU.subtract))
                        l0 = k_sb[:, bass.ds(K_LAM + 2 * layer, 1)]
                        link(vec.tensor_tensor(lam[:, :], lam[:, :], l0, ALU.add))
                    for branch in range(1 if mla else 2):
                        ps = masked_bank_in(("head_scores", j), 6 + branch)
                        e = (e1, e2)[branch]
                        for t in range(NT):
                            k, n = 2 * branch + t, (t + 1) * P
                            ins = vec.tensor_tensor_reduce(e[:, t * P:t * P + n], ps[:, t * P:t * P + n],
                                                           caus_sb[:, 2 * P - n:2 * P], 1.0, NEG * 4, ALU.add, ALU.max,
                                                           mx[:, k:k + 1])
                        ins.then_inc(bank_free[6 + branch], 1)
                    for b in (6,) if mla else (6, 7):
                        copied(("head_scores", j), b)
                    scale = (MLA_NOPE + MLA_ROPE) ** -0.5 if mla else DIFF_HD ** -0.5
                    vec.tensor_scalar(nmx[:, :], mx[:, :], -scale, None, ALU.mult).then_inc(masked, 1)
                    need(exped, HEADS, j + 1)
                    if mla:
                        link(vec.reciprocal(held[:, 2 * j:2 * j + 2], esum[:, 0:2]))
                        return
                    link(vec.reciprocal(rsum[:, :], esum[:, :]))
                    link(vec.tensor_scalar(rsum[:, 2:4], rsum[:, 2:4], lam[:, 0:1], None, ALU.mult))
                    for t in range(NT):
                        b = e2[:, t * P:t * P + (t + 1) * P]
                        ins = vec.tensor_scalar(b, b, rsum[:, 2 + t:3 + t], None, ALU.mult)
                    link(ins)
                    for t in range(NT):
                        a, b = (e[:, t * P:t * P + (t + 1) * P] for e in (e1, e2))
                        ins = vec.scalar_tensor_tensor(a, a, rsum[:, t:t + 1], b, ALU.mult, ALU.subtract)
                    ins.then_inc(probs_made, 1)

                def head_out(j):
                    ps = bank_in(("head_out", j), 5)
                    if j < MLA_HEADS:
                        for t in range(NT):
                            ins = vec.tensor_scalar(mv[:, t, j, :], ps[:, t * P:(t + 1) * P], held[:, 2 * j + t:2 * j + t + 1],
                                                    None, ALU.mult)
                        ins.then_inc(bank_free[5], 1)
                        return
                    col = C_DV + (j - MLA_HEADS) * P
                    ins = vec.tensor_copy(pd[:, :, col:col + P], ps[:, 0:2 * P].rearrange("p (t d) -> p t d", t=NT))
                    ins.then_inc(bank_free[5], 1)

                def diff_rms(g):
                    copied(("head_out", MLA_HEADS + 3 * g + 2), 5)
                    o = pd[:, :, C_DV + g * G3:C_DV + (g + 1) * G3].rearrange("p t (h d) -> p t h d", h=3)
                    link(vec.tensor_tensor(squares[:, :, 0:3, :], o, o, ALU.mult))
                    link(vec.tensor_reduce(ms[:, 0:6].rearrange("p (t h) -> p t h", t=NT), squares[:, :, 0:3, :], AX.X, ALU.add))
                    scaled(6, DIFF_VD, ms[:, 0:6])
                    if g == 0:
                        w = row_sb[:, W_SUB:W_SUB + P]
                        link(vec.tensor_scalar(w, w, k_sb[:, bass.ds(K_LAM + 2 * layer + 1, 1)], None, ALU.mult))

                def diff_scale(g):
                    need(rstd_made, len(POW), POW[f"diff{g}"] + 1)
                    for t in range(NT):
                        o = pd[:, t, C_DV + g * G3:C_DV + (g + 1) * G3].rearrange("p (h d) -> p h d", h=3)
                        r = rstd[:, 3 * t:3 * t + 3].rearrange("p (h o) -> p h o", o=1).to_broadcast([P, 3, P])
                        w = row_sb[:, W_SUB:W_SUB + P].rearrange("p (o d) -> p o d", o=1).to_broadcast([P, 3, P])
                        link(vec.tensor_tensor(o, o, r, ALU.mult))
                        ins = vec.tensor_tensor(o, o, w, ALU.mult)
                    ins.then_inc(diff_mixed, 1)

                def mix_turn(kt0):
                    b = 4 + kt0 // 2 % 2
                    ps = bank_in(("mix_turn", kt0), b)
                    order = [6, 8, 10, 12, 14, 0, 2, 4].index(kt0)
                    need(xt_hi_made, 48, 16 + 2 * order + 2)
                    vec.tensor_tensor(xt_lo[:, kt0:kt0 + 2, :].rearrange("p a b -> p (a b)"), ps[:, :],
                                      xt_hi[:, kt0:kt0 + 2, :].rearrange("p a b -> p (a b)").bitcast(F32), ALU.subtract)\
                       .then_inc(bank_free[b], 1)

                steps = {"evac": evac, "qa_rms": qa_rms, "qa_scale": qa_scale, "qa_turn": qa_turn, "mla_q": mla_q,
                         "mla_kv": mla_kv, "gla_turn": gla_turn, "gla_logits": gla_logits, "gla_decay": gla_decay,
                         "level_prep": level_prep, "level_mm": level_mm, "gla_out": gla_out, "gla_rms": gla_rms,
                         "gla_gated": gla_gated, "rope": rope, "rope_turn": rope_turn, "diff_turn": diff_turn,
                         "head_scores": head_scores, "head_out": head_out, "diff_rms": diff_rms,
                         "diff_scale": diff_scale, "mix_turn": mix_turn}

                def add_to_resid(c, parity, n):
                    complete(n)
                    for t in range(NT):
                        part = resid[:, t, c * NCH:(c + 1) * NCH]
                        vec.tensor_tensor(part, bank[2 * parity + t][:, :], part, ALU.add)\
                           .then_inc(x_added, 1)

                norm("norm1", 0)
                for n in range(U_FF):
                    rest_of_unit(layer * QUADS + (n + 2) // 4, n + 2)
                    for name, arg in HOOKS.get(n, []):
                        if name in steps:
                            steps[name](arg)
                    if n >= U_OUT and (n - U_OUT) % 8 >= 6:
                        pair, c = (n - U_OUT) // 8, (n - U_OUT) % 2
                        add_to_resid(2 * pair + c, c, n)
                norm("norm2", 1)

                def ff_turn(f):
                    for b in (4, 5):
                        vec.wait_ge(bank_full[b], layer * USES[b] + ROUND[("ff_turn", 0)][b] + f + 1)
                        vec.wait_ge(ft_hi_made, layer * (2 * FF_CHUNKS) + 2 * f + b - 3)
                        at = bass.ds(f * 4 + 2 * (b - 4), 2)
                        vec.tensor_tensor(f_lo[:, at, :].rearrange("p a b -> p (a b)"), bank[b][:, :],
                                          f_hi[:, at, :].rearrange("p a b -> p (a b)").bitcast(F32), ALU.subtract)\
                           .then_inc(bank_free[b], 1)

                def ff_chunk(f, first):
                    for i in range(8):
                        rest_of_unit(layer * QUADS + (U_FF + i + 2) // 4 + 2 * f, U_FF + i + 2)
                        if i == 1 and not first:
                            ff_turn(f - 1)
                        if i == 7:
                            vec.wait_ge(used[3], layer * QUADS + (U_FF + 7) // 4 + 1 + 2 * f)
                            for t in range(NT):
                                vec.wait_ge(silu_made, layer * (FF_CHUNKS * NT) + f * NT + t + 1)
                                vec.tensor_tensor(act_sb[:, t, :], act_sb[:, t, :], bank[2 + t][:, :], ALU.mult)\
                                   .then_inc(act_made, 1)

                ff_chunk(0, True)
                with vec.Fori(1, FF_CHUNKS) as f:
                    ff_chunk(f, False)
                for n in range(U_DOWN, UNITS):
                    i = n - U_DOWN
                    rest_of_unit(layer * QUADS + (n + 2) // 4, n + 2)
                    if i == 1:
                        ff_turn(FF_CHUNKS - 1)
                    if i % len(DOWN_KT) == len(DOWN_KT) - 1:
                        c = i // len(DOWN_KT)
                        add_to_resid(c, c % 2, n)
                assert count[0] == VEC_LINKS, count[0]

            vec.wait_ge(squared, 16 * DEPTH + 8)
            vec.tensor_reduce(ms[:, 0:NT], ssq[:, :, :], AX.X, ALU.add).then_inc(vec_chain, 1)
            vec.wait_ge(vec_chain, DEPTH * VEC_LINKS + 1)
            vec.tensor_scalar(ms[:, 0:NT], ms[:, 0:NT], 1.0 / D_MODEL, EPS, ALU.mult, ALU.add).then_inc(ms_made, 1)
            vec.wait_ge(rstd_made, DEPTH * len(POW) + 1)
            vec.wait_ge(setup_in, 80)
            vec.scalar_tensor_tensor(xn[:, 0, :], resid[:, 0, :], rstd[:, 0:1], last_gain[:, :], ALU.mult, ALU.mult)\
               .then_inc(out_made, 1)
            vec.wait_ge(xn_act, 8 * DEPTH + 1)
            vec.tensor_tensor(xn[:, 1, :], xn[:, 1, :], last_gain[:, :], ALU.mult).then_inc(out_made, 1)


_OUTS = [((1, SEQ, D_MODEL), "float32")]


def build(nc, shapes):
    aps = {name: nc.dram_tensor(f"in_{name}", shape, dt, kind="ExternalInput").ap() for name, (shape, dt) in shapes.items()}
    out = nc.dram_tensor("out_0_dram", (SEQ, D_MODEL), F32, kind="ExternalOutput").ap()
    program(nc, out=out, **aps)


def kernel(**inputs):
    import concourse.bacc as bacc
    from concourse.bass_utils import run_bass_kernel_spmd

    a = {k: np.ascontiguousarray(v) for k, v in inputs.items()}

    def columns(v, n):
        return v.reshape(DEPTH, n, P).transpose(2, 0, 1)

    consts = np.zeros((P, K_END), np.float32)
    consts[:, K_ID:K_ID + P] = np.eye(P)
    consts[:, K_INV:K_INV + 32] = 1.0 / ROPE_THETA ** (np.arange(0, MLA_ROPE, 2, dtype=np.float32) / MLA_ROPE)
    for layer in range(DEPTH):
        first = 0.8 - 0.6 * np.exp(-0.3 * layer)
        consts[:, K_LAM + 2 * layer:K_LAM + 2 * layer + 2] = first, 1.0 - first
    key, query = np.arange(P)[:, None], np.arange(P)[None, :]
    levels = np.zeros((P, len(LEVELS), P), np.float32)
    for i, size in enumerate(LEVELS):
        if size:
            levels[:, i] = (key // (2 * size) == query // (2 * size)) & (key % (2 * size) < size) & (query % (2 * size) >= size)
        else:
            levels[:, i] = key == query
    causal = np.zeros((P, 2 * P), np.float32)
    causal[:, P:] = np.where(query <= key, 0.0, NEG)

    arrays = {
        "x": a["x"].reshape(SEQ, D_MODEL),
        "positions": a["positions"].reshape(NT, P).T,
        "w_in": a["w_in"], "w_q_b": a["mla_w_q_b"], "w_kv_b": a["mla_w_kv_b"], "w_out": a["w_out"],
        "w_gate": a["w_gate"], "w_up": a["w_up"], "w_down": a["w_down"], "gate_w": a["gla_gate_w"],
        "gains": np.concatenate([columns(a["attn_norm"], KT), columns(a["ffn_norm"], KT), columns(a["mla_q_norm"], 4),
                                 columns(a["mla_kv_norm"], 2), columns(a["gla_gate_b"], 2)], axis=2),
        "rows": np.concatenate([a["diff_subln"], a["gla_norm"], a["diff_lambda_q1"], a["diff_lambda_q2"],
                                a["diff_lambda_k1"], a["diff_lambda_k2"]], axis=1).reshape(DEPTH, 1, W_END),
        "final_norm": a["final_norm"].reshape(1, D_MODEL),
        "consts": consts, "levels": levels, "causal": causal,
    }
    arrays = {k: np.ascontiguousarray(v) for k, v in arrays.items()}
    nc = bacc.Bacc("TRN2", target_bir_lowering=False, num_devices=1)
    build(nc, {k: (v.shape, mybir.dt.from_np(v.dtype)) for k, v in arrays.items()})
    r = run_bass_kernel_spmd(nc, [{f"in_{k}": v for k, v in arrays.items()}], core_ids=[0])
    return r.results[0]["out_0_dram"].reshape(1, SEQ, D_MODEL)
```

```python
from contextlib import ExitStack

import numpy as np

import concourse.bass as bass
from concourse import mybir

F32 = mybir.dt.float32
F32R = mybir.dt.float32r
U8 = mybir.dt.uint8
I32 = mybir.dt.int32
ALU = mybir.AluOpType
ACT = mybir.ActivationFunctionType
AX = mybir.AxisListType

P = 128
D_MODEL, SEQ, DEPTH = 2048, 256, 2
DIFF_HEADS, DIFF_HD, DIFF_VD = 6, 64, 128
GLA_HEADS, GLA_DK, GLA_DV, GLA_RANK, GLA_TAU = 4, 64, 128, 16, 16.0
MLA_HEADS, MLA_Q_RANK, MLA_KV_RANK, MLA_NOPE, MLA_ROPE, MLA_VD = 6, 512, 256, 128, 64, 128
ROPE_THETA, D_FF, EPS = 10000.0, 5632, 1e-6

NT = SEQ // P
KT = D_MODEL // P
FT = D_FF // P
NCH = 512
FF_CHUNKS = D_FF // NCH
LEAD = 3

C_DV = 2 * DIFF_HEADS * 2 * DIFF_HD
C_GQ = C_DV + DIFF_HEADS * DIFF_VD
C_GK = C_GQ + GLA_HEADS * GLA_DK
C_GV = C_GK + GLA_HEADS * GLA_DK
C_GR = C_GV + GLA_HEADS * GLA_DV
C_GO = C_GR + GLA_RANK
C_QA = C_GO + GLA_HEADS * GLA_DV
C_KVA = C_QA + MLA_Q_RANK
C_KR = C_KVA + MLA_KV_RANK
IN_COLS = C_KR + MLA_ROPE
DIFF_QK = DIFF_HEADS * 2 * DIFF_HD
G3 = 3 * 2 * DIFF_HD

EARLY = [(C_QA, MLA_Q_RANK), (C_KVA, IN_COLS - C_KVA), (C_GQ, NCH), (C_GV, NCH), (C_GR, 272), (C_GR + 272, 256)]
LATE = [(part + g * G3, G3) for g in range(2) for part in (0, DIFF_QK)] + [(2 * DIFF_QK + g * G3, G3) for g in range(2)]

U_MLA = 4 * len(EARLY)
U_LATE = U_MLA + 2 * MLA_HEADS
U_OUT = U_LATE + 4 * len(LATE)
U_FF = U_OUT + 4 * (D_MODEL // NCH)
U_DOWN = U_FF + 8 * FF_CHUNKS
DOWN_KT = [range(4 * u, 4 * u + 4) for u in range(8)] + [range(32 + 3 * u, 35 + 3 * u) for u in range(4)]
UNITS = U_DOWN + len(DOWN_KT) * (D_MODEL // NCH)
QUADS = UNITS // 4
R_MLA = len(EARLY) // 2
R_LATE = R_MLA + MLA_HEADS
R_OUT = R_LATE + len(LATE) // 2
R_FF = R_OUT + 2
R_DOWN = R_FF + FF_CHUNKS
ROUNDS = R_DOWN + 2

OUT_KT = [[6, 7, 8, 9], [10, 11, 12, 13], [14, 15, 0, 1], [2, 3, 4, 5]]

LEVELS = [64, 32, 16, 8, 4, 2, 1, 0]
N_LEVELS = 1 + len(LEVELS)
HEADS = MLA_HEADS + DIFF_HEADS


SCORES_AT = [40, 41, 42, 43, 44, 45, 47, 49, 51, 54, 56, 58]
TURN_AT = [n + 2 for n in SCORES_AT[:MLA_HEADS]] + [n + 3 for n in SCORES_AT[MLA_HEADS:]]
OUT_AT = [n + 3 for n in SCORES_AT[:MLA_HEADS]] + [56, 57, 58, 60, 61, 62]
PT_OF = [0] * MLA_HEADS + [j % 3 for j in range(DIFF_HEADS)]


def hooks():
    at = {}

    def put(n, *steps):
        at.setdefault(n, []).extend(steps)

    for c in range(len(EARLY)):
        put(4 * c + 3, ("evac", c))
    put(7, ("qa_rms", 0))
    put(8, ("qa_scale", 0))
    for b in range(3):
        put(10 + b, ("qa_turn", b))
    put(13, ("angles", 0))
    put(20, ("gla_turn", 0))
    put(21, ("gla_logits", 0))
    put(22, ("gla_decay", 0))
    put(23, ("gla_silu", 0))
    for h in range(MLA_HEADS):
        put(U_MLA + 2 * h, ("mla_q", h))
        put(U_MLA + 2 * h + 1, ("mla_kv", h))
    for i in range(N_LEVELS - 1):
        put(24 + 2 * i, ("level_prep", i))
        put(25 + 2 * i, ("level_exp", i))
    for i in range(N_LEVELS):
        put(27 + 2 * i, ("level_mm", i))
    for c in range(len(LATE)):
        put(U_LATE + 4 * c + 3, ("evac", len(EARLY) + c))
    put(36, ("rope", 0))
    put(39, ("rope_turn", 0))
    put(45, ("gla_out", 0))
    put(46, ("gla_rms", 0), ("lambdas", 0))
    put(47, ("gla_gated", 0))
    put(59, ("mix_turn", 6), ("mix_turn", 8))
    put(60, ("mix_turn", 10))
    put(61, ("mix_turn", 12))
    put(62, ("mix_turn", 14))
    put(63, ("mix_turn", 0))
    for i, n in enumerate((44, 45, 52, 53)):
        put(n, ("diff_turn", i))
    for j in range(HEADS):
        put(OUT_AT[j], ("head_out", j))
        put(TURN_AT[j], ("head_turn", j))
        put(SCORES_AT[j] + 2, ("head_norm", j))
        put(SCORES_AT[j] + 1, ("head_exp", j))
        put(SCORES_AT[j], ("head_scores", j))
    put(58, ("diff_rms", 0))
    put(60, ("diff_scale", 0))
    put(62, ("diff_rms", 1))
    put(63, ("diff_scale", 1))
    put(64, ("mix_turn", 2), ("mix_turn", 4))
    order = ["", "head_out", "head_turn", "head_norm", "head_exp", "head_scores", "diff_rms", "diff_scale"]
    for steps in at.values():
        steps.sort(key=lambda step: order.index(step[0]) if step[0] in order else 0)
    return at


HOOKS = hooks()
BANKS_OF = {"qa_turn": lambda b: [4 + b], "gla_turn": lambda _: [4, 5, 6], "gla_logits": lambda _: [7],
            "level_mm": lambda _: [6, 7], "rope_turn": lambda _: [4, 5],
            "head_scores": lambda j: [6] if j < MLA_HEADS else [6, 7], "head_turn": lambda _: [4],
            "head_out": lambda _: [5], "gla_out": lambda _: [6, 7], "diff_turn": lambda _: [4, 5],
            "mix_turn": lambda kt: [4 + kt // 2 % 2]}


def chunk_round(c):
    return c % 2, c // 2 if c < len(EARLY) else R_LATE + (c - len(EARLY)) // 2


def bank_rounds():
    used = {b: 0 for b in (4, 5, 6, 7)}
    of = {}

    def take(key, banks):
        of[key] = {}
        for b in banks:
            of[key][b] = used[b]
            used[b] += 1

    for r in range(KT // 2):
        take(("norm1", r), [4 + r % 4])
    for n in sorted(HOOKS):
        for step in HOOKS[n]:
            if step[0] in BANKS_OF:
                take(step, BANKS_OF[step[0]](step[1]))
    for r in range(KT // 2):
        take(("norm2", r), [4 + r % 4])
    take(("ff_turn", 0), [4, 5])
    for b in (4, 5):
        used[b] += FF_CHUNKS - 1
    return of, used


ROUND, USES = bank_rounds()
POW = {"norm1": 0, "mla": 1, "gla": 2, "diff0": 3, "diff1": 4, "norm2": 5}

ARENA = 2 * FT * SEQ
A_PD = 0
A_P2 = A_PD + NT * C_GQ
P2 = IN_COLS - C_GQ
A_QNT = A_P2 + NT * P2
A_KNT = A_QNT + MLA_HEADS * SEQ
A_MV = A_KNT + MLA_HEADS * SEQ
A_QRT = A_MV + NT * MLA_HEADS * MLA_VD
A_QR = A_QRT + 4 * SEQ
A_GQT = A_QR + NT * 8 * MLA_ROPE
A_GKT = A_GQT + 2 * SEQ
A_B = A_GKT + 2 * SEQ
A_QL = A_B + 2 * SEQ
A_KL = A_QL + 2 * 2 * SEQ
A_ATT = A_KL + 2 * 2 * SEQ
A_CROSS = A_ATT + 2 * NT * 2 * P
A_E1 = A_CROSS + 2 * 2 * P
A_E2 = A_E1 + 3 * P
A_PT = A_E2 + 3 * P
A_END = A_PT + 3 * P
assert A_END <= ARENA

K_ID, K_INV, K_LAM, K_END = 0, P, P + MLA_ROPE // 2, P + MLA_ROPE // 2 + 2 * DEPTH
G_ATTN, G_FFN, G_QA, G_KVA, G_BIAS, G_END = 0, KT, 2 * KT, 2 * KT + 4, 2 * KT + 6, 2 * KT + 8
W_SUB, W_GLA, W_LAM, W_END = 0, P, 2 * P, 2 * P + 4 * DIFF_HD
NEG = -1e30
ACT_LINKS, VEC_LINKS = 1, 67
TWO_PI = [6.28125, 0.0019350051879882812, 3.0199159819e-07]
ROUNDER = 12582912.0


def program(nc, x, positions, w_in, w_q_b, w_kv_b, w_out, w_gate, w_up, w_down, gate_w, gains, rows,
            final_norm, consts, levels, causal, out):
    with ExitStack() as ctx:
        def sem(name):
            return ctx.enter_context(nc.semaphore(name))

        def sb(name, shape, dt):
            return ctx.enter_context(nc.sbuf_tensor(name, shape, dt))

        arena_at = nc.sbuf_base + (-nc.sbuf_base) % 64
        xt_at = arena_at + 4 * ARENA
        g_at = xt_at + 4 * 2 * KT * SEQ
        stage_at = g_at + 4 * NT * NCH
        sb("slab", [P, (stage_at - arena_at) // 4 + 4 * 4 * NCH], F32)

        def place(name, shape, dt, offset):
            return nc.alloc_sbuf_tensor_at(name, shape, dt, offset=offset)

        def arena(name, shape, dt, word):
            return place(name, shape, dt, arena_at + 4 * word)

        pd = arena("pd", [P, NT, C_GQ], F32, A_PD)
        p2 = arena("p2", [P, NT, P2], F32, A_P2)
        qa_hi = arena("qa_hi", [P, 6, SEQ], F32R, A_PD)
        qa_lo = arena("qa_lo", [P, 6, SEQ], F32R, A_PD + 6 * SEQ)
        turn1, turn2, turn3, turn4 = (arena(f"rope_product{i}", [P, NT, 7, 32], F32, A_PD + 448 * i) for i in range(4))
        qnt = arena("qnt", [P, MLA_HEADS, SEQ], F32, A_QNT)
        knt = arena("knt", [P, MLA_HEADS, SEQ], F32, A_KNT)
        mv = arena("mv", [P, NT, MLA_HEADS, MLA_VD], F32, A_MV)
        levels_in = arena("levels_in", [P, len(LEVELS), P], F32, A_QNT)
        qrt = arena("qrt", [P, 4, SEQ], F32, A_QRT)
        qr = arena("qr", [P, NT, 8, MLA_ROPE], F32, A_QR)
        gqt = arena("gqt", [P, 2, SEQ], F32, A_GQT)
        gkt = arena("gkt", [P, 2, SEQ], F32, A_GKT)
        dqt = arena("dqt", [P, 3, SEQ], F32, A_QR)
        dkt = arena("dkt", [P, 3, SEQ], F32, A_QR + 3 * SEQ)
        logs = arena("logs", [P, 2, SEQ], F32, A_B)
        ql = arena("ql", [P, 2, 2, SEQ], F32, A_QL)
        kl = arena("kl", [P, 2, 2, SEQ], F32, A_KL)
        grt = arena("grt", [GLA_RANK, SEQ], F32, A_QL)
        squares = arena("squares", [P, NT, 4, P], F32, A_QL)
        att = arena("att", [P, 2, NT, 2, P], F32, A_ATT)
        cross = arena("cross", [P, 2, 2, P], F32, A_CROSS)
        gate_z = arena("gate_z", [P, 2, SEQ], F32, A_ATT)
        gate_e = arena("gate_e", [P, 2, SEQ], F32, A_ATT + 2 * SEQ)
        lam_prod = arena("lam_prod", [P, 2 * DIFF_HD], F32, A_CROSS)
        ones = arena("ones", [P, SEQ], F32, A_CROSS)
        e = [arena(f"e{i}", [P, 3 * P], F32, at) for i, at in enumerate((A_E1, A_E2, A_ATT, A_ATT + 3 * P))]
        pt = [arena(f"pt{i}", [P, 3 * P], F32, at) for i, at in enumerate((A_PT, A_KL, A_KL + 3 * P))]
        xn = arena("xn", [P, NT, D_MODEL], F32, 0)
        f_hi = arena("f_hi", [P, FT, SEQ], F32R, 0)
        f_lo = arena("f_lo", [P, FT, SEQ], F32R, FT * SEQ)
        xt_hi = place("xt_hi", [P, KT, SEQ], F32R, xt_at)
        xt_lo = place("xt_lo", [P, KT, SEQ], F32R, xt_at + 4 * KT * SEQ)
        last_gain = place("last_gain", [P, D_MODEL], F32, xt_at)
        row_sb = place("row_sb", [P, W_END], F32, g_at)
        gw_sb = place("gw_sb", [GLA_RANK, GLA_HEADS * GLA_DK], F32, g_at + 4 * W_END)
        small_at = g_at + 4 * (W_END + GLA_HEADS * GLA_DK)
        m_ss = place("m_ss", [P, 4], F32, small_at)
        rsum = place("rsum", [P, 4], F32, small_at + 32)
        held = place("held", [P, 2 * MLA_HEADS], F32, small_at + 64)
        lam2 = place("lam2", [P, 2], F32, small_at + 128)
        lam2e = place("lam2e", [P, 2], F32, small_at + 160)
        lam = place("lam", [P, 1], F32, small_at + 192)
        junk = place("junk", [P, NCH], F32, g_at)
        act_sb = place("act_sb", [P, NT, NCH], F32, g_at)

        resid = sb("resid", [P, NT, D_MODEL], F32)
        stage = [place(f"stage{i}", [P, 4 * NCH], F32, stage_at + 16 * NCH * i) for i in range(4)]
        w_lo = [place(f"w_lo{i}", [P, 4 * NCH], F32R, stage_at + 16 * NCH * i) for i in range(4)]
        w_hi = [sb(f"w_hi{i}", [P, 4 * NCH], F32R) for i in range(4)]
        k_sb = sb("k_sb", [P, K_END], F32)
        gain_sb = sb("gain_sb", [P, DEPTH, G_END], F32)
        lev_sb = sb("lev_sb", [P, len(LEVELS), P], U8)
        caus_sb = sb("caus_sb", [P, 2 * P], F32)
        cos_sb = sb("cos_sb", [P, NT, 1, 32], F32)
        sin_sb = sb("sin_sb", [P, NT, 1, 32], F32)
        pos_i = sb("pos_i", [P, NT], I32)
        pos_f = sb("pos_f", [P, NT], F32)
        ssq = sb("ssq", [P, NT, 4], F32)
        ms = sb("ms", [P, 8], F32)
        rstd = sb("rstd", [P, 8], F32)
        rstd_x = sb("rstd_x", [P, NT], F32)
        halves = sb("halves", [P, 8], F32)
        mx = sb("mx", [P, 8], F32)
        nmx = sb("nmx", [P, 8], F32)
        esum = sb("esum", [P, 8], F32)

        ident = k_sb[:, K_ID:K_ID + P]
        bank = [ctx.enter_context(nc.psum_tensor(f"bank{i}", [P, NCH], F32)) for i in range(8)]

        full = [sem(f"full{s}") for s in range(4)]
        hi_made = [sem(f"hi_made{s}") for s in range(4)]
        lo_made = [sem(f"lo_made{s}") for s in range(4)]
        used = [sem(f"used{s}") for s in range(4)]
        acc_out_act = [sem(f"acc_out_act{p}") for p in range(2)]
        acc_out_vec = [sem(f"acc_out_vec{p}") for p in range(2)]
        bank_full = {b: sem(f"bank_full{b}") for b in USES}
        bank_free = {b: sem(f"bank_free{b}") for b in USES}
        setup_in, rows_in, halves_made = sem("setup_in"), sem("rows_in"), sem("halves_made")
        consts_in = sem("consts_in")
        x_in = [sem(f"x_in{c}") for c in range(4)]
        squared = sem("squared")
        x_added = sem("x_added")
        ms_made, rstd_made = sem("ms_made"), sem("rstd_made")
        xn_act = sem("xn_act")
        xt_hi_made = sem("xt_hi_made")
        m_squared, qa_scaled = sem("m_squared"), sem("qa_scaled")
        qa_hi_made = sem("qa_hi_made")
        roped, rope_mul = sem("roped"), sem("rope_mul")
        kr_in = sem("kr_in")
        gate_neg, gate_ln, gate_silu = sem("gate_neg"), sem("gate_ln"), sem("gate_silu")
        span_made, decay_made, level_made = sem("span_made"), sem("decay_made"), sem("level_made")
        gla_mixed, diff_mixed = sem("gla_mixed"), sem("diff_mixed")
        masked, exped, probs_made = sem("masked"), sem("exped"), sem("probs_made")
        sums_inverted = sem("sums_inverted")
        lam_dot, lam_exp = sem("lam_dot"), sem("lam_exp")
        silu_made, act_made, ft_hi_made = sem("silu_made"), sem("act_made"), sem("ft_hi_made")
        positions_made, angles, waves = sem("positions_made"), sem("angles"), sem("waves")
        act_chain, vec_chain = sem("act_chain"), sem("vec_chain")
        out_made, stored = sem("out_made"), sem("stored")

        def e_of(j):
            return (e[j % 2],) if j < MLA_HEADS else e[2 * (j % 2):2 * (j % 2) + 2]

        def decay_of(i):
            return p2[:, :, SEQ * (i % 2):SEQ * (i % 2) + SEQ]

        def p2c(t, col, n):
            return p2[:, t, col - C_GQ:col - C_GQ + n]

        def projected(t, col, n):
            return pd[:, t, col:col + n] if col < C_GQ else p2c(t, col, n)

        def unit_shape(n):
            n %= UNITS
            if n < U_MLA:
                return 4, EARLY[n // 4][1]
            if n < U_LATE:
                return (4, MLA_NOPE + MLA_ROPE) if n % 2 == 0 else (2, MLA_NOPE + MLA_VD)
            if n < U_OUT:
                return 4, LATE[(n - U_LATE) // 4][1]
            if n < U_DOWN:
                return 4, NCH
            return len(DOWN_KT[(n - U_DOWN) % len(DOWN_KT)]), NCH

        block = ctx.enter_context(nc.Block())

        @block.sync
        def _(sp):
            sp.dma_start(k_sb[:, :], consts).then_inc(consts_in, 16)
            for c in range(4):
                part = slice(c * NCH, (c + 1) * NCH)
                sp.dma_start(resid[:, :, part], x[:, part].rearrange("(t p) d -> p t d", p=P)).then_inc(x_in[c], 16)
            sp.dma_start(gain_sb[:, :, :], gains).then_inc(setup_in, 16)
            sp.dma_start(pos_i[:, :], positions).then_inc(setup_in, 16)
            sp.dma_start(levels_in[:, :, :], levels).then_inc(setup_in, 16)
            sp.dma_start(caus_sb[:, :], causal).then_inc(setup_in, 16)

            def load(quad, n, sources, second_first=False):
                s = n % 4
                kts, cols = unit_shape(n)
                view = stage[s][:, 0:kts * cols].rearrange("p (k n) -> p k n", k=kts)
                sp.wait_ge(used[s], quad + 1)
                parts = []
                for src in sources:
                    at, m = sum(n_rows for _, n_rows, _ in parts), src.shape[0] // P
                    parts.append((at, m, src))
                for at, m, src in reversed(parts) if second_first else parts:
                    sp.dma_start(view[:, at:at + m, :], src.rearrange("(k p) n -> p k n", p=P)).then_inc(full[s], 16)

            def halves_of(w, layer, kts, col, cols):
                kts = list(kts)
                cut = (len(kts) + 1) // 2
                return [w[layer, part[0] * P:(part[-1] + 1) * P, bass.ds(col, cols)] for part in (kts[:cut], kts[cut:])]

            with sp.Fori(0, DEPTH) as layer:
                def quad(n):
                    return layer * QUADS + n // 4

                for n in range(U_MLA):
                    col, cols = EARLY[n // 4]
                    load(quad(n), n, halves_of(w_in, layer, range(4 * (n % 4), 4 * (n % 4) + 4), col, cols))
                    if n == 7:
                        sp.wait_ge(squared, layer * 16 + 8)
                        sp.dma_start(row_sb[:, :], rows[layer].to_broadcast([P, W_END])).then_inc(rows_in, 16)
                        sp.dma_start(gw_sb[:, :], gate_w[layer]).then_inc(rows_in, 16)
                for h in range(MLA_HEADS):
                    n = U_MLA + 2 * h
                    load(quad(n), n, halves_of(w_q_b, layer, range(4), 192 * h, 192))
                    load(quad(n + 1), n + 1, halves_of(w_kv_b, layer, range(2), 256 * h, 256))
                for n in range(U_LATE, U_OUT):
                    i = n - U_LATE
                    col, cols = LATE[i // 4]
                    load(quad(n), n, halves_of(w_in, layer, range(4 * (i % 4), 4 * (i % 4) + 4), col, cols), i == 0)
                for pair in range(2):
                    for i in range(8):
                        n = U_OUT + 8 * pair + i
                        load(quad(n), n, [part for kts in (OUT_KT[i // 2][:2], OUT_KT[i // 2][2:])
                                          for part in [w_out[layer, kts[0] * P:(kts[1] + 1) * P,
                                                             bass.ds((2 * pair + i % 2) * NCH, NCH)]]])
                with sp.Fori(0, FF_CHUNKS) as f:
                    for i in range(8):
                        w = w_gate if i < 4 else w_up
                        load(quad(U_FF + i) + 2 * f, U_FF + i,
                             halves_of(w, layer, range(4 * (i % 4), 4 * (i % 4) + 4), f * NCH, NCH))
                for c in range(4):
                    for i, kts in enumerate(DOWN_KT):
                        n = U_DOWN + len(DOWN_KT) * c + i
                        load(quad(n), n, halves_of(w_down, layer, kts, c * NCH, NCH))
            for n in range(LEAD - 1):
                load(DEPTH * QUADS, n, halves_of(w_in, 0, range(4 * n, 4 * n + 4), EARLY[0][0], EARLY[0][1]))
            sp.wait_ge(act_made, DEPTH * FF_CHUNKS * NT)
            sp.dma_start(last_gain[:, :], final_norm.to_broadcast([P, D_MODEL])).then_inc(setup_in, 16)
            for t in range(NT):
                sp.wait_ge(out_made, t + 1)
                sp.dma_start(out[t * P:(t + 1) * P, :], xn[:, t, :]).then_inc(stored, 16)
            sp.wait_ge(stored, 16 * NT)

        @block.tensor
        def _(pe):
            pe.wait_ge(consts_in, 16)
            with pe.Fori(0, DEPTH) as layer:
                def need(s, per_layer, k):
                    pe.wait_ge(s, layer * per_layer + k)

                def bank_taken(key, b):
                    need(bank_free[b], USES[b], ROUND[key][b] + 1)
                    return bank[b]

                def copied(key, b):
                    need(bank_free[b], USES[b], ROUND[key][b] + 2)

                def projected_by_now(chunks):
                    parity, r = chunk_round(chunks - 1)
                    need(acc_out_act[parity], R_OUT, r + 1)
                    need(acc_out_vec[parity], R_OUT, r + 1)

                def transpose(dst, src):
                    return pe.transpose(dst, src, ident)

                def unit(n, kts, parity, hi, lo, first, last, turn=0):
                    s = n % 4
                    _, cols = unit_shape(n)
                    pe.wait_ge(lo_made[s], layer * QUADS + n // 4 + 1 + turn)
                    wh = w_hi[s][:, 0:len(kts) * cols].rearrange("p (k n) -> p k n", n=cols)
                    wl = w_lo[s][:, 0:len(kts) * cols].rearrange("p (k n) -> p k n", n=cols)
                    for i, kt in enumerate(kts):
                        for t in range(NT):
                            acc = bank[2 * parity + t][:, 0:cols]
                            a = hi[:, kt, t * P:(t + 1) * P]
                            b = lo[:, kt, t * P:(t + 1) * P]
                            pe.matmul(acc, a, wh[:, i, :], start=first and i == 0, stop=False)
                            pe.matmul(acc, a, wl[:, i, :], start=False, stop=False)
                            mm = pe.matmul(acc, b, wh[:, i, :], start=False, stop=last and i == len(kts) - 1)
                    mm.then_inc(used[s], 1)

                def acc_taken(parity, r, in_loop=False, f=0):
                    if r == 0:
                        need(x_added, 16, NT * (3 + parity))
                        return
                    if r <= R_OUT:
                        need(acc_out_act[parity], R_OUT, r)
                        need(acc_out_vec[parity], R_OUT, r)
                    elif r < R_FF or r == R_FF and not in_loop:
                        need(x_added, 16, 8 + NT * (2 * (r - 1 - R_OUT) + parity + 1))
                    elif r == R_FF:
                        need((silu_made, act_made)[parity], FF_CHUNKS * NT, NT * f)
                    elif r == R_DOWN:
                        need((silu_made, act_made)[parity], FF_CHUNKS * NT, NT * FF_CHUNKS)
                    else:
                        need(x_added, 16, 16 + NT * (parity + 1))

                def norm_turn(which, rounds):
                    for r in rounds:
                        need(x_added, 16, (0 if which == "norm1" else 8) + NT * (r // 2 + 1))
                        b = 4 + r % 4
                        ps = bank_taken((which, r), b)
                        for i in range(2):
                            for t in range(NT):
                                kt = 2 * r + i
                                mm = transpose(ps[:, i * SEQ + t * P:i * SEQ + (t + 1) * P], resid[:, t, kt * P:(kt + 1) * P])
                        mm.then_inc(bank_full[b], 1)

                def qa_turn(b):
                    need(qa_scaled, 1, 1)
                    ps = bank_taken(("qa_turn", b), 4 + b)
                    for i in range(2):
                        for t in range(NT):
                            mm = transpose(ps[:, i * SEQ + t * P:i * SEQ + (t + 1) * P],
                                           p2c(t, C_QA + (2 * b + i) * P, P))
                    mm.then_inc(bank_full[4 + b], 1)

                def mla_unit(h, kv):
                    n = U_MLA + 2 * h + kv
                    s, (kts, cols) = n % 4, unit_shape(n)
                    if h == 0:
                        for b in range(3):
                            copied(("qa_turn", b), 4 + b)
                    pe.wait_ge(lo_made[s], layer * QUADS + n // 4 + 1)
                    need(acc_out_act[kv], R_OUT, R_MLA + max(h - 1, 0))
                    need(acc_out_vec[kv], R_OUT, R_MLA + max(h - 1, 0))
                    wh = w_hi[s][:, 0:kts * cols].rearrange("p (k n) -> p k n", n=cols)
                    wl = w_lo[s][:, 0:kts * cols].rearrange("p (k n) -> p k n", n=cols)
                    ps, k0 = bank[2 * kv + h % 2], 4 * kv
                    for k in range(kts):
                        a, b = wh[:, k, 0:P], wl[:, k, 0:P]
                        pe.matmul(ps[:, 0:SEQ], a, qa_hi[:, k0 + k, :], start=k == 0, stop=False)
                        pe.matmul(ps[:, 0:SEQ], a, qa_lo[:, k0 + k, :], start=False, stop=False)
                        pe.matmul(ps[:, 0:SEQ], b, qa_hi[:, k0 + k, :], start=False, stop=k == kts - 1)
                    w = cols - P
                    for t in range(NT):
                        dst = ps[:, SEQ + t * w:SEQ + (t + 1) * w]
                        for k in range(kts):
                            a = qa_hi[:, k0 + k, t * P:(t + 1) * P]
                            b = qa_lo[:, k0 + k, t * P:(t + 1) * P]
                            pe.matmul(dst, a, wh[:, k, P:cols], start=k == 0, stop=False)
                            pe.matmul(dst, a, wl[:, k, P:cols], start=False, stop=False)
                            mm = pe.matmul(dst, b, wh[:, k, P:cols], start=False, stop=k == kts - 1)
                    mm.then_inc(used[s], 1)

                def gla_turn(_):
                    projected_by_now(5)
                    for b, col in ((4, C_GQ), (5, C_GK)):
                        ps = bank_taken(("gla_turn", 0), b)
                        for g in range(2):
                            for t in range(NT):
                                mm = transpose(ps[:, g * SEQ + t * P:g * SEQ + (t + 1) * P], p2c(t, col + g * P, P))
                        mm.then_inc(bank_full[b], 1)
                    ps = bank_taken(("gla_turn", 0), 6)
                    for t in range(NT):
                        mm = transpose(ps[:, t * P:(t + 1) * P], p2c(t, C_GR, P))
                    mm.then_inc(bank_full[6], 1)

                def gla_logits(_):
                    copied(("gla_turn", 0), 6)
                    need(rows_in, 32, 32)
                    ps = bank_taken(("gla_logits", 0), 7)
                    for g in range(2):
                        mm = pe.matmul(ps[:, g * SEQ:(g + 1) * SEQ], gw_sb[:, g * P:(g + 1) * P], grt[:, :],
                                       start=True, stop=True)
                    mm.then_inc(bank_full[7], 1)

                def level_mm(i):
                    if i == 0:
                        copied(("gla_turn", 0), 4)
                        copied(("gla_turn", 0), 5)
                    if i < N_LEVELS - 1:
                        need(level_made, N_LEVELS - 1, i + 1)
                    q, k = (gqt, gkt) if i == N_LEVELS - 1 else (ql[:, i % 2], kl[:, i % 2])
                    for par in range(2):
                        ps = bank_taken(("level_mm", i), 6 + par)
                        rows_ = slice(par * 64, par * 64 + 64)
                        for g in range(2):
                            if i == 0:
                                mm = pe.matmul(ps[:, g * P:(g + 1) * P], k[rows_, g, 0:P], q[rows_, g, P:SEQ],
                                               start=True, stop=True)
                                continue
                            for t in range(NT):
                                at = (t * 2 + g) * P
                                mm = pe.matmul(ps[:, at:at + P], k[rows_, g, t * P:(t + 1) * P],
                                               q[rows_, g, t * P:(t + 1) * P], start=True, stop=True)
                        mm.then_inc(bank_full[6 + par], 1)

                def gla_out(_):
                    copied(("level_mm", N_LEVELS - 1), 7)
                    for t in range(NT):
                        ps = bank_taken(("gla_out", 0), 6 + t)
                        for h in range(GLA_HEADS):
                            dst, par, g = ps[:, h * P:(h + 1) * P], h % 2, h // 2
                            if t == 1:
                                pe.matmul(dst, cross[:, par, g, :], p2c(0, C_GV + h * P, P), start=True, stop=False)
                            mm = pe.matmul(dst, att[:, par, t, g, :], p2c(t, C_GV + h * P, P), start=t == 0, stop=True)
                        mm.then_inc(bank_full[6 + t], 1)

                def rope_turn(_):
                    need(roped, 1, 1)
                    for b in range(2):
                        ps = bank_taken(("rope_turn", 0), 4 + b)
                        for i in range(2):
                            for t in range(NT):
                                pair = 2 * b + i
                                mm = transpose(ps[:, i * SEQ + t * P:i * SEQ + (t + 1) * P],
                                               qr[:, t, 2 * pair:2 * pair + 2, :].rearrange("p a b -> p (a b)"))
                        mm.then_inc(bank_full[4 + b], 1)

                def diff_turn(i):
                    g, part = i // 2, i % 2
                    projected_by_now(7 + i)
                    for b, heads in ((4, (0, 1)), (5, (2,))):
                        ps = bank_taken(("diff_turn", i), b)
                        for k, h in enumerate(heads):
                            for t in range(NT):
                                col = part * DIFF_QK + (3 * g + h) * P
                                mm = transpose(ps[:, k * SEQ + t * P:k * SEQ + (t + 1) * P], pd[:, t, col:col + P])
                        mm.then_inc(bank_full[b], 1)

                def head_scores(j):
                    key = ("head_scores", j)
                    if j < MLA_HEADS:
                        if j == 0:
                            copied(("rope_turn", 0), 4)
                            copied(("rope_turn", 0), 5)
                            for parity in range(2):
                                need(acc_out_act[parity], R_OUT, R_LATE)
                        ps = bank_taken(key, 6)
                        r = slice(64 * (j % 2), 64 * (j % 2) + 64)
                        for t in range(NT):
                            dst = ps[:, t * P:t * P + (t + 1) * P]
                            n = (t + 1) * P
                            pe.matmul(dst, qnt[:, j, t * P:n], knt[:, j, 0:n], start=True, stop=False)
                            mm = pe.matmul(dst, qrt[r, j // 2, t * P:n], qrt[r, 3, 0:n], start=False, stop=True)
                        mm.then_inc(bank_full[6], 1)
                        return
                    h = j - MLA_HEADS
                    copied(("diff_turn", 2 * (h // 3) + 1), 4)
                    copied(("diff_turn", 2 * (h // 3) + 1), 5)
                    for branch in range(2):
                        ps = bank_taken(key, 6 + branch)
                        r = slice(64 * branch, 64 * branch + 64)
                        for t in range(NT):
                            n = (t + 1) * P
                            mm = pe.matmul(ps[:, t * P:t * P + n], dqt[r, h % 3, t * P:n], dkt[r, h % 3, 0:n],
                                           start=True, stop=True)
                        mm.then_inc(bank_full[6 + branch], 1)

                def head_turn(j):
                    if j < MLA_HEADS:
                        need(exped, HEADS, j + 1)
                    else:
                        need(probs_made, DIFF_HEADS, j - MLA_HEADS + 1)
                    ps = bank_taken(("head_turn", j), 4)
                    for i in range(3):
                        mm = transpose(ps[:, i * P:(i + 1) * P], e_of(j)[0][:, i * P:(i + 1) * P])
                    mm.then_inc(bank_full[4], 1)

                def head_out(j):
                    copied(("head_turn", j), 4)
                    if j == 0:
                        need(acc_out_vec[1], R_OUT, R_LATE)
                    if j in (MLA_HEADS, MLA_HEADS + 3):
                        projected_by_now(11 + (j - MLA_HEADS) // 3)

                    def v(t):
                        if j < MLA_HEADS:
                            return mv[:, t, j, :]
                        return pd[:, t, C_DV + (j - MLA_HEADS) * P:C_DV + (j - MLA_HEADS + 1) * P]

                    ps, p = bank_taken(("head_out", j), 5), pt[PT_OF[j]]
                    pe.matmul(ps[:, 0:P], p[:, 0:P], v(0), start=True, stop=True)
                    pe.matmul(ps[:, P:2 * P], p[:, P:2 * P], v(0), start=True, stop=False)
                    pe.matmul(ps[:, P:2 * P], p[:, 2 * P:3 * P], v(1), start=False, stop=True).then_inc(bank_full[5], 1)

                def mix_turn(kt0):
                    b = 4 + kt0 // 2 % 2
                    if kt0 in (6, 8):
                        need(gla_mixed, 1, 1)
                    elif kt0 >= 10:
                        if b != 5:
                            copied(("head_out", kt0 - 10 + 1), 5)
                    else:
                        need(diff_mixed, 2, 2 if kt0 else 1)
                    ps = bank_taken(("mix_turn", kt0), b)
                    for i in range(2):
                        for t in range(NT):
                            kt = kt0 + i
                            src = (pd[:, t, C_DV + kt * P:C_DV + (kt + 1) * P] if kt < 6 else
                                   p2c(t, C_GV + (kt - 6) * P, P) if kt < 10 else mv[:, t, kt - 10, :])
                            mm = transpose(ps[:, i * SEQ + t * P:i * SEQ + (t + 1) * P], src)
                    mm.then_inc(bank_full[b], 1)

                steps = {"qa_turn": qa_turn, "gla_turn": gla_turn, "gla_logits": gla_logits, "level_mm": level_mm,
                         "gla_out": gla_out, "rope_turn": rope_turn, "diff_turn": diff_turn, "head_scores": head_scores,
                         "head_turn": head_turn, "head_out": head_out, "mix_turn": mix_turn}

                def hook(n):
                    for name, arg in HOOKS.get(n, []):
                        if name in steps:
                            steps[name](arg)

                norm_turn("norm1", range(KT // 4))
                for c in range(len(EARLY)):
                    acc_taken(c % 2, c // 2)
                    for u in range(4):
                        if c == 0:
                            for r in (2 * u, 2 * u + 1):
                                copied(("norm1", r), 4 + r % 4)
                        n = 4 * c + u
                        unit(n, range(4 * u, 4 * u + 4), c % 2, xt_hi, xt_lo, u == 0, u == 3)
                        if n == 0:
                            norm_turn("norm1", range(KT // 4, KT // 2))
                        hook(n)
                for h in range(MLA_HEADS):
                    for kv in range(2):
                        mla_unit(h, kv)
                        hook(U_MLA + 2 * h + kv)
                for c in range(len(LATE)):
                    acc_taken(c % 2, R_LATE + c // 2)
                    for u in range(4):
                        n = U_LATE + 4 * c + u
                        unit(n, range(4 * u, 4 * u + 4), c % 2, xt_hi, xt_lo, u == 0, u == 3)
                        hook(n)
                for pair in range(2):
                    acc_taken(0, R_OUT + pair)
                    acc_taken(1, R_OUT + pair)
                    for i in range(8):
                        if pair == 0 and i % 2 == 0:
                            for kt0 in {kt - kt % 2 for kt in OUT_KT[i // 2]}:
                                copied(("mix_turn", kt0), 4 + kt0 // 2 % 2)
                        n = U_OUT + 8 * pair + i
                        unit(n, OUT_KT[i // 2], i % 2, xt_hi, xt_lo, i < 2, i >= 6)
                        hook(n)
                norm_turn("norm2", range(KT // 4))

                def ff_turn(f):
                    pe.wait_ge(act_made, layer * (FF_CHUNKS * NT) + NT * f + NT)
                    for b in (4, 5):
                        pe.wait_ge(bank_free[b], layer * USES[b] + ROUND[("ff_turn", 0)][b] + f + 1)
                        for i in range(2):
                            for t in range(NT):
                                j = 2 * (b - 4) + i
                                mm = transpose(bank[b][:, i * SEQ + t * P:i * SEQ + (t + 1) * P],
                                               act_sb[:, t, j * P:(j + 1) * P])
                        mm.then_inc(bank_full[b], 1)

                def ff_chunk(f, first):
                    for half in range(2):
                        acc_taken(half, R_FF, not first, f)
                        for u in range(4):
                            if first and half == 0:
                                for r in (2 * u, 2 * u + 1):
                                    copied(("norm2", r), 4 + r % 4)
                            unit(U_FF + 4 * half + u, range(4 * u, 4 * u + 4), half, xt_hi, xt_lo, u == 0, u == 3,
                                 turn=2 * f)
                            if first and half == 0 and u == 0:
                                norm_turn("norm2", range(KT // 4, KT // 2))
                            if half == 0 and u == 1 and not first:
                                ff_turn(f - 1)

                ff_chunk(0, True)
                with pe.Fori(1, FF_CHUNKS) as f:
                    ff_chunk(f, False)
                for c in range(4):
                    acc_taken(c % 2, R_DOWN + c // 2)
                    for i, kts in enumerate(DOWN_KT):
                        if c == 0 and i in (0, 10):
                            for b in (4, 5):
                                need(bank_free[b], USES[b], USES[b] + (i != 0))
                        unit(U_DOWN + len(DOWN_KT) * c + i, kts, c % 2, f_hi, f_lo, i == 0, i == len(DOWN_KT) - 1)
                        if c == 0 and i == 1:
                            ff_turn(FF_CHUNKS - 1)

        @block.scalar
        def _(act):
            count = [0]

            def link(ins):
                count[0] += 1
                ins.then_inc(act_chain, 1)
                return count[0]

            for c in range(3):
                act.wait_ge(x_in[c], 16)
                for t in range(NT):
                    if t + c:
                        act.wait_ge(squared, NT * c + t)
                    act.activation(junk[:, :], resid[:, t, c * NCH:(c + 1) * NCH], ACT.Square,
                                   accum_out=ssq[:, t, c:c + 1]).then_inc(squared, 1)
            def round_unit(quad, n):
                s = n % 4
                kts, cols = unit_shape(n)
                act.wait_ge(full[s], (quad + 1) * 32)
                act.activation(w_hi[s][:, 0:kts * cols], stage[s][:, 0:kts * cols], ACT.Copy).then_inc(hi_made[s], 1)

            for n in range(LEAD - 1):
                round_unit(0, n)
            act.wait_ge(setup_in, 64)

            with act.Fori(0, DEPTH) as layer:
                def need(s, per_layer, k):
                    act.wait_ge(s, layer * per_layer + k)

                def bank_in(key, b):
                    need(bank_full[b], USES[b], ROUND[key][b] + 1)
                    return bank[b]

                def complete(n):
                    need(used[n % 4], QUADS, n // 4 + 2)

                def gain(i):
                    return gain_sb[:, bass.ds(layer, 1), i:i + 1].rearrange("p a b -> p (a b)")

                def squares_of(c, done):
                    for t in range(NT):
                        need(x_added, 16, done + NT * c + t + 1)
                        need(squared, 16, done + NT * c + t)
                        act.activation(junk[:, :], resid[:, t, c * NCH:(c + 1) * NCH], ACT.Square,
                                       accum_out=ssq[:, t, c:c + 1]).then_inc(squared, 1)

                def norm(which, seen):
                    g0 = G_ATTN if which == "norm1" else G_FFN
                    for r in range(KT // 2):
                        if r == KT // 4:
                            n = (U_FF if seen else 0) + LEAD - 1
                            round_unit(layer * QUADS + n // 4, n)
                        ps = bank_in((which, r), 4 + r % 4)
                        for i in range(2):
                            act.activation(xt_hi[:, 2 * r + i, :], ps[:, i * SEQ:(i + 1) * SEQ], ACT.Copy,
                                           scale=gain(g0 + 2 * r + i)).then_inc(xt_hi_made, 1)
                    squares_of(3, 8 * seen)

                def evac(c):
                    if c == 0:
                        need(rstd_made, len(POW), POW["norm1"] + 1)
                    col, cols = (EARLY + LATE)[c]
                    complete(4 * c + 3 if c < len(EARLY) else U_LATE + 4 * (c - len(EARLY)) + 3)
                    act.activation(projected(0, col, cols), bank[2 * (c % 2)][:, 0:cols], ACT.Copy, scale=rstd_x[:, 0:1])\
                       .then_inc(acc_out_act[c % 2], 1)

                def angles_made(_):
                    need(angles, NT, NT)
                    act.activation(sin_sb[:, :, 0, :], sin_sb[:, :, 0, :], ACT.Sin)
                    act.activation(cos_sb[:, :, 0, :], cos_sb[:, :, 0, :], ACT.Sin).then_inc(waves, 1)

                def qa_rms(_):
                    need(acc_out_vec[1], R_OUT, 1)
                    need(acc_out_act[1], R_OUT, 1)
                    for t in range(NT):
                        for i, (col, n) in enumerate(((C_QA, MLA_Q_RANK), (C_KVA, MLA_KV_RANK))):
                            at, m = 4 * i + t * n // SEQ, n // SEQ
                            act.activation(qnt[:, at:at + m, :].rearrange("p a b -> p (a b)"), p2c(t, col, n), ACT.Square,
                                           accum_out=m_ss[:, 2 * i + t:2 * i + t + 1]).then_inc(m_squared, 1)

                def qa_turn(b):
                    ps = bank_in(("qa_turn", b), 4 + b)
                    for i in range(2):
                        act.activation(qa_hi[:, 2 * b + i, :], ps[:, i * SEQ:(i + 1) * SEQ], ACT.Copy,
                                       scale=gain(G_QA + 2 * b + i)).then_inc(qa_hi_made, 1)

                def mla_q(h):
                    complete(U_MLA + 2 * h)
                    act.activation(qnt[:, h, :], bank[h % 2][:, 0:SEQ], ACT.Copy).then_inc(acc_out_act[0], 1)

                def mla_kv(h):
                    complete(U_MLA + 2 * h + 1)
                    act.activation(knt[:, h, :], bank[2 + h % 2][:, 0:SEQ], ACT.Copy).then_inc(acc_out_act[1], 1)

                def gla_turn(_):
                    ps = bank_in(("gla_turn", 0), 6)
                    act.activation(grt[:, :], ps[0:GLA_RANK, 0:SEQ], ACT.Copy).then_inc(bank_free[6], 1)
                    ps = bank_in(("gla_turn", 0), 4)
                    act.activation(gqt[:, :, :].rearrange("p a b -> p (a b)"), ps[:, :], ACT.Copy,
                                   scale=GLA_DK ** -0.5).then_inc(bank_free[4], 1)

                def gla_decay(_):
                    need(gate_neg, 1, 1)
                    link(act.activation(gate_e[:, :, :], gate_e[:, :, :], ACT.Exp))
                    need(act_chain, ACT_LINKS, count[0])
                    act.activation(gate_e[:, :, :], gate_e[:, :, :], ACT.Ln, bias=1.0).then_inc(gate_ln, 1)

                def gla_silu(_):
                    need(acc_out_vec[1], R_OUT, 3)
                    need(acc_out_act[1], R_OUT, 3)
                    for t in range(NT):
                        act.activation(p2c(t, C_GO, NCH), p2c(t, C_GO, NCH), ACT.Silu).then_inc(gate_silu, 1)

                def level_exp(i):
                    need(span_made, N_LEVELS - 1, i + 1)
                    act.activation(decay_of(i), decay_of(i), ACT.Exp, scale=1.0 / GLA_TAU).then_inc(decay_made, 1)

                def rope_turn(_):
                    ps = bank_in(("rope_turn", 0), 4)
                    act.activation(qrt[:, 0:2, :].rearrange("p a b -> p (a b)"), ps[:, :], ACT.Copy)\
                       .then_inc(bank_free[4], 1)

                def diff_turn(i):
                    dst = dkt if i % 2 else dqt
                    ps = bank_in(("diff_turn", i), 4)
                    act.activation(dst[:, 0:2, :].rearrange("p a b -> p (a b)"), ps[:, :], ACT.Copy)\
                       .then_inc(bank_free[4], 1)

                def head_exp(j):
                    scale = (MLA_NOPE + MLA_ROPE) ** -0.5 if j < MLA_HEADS else DIFF_HD ** -0.5
                    if j == MLA_HEADS:
                        need(lam_dot, 1, 1)
                        act.activation(lam2e[:, :], lam2[:, :], ACT.Exp).then_inc(lam_exp, 1)
                    need(masked, HEADS, j + 1)
                    for branch in range(1 if j < MLA_HEADS else 2):
                        for t in range(NT):
                            k = 4 * (j % 2) + 2 * branch + t
                            part = e_of(j)[branch][:, t * P:t * P + (t + 1) * P]
                            last = act.activation(part, part, ACT.Exp, bias=nmx[:, k:k + 1], scale=scale,
                                                  accum_out=esum[:, k:k + 1])
                    last.then_inc(exped, 1)

                def head_turn(j):
                    ps = bank_in(("head_turn", j), 4)
                    act.activation(pt[PT_OF[j]][:, :], ps[:, 0:3 * P], ACT.Copy).then_inc(bank_free[4], 1)

                def mix_turn(kt0):
                    ps = bank_in(("mix_turn", kt0), 4 + kt0 // 2 % 2)
                    act.activation(xt_hi[:, kt0:kt0 + 2, :].rearrange("p a b -> p (a b)"), ps[:, :], ACT.Copy)\
                       .then_inc(xt_hi_made, 2)

                steps = {"evac": evac, "angles": angles_made, "qa_rms": qa_rms, "qa_turn": qa_turn, "mla_q": mla_q, "mla_kv": mla_kv,
                         "gla_turn": gla_turn, "gla_decay": gla_decay, "gla_silu": gla_silu, "level_exp": level_exp,
                         "rope_turn": rope_turn, "diff_turn": diff_turn, "head_exp": head_exp,
                         "head_turn": head_turn, "mix_turn": mix_turn}

                norm("norm1", 0)
                for n in range(U_FF):
                    if n < U_FF - 1:
                        round_unit(layer * QUADS + (n + LEAD) // 4, n + LEAD)
                    for name, arg in HOOKS.get(n, []):
                        if name in steps:
                            steps[name](arg)
                    if n >= U_OUT and (n - U_OUT) % 8 >= 6 and n < U_FF - 1:
                        squares_of(2 * ((n - U_OUT) // 8) + (n - U_OUT) % 2, 8)
                norm("norm2", 1)

                def ff_turn(f):
                    for b in (4, 5):
                        act.wait_ge(bank_full[b], layer * USES[b] + ROUND[("ff_turn", 0)][b] + f + 1)
                        dst = f_hi[:, bass.ds(f * 4 + 2 * (b - 4), 2), :].rearrange("p a b -> p (a b)")
                        act.activation(dst, bank[b][:, :], ACT.Copy).then_inc(ft_hi_made, 1)

                def ff_chunk(f, first):
                    for i in range(8):
                        round_unit(layer * QUADS + (U_FF + i + LEAD) // 4 + 2 * f, U_FF + i + LEAD)
                        if i == 1 and not first:
                            ff_turn(f - 1)
                        if i == 3:
                            if first:
                                need(rstd_made, len(POW), POW["norm2"] + 1)
                            act.wait_ge(used[3], layer * QUADS + (U_FF + 3) // 4 + 2 + 2 * f)
                            for t in range(NT):
                                act.activation(act_sb[:, t, :], bank[t][:, :], ACT.Silu, scale=rstd_x[:, t:t + 1]).then_inc(silu_made, 1)

                ff_chunk(0, True)
                with act.Fori(1, FF_CHUNKS) as f:
                    ff_chunk(f, False)
                for n in range(U_DOWN, UNITS):
                    i = n - U_DOWN
                    if n < UNITS - 1:
                        round_unit(layer * QUADS + (n + LEAD) // 4, n + LEAD)
                    if i == 1:
                        ff_turn(FF_CHUNKS - 1)
                    if i % len(DOWN_KT) == len(DOWN_KT) - 1 and n < UNITS - 1:
                        squares_of(i // len(DOWN_KT), 16)
            for t in range(NT):
                act.wait_ge(x_added, 16 * DEPTH + 7 + t)
                act.wait_ge(squared, 16 * DEPTH + 6 + t)
                act.activation(junk[:, :], resid[:, t, 3 * NCH:4 * NCH], ACT.Square, accum_out=ssq[:, t, 3:4])\
                   .then_inc(squared, 1)
            act.wait_ge(rstd_made, DEPTH * len(POW) + 1)
            act.activation(xn[:, 1, :], resid[:, 1, :], ACT.Copy, scale=rstd_x[:, 1:2]).then_inc(xn_act, 1)
            assert count[0] == ACT_LINKS, count[0]

        @block.gpsimd
        def _(pool):
            pool.memset(halves[:, :], -0.5).then_inc(halves_made, 1)
            pool.wait_ge(halves_made, 1)
            with pool.Fori(0, DEPTH) as layer:
                def need(s, per_layer, k):
                    pool.wait_ge(s, layer * per_layer + k)

                def power(name, n, to=rstd):
                    need(ms_made, len(POW), POW[name] + 1)
                    pool.tensor_tensor(to[:, 0:n], ms[:, 0:n], halves[:, 0:n], ALU.pow).then_inc(rstd_made, 1)

                power("norm1", NT, rstd_x)
                for n in range(U_FF):
                    for name, arg in HOOKS.get(n, []):
                        if name == "qa_rms":
                            power("mla", 4)
                        if name == "gla_rms":
                            power("gla", 8)
                        if name == "diff_rms":
                            power(f"diff{arg}", 6)
                        if name == "level_exp":
                            need(decay_made, N_LEVELS - 1, arg + 1)
                            if arg == 0:
                                for b in (4, 5):
                                    need(bank_free[b], USES[b], ROUND[("gla_turn", 0)][b] + 2)
                            if arg >= 2:
                                need(bank_full[7], USES[7], ROUND[("level_mm", arg - 2)][7] + 1)
                            pool.tensor_tensor(ql[:, arg % 2], gqt[:, :, :], decay_of(arg), ALU.mult)
                            pool.tensor_tensor(kl[:, arg % 2], gkt[:, :, :], decay_of(arg), ALU.mult)\
                                .then_inc(level_made, 1)
                        if name == "rope":
                            need(kr_in, 1, 1)
                            need(waves, 1, 1)
                            cos = cos_sb[:, :, :, :].to_broadcast([P, NT, 7, 32])
                            sin = sin_sb[:, :, :, :].to_broadcast([P, NT, 7, 32])
                            a, b = qr[:, :, 0:7, 0:32], qr[:, :, 0:7, 32:64]
                            pool.tensor_tensor(turn1[:, :, :, :], a, cos, ALU.mult)
                            pool.tensor_tensor(turn2[:, :, :, :], b, sin, ALU.mult)
                            pool.tensor_tensor(turn3[:, :, :, :], a, sin, ALU.mult)
                            pool.tensor_tensor(turn4[:, :, :, :], b, cos, ALU.mult).then_inc(rope_mul, 1)
                power("norm2", NT, rstd_x)
            pool.wait_ge(ms_made, DEPTH * len(POW) + 1)
            pool.tensor_tensor(rstd_x[:, :], ms[:, 0:NT], halves[:, 0:NT], ALU.pow).then_inc(rstd_made, 1)

        @block.vector
        def _(vec):
            count = [0]

            def rest_of_unit(quad, n):
                s = n % 4
                kts, cols = unit_shape(n)
                vec.wait_ge(hi_made[s], quad + 1)
                vec.tensor_tensor(w_lo[s][:, 0:kts * cols], stage[s][:, 0:kts * cols],
                                  w_hi[s][:, 0:kts * cols].bitcast(F32), ALU.subtract).then_inc(lo_made[s], 1)

            for i, free in enumerate([*used, *bank_free.values()]):
                vec.memset(mx[:, i:i + 1], 0.0).then_inc(free, 1)

            for c in range(4):
                vec.wait_ge(x_in[c], 16)
                vec.memset(esum[:, c:c + 1], 1.0).then_inc(x_added, NT)

            vec.wait_ge(consts_in, 16)
            vec.wait_ge(setup_in, 64)
            vec.tensor_copy(lev_sb[:, :, :], levels_in[:, :, :])
            vec.tensor_copy(pos_f[:, :], pos_i[:, :]).then_inc(positions_made, 1)
            vec.wait_ge(positions_made, 1)
            for n in range(LEAD - 1):
                rest_of_unit(0, n)

            with vec.Fori(0, DEPTH) as layer:
                def need(s, per_layer, k):
                    vec.wait_ge(s, layer * per_layer + k)

                def link(ins):
                    count[0] += 1
                    ins.then_inc(vec_chain, 1)
                    need(vec_chain, VEC_LINKS, count[0])

                def bank_in(key, b):
                    need(bank_full[b], USES[b], ROUND[key][b] + 1)
                    return bank[b]

                def masked_bank_in(key, b):
                    turn = vec.to_reg(layer * USES[b] + (ROUND[key][b] + 1))
                    vec.wait_ge(setup_in, 64)
                    vec.wait_ge(bank_full[b], turn)
                    return bank[b]

                def complete(n):
                    need(used[n % 4], QUADS, n // 4 + 2)

                def copied(key, b):
                    need(bank_free[b], USES[b], ROUND[key][b] + 2)

                def gain(i):
                    return gain_sb[:, bass.ds(layer, 1), i:i + 1].rearrange("p a b -> p (a b)")

                def scaled(n, width, of):
                    vec.tensor_scalar(ms[:, 0:n], of, 1.0 / width, EPS, ALU.mult, ALU.add).then_inc(ms_made, 1)

                def norm(which, seen):
                    g0 = G_ATTN if which == "norm1" else G_FFN
                    for r in range(KT // 2):
                        if r == KT // 4:
                            n = (U_FF if seen else 0) + LEAD - 1
                            rest_of_unit(layer * QUADS + n // 4, n)
                        ps = bank_in((which, r), 4 + r % 4)
                        need(xt_hi_made, 48, 32 * seen + 2 * r + 2)
                        for i in range(2):
                            kt = 2 * r + i
                            ins = vec.scalar_tensor_tensor(xt_lo[:, kt, :], ps[:, i * SEQ:(i + 1) * SEQ], gain(g0 + kt),
                                                           xt_hi[:, kt, :].bitcast(F32), ALU.mult, ALU.subtract)
                        ins.then_inc(bank_free[4 + r % 4], 1)
                    vec.wait_ge(squared, layer * 16 + 8 * seen + 8)
                    link(vec.tensor_reduce(ms[:, 0:NT], ssq[:, :, :], AX.X, ALU.add))
                    scaled(NT, D_MODEL, ms[:, 0:NT])

                def evac(c):
                    if c == 0:
                        need(rstd_made, len(POW), POW["norm1"] + 1)
                    col, cols = (EARLY + LATE)[c]
                    complete(4 * c + 3 if c < len(EARLY) else U_LATE + 4 * (c - len(EARLY)) + 3)
                    vec.tensor_scalar(projected(1, col, cols), bank[2 * (c % 2) + 1][:, 0:cols], rstd_x[:, 1:2], None, ALU.mult)\
                       .then_inc(acc_out_vec[c % 2], 1)

                def angles_made(_):
                    inv = k_sb[:, K_INV:K_INV + 32]
                    for t in range(NT):
                        ang, turns = sin_sb[:, t, 0, :], cos_sb[:, t, 0, :]
                        link(vec.tensor_scalar(ang, inv, pos_f[:, t:t + 1], None, ALU.mult))
                        link(vec.tensor_scalar(turns, ang, 1.0 / (2 * np.pi), ROUNDER, ALU.mult, ALU.add))
                        link(vec.tensor_scalar(turns, turns, ROUNDER, None, ALU.subtract))
                        for part in TWO_PI:
                            link(vec.scalar_tensor_tensor(ang, turns, -part, ang, ALU.mult, ALU.add))
                        link(vec.tensor_scalar(ang, ang, 3.1415925, -3.1415925, ALU.min, ALU.max))
                        link(vec.scalar_tensor_tensor(turns, ang, -1.0, ang, ALU.mult, ALU.min))
                        vec.tensor_scalar(turns, turns, float(np.pi / 2), None, ALU.add).then_inc(angles, 1)

                def qa_rms(_):
                    need(m_squared, 4, 4)
                    vec.tensor_scalar(ms[:, 0:2], m_ss[:, 0:2], 1.0 / MLA_Q_RANK, EPS, ALU.mult, ALU.add)
                    vec.tensor_scalar(ms[:, 2:4], m_ss[:, 2:4], 1.0 / MLA_KV_RANK, EPS, ALU.mult, ALU.add)\
                       .then_inc(ms_made, 1)

                def qa_scale(_):
                    need(rstd_made, len(POW), POW["mla"] + 1)
                    need(acc_out_act[1], R_OUT, 1)
                    need(acc_out_vec[1], R_OUT, 1)
                    for t in range(NT):
                        for i, (col, n) in enumerate(((C_QA, MLA_Q_RANK), (C_KVA, MLA_KV_RANK))):
                            ins = vec.tensor_scalar(p2c(t, col, n), p2c(t, col, n), rstd[:, 2 * i + t:2 * i + t + 1], None,
                                                    ALU.mult)
                    ins.then_inc(qa_scaled, 1)

                def qa_turn(b):
                    ps = bank_in(("qa_turn", b), 4 + b)
                    need(qa_hi_made, 6, 2 * b + 2)
                    for i in range(2):
                        k = 2 * b + i
                        ins = vec.scalar_tensor_tensor(qa_lo[:, k, :], ps[:, i * SEQ:(i + 1) * SEQ], gain(G_QA + k),
                                                       qa_hi[:, k, :].bitcast(F32), ALU.mult, ALU.subtract)
                    ins.then_inc(bank_free[4 + b], 1)

                def mla_q(h):
                    need(acc_out_act[0], R_OUT, R_MLA + h + 1)
                    vec.tensor_copy(qr[:, :, h, :], bank[h % 2][:, SEQ:SEQ + NT * 64].rearrange("p (t d) -> p t d", t=NT))\
                       .then_inc(acc_out_vec[0], 1)

                def mla_kv(h):
                    need(acc_out_act[1], R_OUT, R_MLA + h + 1)
                    vec.tensor_copy(mv[:, :, h, :], bank[2 + h % 2][:, SEQ:2 * SEQ].rearrange("p (t d) -> p t d", t=NT))\
                       .then_inc(acc_out_vec[1], 1)

                def gla_turn(_):
                    ps = bank_in(("gla_turn", 0), 5)
                    vec.tensor_copy(gkt[:, :, :].rearrange("p a b -> p (a b)"), ps[:, :]).then_inc(bank_free[5], 1)

                def gla_logits(_):
                    ps = bank_in(("gla_logits", 0), 7)
                    for g in range(2):
                        ins = vec.tensor_scalar(gate_z[:, g, :], ps[:, g * SEQ:(g + 1) * SEQ], gain(G_BIAS + g), None, ALU.add)
                    ins.then_inc(bank_free[7], 1)
                    copied(("gla_logits", 0), 7)
                    vec.scalar_tensor_tensor(gate_e[:, :, :], gate_z[:, :, :], -1.0, gate_z[:, :, :], ALU.mult, ALU.min)\
                       .then_inc(gate_neg, 1)
                    link(vec.memset(ones[:, :], 1.0))

                def gla_decay(_):
                    need(gate_ln, 1, 1)
                    link(vec.scalar_tensor_tensor(gate_z[:, :, :], gate_z[:, :, :], 0.0, gate_e[:, :, :], ALU.min,
                                                  ALU.subtract))
                    for g in range(2):
                        ins = vec.tensor_tensor_scan(logs[:, g, :], ones[:, :], gate_z[:, g, :], 0.0, ALU.mult, ALU.add)
                    link(ins)
                    link(vec.memset(att[:, :, :, :, :].rearrange("p a b c d -> p (a b c d)"), 0.0))

                def level_prep(i):
                    size = SEQ // 2 if i == 0 else LEVELS[i - 1]
                    b = logs[:, :, :].rearrange("p g (n w) -> p g n w", w=2 * size)
                    o = decay_of(i).rearrange("p g (n w) -> p g n w", w=2 * size)
                    if i > 1:
                        need(level_made, N_LEVELS - 1, i - 1)
                    nb = SEQ // (2 * size)
                    mid = b[:, :, :, size - 1:size].to_broadcast([P, 2, nb, 2 * size])
                    link(vec.tensor_tensor(o, b, mid, ALU.subtract))
                    vec.scalar_tensor_tensor(decay_of(i), decay_of(i), -1.0, decay_of(i), ALU.mult, ALU.min)\
                       .then_inc(span_made, 1)

                def level_mm(i):
                    for par in range(2):
                        ps = masked_bank_in(("level_mm", i), 6 + par)
                        if i == 0:
                            ins = vec.tensor_copy(cross[:, par, :, :].rearrange("p g n -> p (g n)"), ps[:, 0:2 * P])
                        else:
                            mask = lev_sb[:, i - 1:i, :].to_broadcast([P, 4, P])
                            ins = vec.copy_predicated(att[:, par, :, :, :].rearrange("p t g n -> p (t g) n"), mask,
                                                      ps[:, :].rearrange("p (a n) -> p a n", a=4))
                        ins.then_inc(bank_free[6 + par], 1)

                def gla_out(_):
                    bank_in(("gla_out", 0), 7)
                    for t in range(NT):
                        ps = bank_in(("gla_out", 0), 6 + t)
                        ins = vec.tensor_copy(p2c(t, C_GV, NCH), ps[:, :])
                        ins.then_inc(bank_free[6 + t], 1)
                    copied(("gla_out", 0), 7)

                def gla_rms(_):
                    o = p2[:, :, C_GV - C_GQ:C_GV - C_GQ + NCH]
                    link(vec.tensor_tensor(squares[:, :, :, :].rearrange("p t h d -> p t (h d)"), o, o, ALU.mult))
                    link(vec.tensor_reduce(ms[:, 0:8], squares[:, :, :, :].rearrange("p t h d -> p (t h) d"), AX.X, ALU.add))
                    scaled(8, GLA_DV, ms[:, 0:8])

                def gla_gated(_):
                    need(rstd_made, len(POW), POW["gla"] + 1)
                    need(gate_silu, 2, 2)
                    need(rows_in, 32, 32)
                    for t in range(NT):
                        o = p2c(t, C_GV, NCH).rearrange("p (h d) -> p h d", h=4)
                        r = rstd[:, 4 * t:4 * t + 4].rearrange("p (h o) -> p h o", o=1).to_broadcast([P, 4, P])
                        w = row_sb[:, W_GLA:W_GLA + P].rearrange("p (o d) -> p o d", o=1).to_broadcast([P, 4, P])
                        link(vec.tensor_tensor(o, o, r, ALU.mult))
                        link(vec.tensor_tensor(o, o, w, ALU.mult))
                        ins = vec.tensor_tensor(p2c(t, C_GV, NCH), p2c(t, C_GV, NCH), p2c(t, C_GO, NCH), ALU.mult)
                    ins.then_inc(gla_mixed, 1)

                def rope(_):
                    need(acc_out_vec[0], R_OUT, R_LATE)
                    vec.tensor_copy(qr[:, :, 6, :], p2[:, :, C_KR - C_GQ:C_KR - C_GQ + 64]).then_inc(kr_in, 1)
                    need(rope_mul, 1, 1)
                    vec.tensor_tensor(qr[:, :, 0:7, 0:32], turn1[:, :, :, :], turn2[:, :, :, :], ALU.subtract)
                    link(vec.tensor_tensor(qr[:, :, 0:7, 32:64], turn3[:, :, :, :], turn4[:, :, :, :], ALU.add))
                    vec.tensor_copy(qr[:, :, 7, :], qr[:, :, 6, :]).then_inc(roped, 1)

                def rope_turn(_):
                    ps = bank_in(("rope_turn", 0), 5)
                    vec.tensor_copy(qrt[:, 2:4, :].rearrange("p a b -> p (a b)"), ps[:, :])\
                       .then_inc(bank_free[5], 1)

                def lambdas(_):
                    need(rows_in, 32, 32)
                    link(vec.tensor_tensor(lam_prod[:, :], row_sb[:, W_LAM:W_LAM + P], row_sb[:, W_LAM + P:W_LAM + 2 * P],
                                           ALU.mult))
                    vec.tensor_reduce(lam2[:, :], lam_prod[:, :].rearrange("p (a b) -> p a b", a=2), AX.X, ALU.add)\
                       .then_inc(lam_dot, 1)

                def diff_turn(i):
                    ps = bank_in(("diff_turn", i), 5)
                    vec.tensor_copy((dkt if i % 2 else dqt)[:, 2, :], ps[:, 0:SEQ]).then_inc(bank_free[5], 1)

                def head_scores(j):
                    mla = j < MLA_HEADS
                    for branch in range(1 if mla else 2):
                        ps = masked_bank_in(("head_scores", j), 6 + branch)
                        for t in range(NT):
                            k, n = 4 * (j % 2) + 2 * branch + t, (t + 1) * P
                            ins = vec.tensor_tensor_reduce(e_of(j)[branch][:, t * P:t * P + n], ps[:, t * P:t * P + n],
                                                           caus_sb[:, 2 * P - n:2 * P], 1.0, NEG * 4, ALU.add, ALU.max,
                                                           mx[:, k:k + 1])
                        ins.then_inc(bank_free[6 + branch], 1)
                    for b in (6,) if mla else (6, 7):
                        copied(("head_scores", j), b)
                    scale = (MLA_NOPE + MLA_ROPE) ** -0.5 if mla else DIFF_HD ** -0.5
                    k = slice(4 * (j % 2), 4 * (j % 2) + (2 if mla else 4))
                    vec.tensor_scalar(nmx[:, k], mx[:, k], -scale, None, ALU.mult).then_inc(masked, 1)

                def head_norm(j):
                    mla = j < MLA_HEADS
                    k = slice(4 * (j % 2), 4 * (j % 2) + (2 if mla else 4))
                    need(exped, HEADS, j + 1)
                    if mla:
                        vec.reciprocal(held[:, 2 * j:2 * j + 2], esum[:, k]).then_inc(sums_inverted, 1)
                        return
                    if j == MLA_HEADS:
                        need(lam_exp, 1, 1)
                        link(vec.tensor_tensor(lam[:, :], lam2e[:, 0:1], lam2e[:, 1:2], ALU.subtract))
                        l0 = k_sb[:, bass.ds(K_LAM + 2 * layer, 1)]
                        link(vec.tensor_tensor(lam[:, :], lam[:, :], l0, ALU.add))
                    link(vec.reciprocal(rsum[:, :], esum[:, k]))
                    link(vec.tensor_scalar(rsum[:, 2:4], rsum[:, 2:4], lam[:, 0:1], None, ALU.mult))
                    for t in range(NT):
                        b = e_of(j)[1][:, t * P:t * P + (t + 1) * P]
                        ins = vec.tensor_scalar(b, b, rsum[:, 2 + t:3 + t], None, ALU.mult)
                    link(ins)
                    for t in range(NT):
                        a, b = (x[:, t * P:t * P + (t + 1) * P] for x in e_of(j))
                        ins = vec.scalar_tensor_tensor(a, a, rsum[:, t:t + 1], b, ALU.mult, ALU.subtract)
                    ins.then_inc(probs_made, 1)

                def head_out(j):
                    ps = bank_in(("head_out", j), 5)
                    if j < MLA_HEADS:
                        need(sums_inverted, MLA_HEADS, j + 1)
                        for t in range(NT):
                            ins = vec.tensor_scalar(mv[:, t, j, :], ps[:, t * P:(t + 1) * P], held[:, 2 * j + t:2 * j + t + 1],
                                                    None, ALU.mult)
                        ins.then_inc(bank_free[5], 1)
                        return
                    col = C_DV + (j - MLA_HEADS) * P
                    ins = vec.tensor_copy(pd[:, :, col:col + P], ps[:, 0:2 * P].rearrange("p (t d) -> p t d", t=NT))
                    ins.then_inc(bank_free[5], 1)

                def diff_rms(g):
                    copied(("head_out", MLA_HEADS + 3 * g + 2), 5)
                    o = pd[:, :, C_DV + g * G3:C_DV + (g + 1) * G3].rearrange("p t (h d) -> p t h d", h=3)
                    link(vec.tensor_tensor(squares[:, :, 0:3, :], o, o, ALU.mult))
                    link(vec.tensor_reduce(ms[:, 0:6].rearrange("p (t h) -> p t h", t=NT), squares[:, :, 0:3, :], AX.X, ALU.add))
                    scaled(6, DIFF_VD, ms[:, 0:6])
                    if g == 0:
                        w = row_sb[:, W_SUB:W_SUB + P]
                        link(vec.tensor_scalar(w, w, k_sb[:, bass.ds(K_LAM + 2 * layer + 1, 1)], None, ALU.mult))

                def diff_scale(g):
                    need(rstd_made, len(POW), POW[f"diff{g}"] + 1)
                    for t in range(NT):
                        o = pd[:, t, C_DV + g * G3:C_DV + (g + 1) * G3].rearrange("p (h d) -> p h d", h=3)
                        r = rstd[:, 3 * t:3 * t + 3].rearrange("p (h o) -> p h o", o=1).to_broadcast([P, 3, P])
                        w = row_sb[:, W_SUB:W_SUB + P].rearrange("p (o d) -> p o d", o=1).to_broadcast([P, 3, P])
                        link(vec.tensor_tensor(o, o, r, ALU.mult))
                        ins = vec.tensor_tensor(o, o, w, ALU.mult)
                    ins.then_inc(diff_mixed, 1)

                def mix_turn(kt0):
                    b = 4 + kt0 // 2 % 2
                    ps = bank_in(("mix_turn", kt0), b)
                    order = [6, 8, 10, 12, 14, 0, 2, 4].index(kt0)
                    need(xt_hi_made, 48, 16 + 2 * order + 2)
                    vec.tensor_tensor(xt_lo[:, kt0:kt0 + 2, :].rearrange("p a b -> p (a b)"), ps[:, :],
                                      xt_hi[:, kt0:kt0 + 2, :].rearrange("p a b -> p (a b)").bitcast(F32), ALU.subtract)\
                       .then_inc(bank_free[b], 1)

                steps = {"evac": evac, "angles": angles_made, "qa_rms": qa_rms, "qa_scale": qa_scale, "qa_turn": qa_turn, "mla_q": mla_q,
                         "mla_kv": mla_kv, "gla_turn": gla_turn, "gla_logits": gla_logits, "gla_decay": gla_decay,
                         "level_prep": level_prep, "level_mm": level_mm, "gla_out": gla_out, "gla_rms": gla_rms,
                         "gla_gated": gla_gated, "rope": rope, "rope_turn": rope_turn, "diff_turn": diff_turn,
                         "head_norm": head_norm, "lambdas": lambdas, "head_scores": head_scores, "head_out": head_out, "diff_rms": diff_rms,
                         "diff_scale": diff_scale, "mix_turn": mix_turn}

                def add_to_resid(c, parity, n):
                    complete(n)
                    for t in range(NT):
                        part = resid[:, t, c * NCH:(c + 1) * NCH]
                        vec.tensor_tensor(part, bank[2 * parity + t][:, :], part, ALU.add)\
                           .then_inc(x_added, 1)

                norm("norm1", 0)
                for n in range(U_FF):
                    if n < U_FF - 1:
                        rest_of_unit(layer * QUADS + (n + LEAD) // 4, n + LEAD)
                    for name, arg in HOOKS.get(n, []):
                        if name in steps:
                            steps[name](arg)
                    if n >= U_OUT and (n - U_OUT) % 8 >= 6:
                        pair, c = (n - U_OUT) // 8, (n - U_OUT) % 2
                        add_to_resid(2 * pair + c, c, n)
                norm("norm2", 1)

                def ff_turn(f):
                    for b in (4, 5):
                        vec.wait_ge(bank_full[b], layer * USES[b] + ROUND[("ff_turn", 0)][b] + f + 1)
                        vec.wait_ge(ft_hi_made, layer * (2 * FF_CHUNKS) + 2 * f + b - 3)
                        at = bass.ds(f * 4 + 2 * (b - 4), 2)
                        vec.tensor_tensor(f_lo[:, at, :].rearrange("p a b -> p (a b)"), bank[b][:, :],
                                          f_hi[:, at, :].rearrange("p a b -> p (a b)").bitcast(F32), ALU.subtract)\
                           .then_inc(bank_free[b], 1)

                def ff_chunk(f, first):
                    for i in range(8):
                        rest_of_unit(layer * QUADS + (U_FF + i + LEAD) // 4 + 2 * f, U_FF + i + LEAD)
                        if i == 1 and not first:
                            ff_turn(f - 1)
                        if i == 7:
                            if first:
                                need(rstd_made, len(POW), POW["norm2"] + 1)
                            vec.wait_ge(used[3], layer * QUADS + (U_FF + 7) // 4 + 2 + 2 * f)
                            for t in range(NT):
                                vec.wait_ge(silu_made, layer * (FF_CHUNKS * NT) + f * NT + t + 1)
                                vec.scalar_tensor_tensor(act_sb[:, t, :], bank[2 + t][:, :], rstd_x[:, t:t + 1],
                                                         act_sb[:, t, :], ALU.mult, ALU.mult)\
                                   .then_inc(act_made, 1)

                ff_chunk(0, True)
                with vec.Fori(1, FF_CHUNKS) as f:
                    ff_chunk(f, False)
                for n in range(U_DOWN, UNITS):
                    i = n - U_DOWN
                    if n < UNITS - 1:
                        rest_of_unit(layer * QUADS + (n + LEAD) // 4, n + LEAD)
                    if i == 1:
                        ff_turn(FF_CHUNKS - 1)
                    if i % len(DOWN_KT) == len(DOWN_KT) - 1:
                        c = i // len(DOWN_KT)
                        add_to_resid(c, c % 2, n)
                assert count[0] == VEC_LINKS, count[0]

            vec.wait_ge(squared, 16 * DEPTH + 8)
            vec.tensor_reduce(ms[:, 0:NT], ssq[:, :, :], AX.X, ALU.add).then_inc(vec_chain, 1)
            vec.wait_ge(vec_chain, DEPTH * VEC_LINKS + 1)
            vec.tensor_scalar(ms[:, 0:NT], ms[:, 0:NT], 1.0 / D_MODEL, EPS, ALU.mult, ALU.add).then_inc(ms_made, 1)
            vec.wait_ge(rstd_made, DEPTH * len(POW) + 1)
            vec.wait_ge(setup_in, 80)
            vec.scalar_tensor_tensor(xn[:, 0, :], resid[:, 0, :], rstd_x[:, 0:1], last_gain[:, :], ALU.mult, ALU.mult)\
               .then_inc(out_made, 1)
            vec.wait_ge(xn_act, 1)
            vec.tensor_tensor(xn[:, 1, :], xn[:, 1, :], last_gain[:, :], ALU.mult).then_inc(out_made, 1)


_OUTS = [((1, SEQ, D_MODEL), "float32")]


def build(nc, shapes):
    aps = {name: nc.dram_tensor(f"in_{name}", shape, dt, kind="ExternalInput").ap() for name, (shape, dt) in shapes.items()}
    out = nc.dram_tensor("out_0_dram", (SEQ, D_MODEL), F32, kind="ExternalOutput").ap()
    program(nc, out=out, **aps)


def kernel(**inputs):
    import concourse.bacc as bacc
    from concourse.bass_utils import run_bass_kernel_spmd

    a = {k: np.ascontiguousarray(v) for k, v in inputs.items()}

    def columns(v, n):
        return v.reshape(DEPTH, n, P).transpose(2, 0, 1)

    consts = np.zeros((P, K_END), np.float32)
    consts[:, K_ID:K_ID + P] = np.eye(P)
    consts[:, K_INV:K_INV + 32] = 1.0 / ROPE_THETA ** (np.arange(0, MLA_ROPE, 2, dtype=np.float32) / MLA_ROPE)
    for layer in range(DEPTH):
        first = 0.8 - 0.6 * np.exp(-0.3 * layer)
        consts[:, K_LAM + 2 * layer:K_LAM + 2 * layer + 2] = first, 1.0 - first
    key, query = np.arange(P)[:, None], np.arange(P)[None, :]
    levels = np.zeros((P, len(LEVELS), P), np.float32)
    for i, size in enumerate(LEVELS):
        if size:
            levels[:, i] = (key // (2 * size) == query // (2 * size)) & (key % (2 * size) < size) & (query % (2 * size) >= size)
        else:
            levels[:, i] = key == query
    causal = np.zeros((P, 2 * P), np.float32)
    causal[:, P:] = np.where(query <= key, 0.0, NEG)

    arrays = {
        "x": a["x"].reshape(SEQ, D_MODEL),
        "positions": a["positions"].reshape(NT, P).T,
        "w_in": a["w_in"], "w_q_b": a["mla_w_q_b"], "w_kv_b": a["mla_w_kv_b"], "w_out": a["w_out"],
        "w_gate": a["w_gate"], "w_up": a["w_up"], "w_down": a["w_down"], "gate_w": a["gla_gate_w"],
        "gains": np.concatenate([columns(a["attn_norm"], KT), columns(a["ffn_norm"], KT), columns(a["mla_q_norm"], 4),
                                 columns(a["mla_kv_norm"], 2), columns(a["gla_gate_b"], 2)], axis=2),
        "rows": np.concatenate([a["diff_subln"], a["gla_norm"], a["diff_lambda_q1"], a["diff_lambda_q2"],
                                a["diff_lambda_k1"], a["diff_lambda_k2"]], axis=1).reshape(DEPTH, 1, W_END),
        "final_norm": a["final_norm"].reshape(1, D_MODEL),
        "consts": consts, "levels": levels, "causal": causal,
    }
    arrays = {k: np.ascontiguousarray(v) for k, v in arrays.items()}
    nc = bacc.Bacc("TRN2", target_bir_lowering=False, num_devices=1)
    build(nc, {k: (v.shape, mybir.dt.from_np(v.dtype)) for k, v in arrays.items()})
    r = run_bass_kernel_spmd(nc, [{f"in_{k}": v for k, v in arrays.items()}], core_ids=[0])
    return r.results[0]["out_0_dram"].reshape(1, SEQ, D_MODEL)
```

```python
from contextlib import ExitStack

import numpy as np

import concourse.bass as bass
from concourse import mybir

F32 = mybir.dt.float32
F32R = mybir.dt.float32r
U8 = mybir.dt.uint8
I32 = mybir.dt.int32
ALU = mybir.AluOpType
ACT = mybir.ActivationFunctionType
AX = mybir.AxisListType

P = 128
D_MODEL, SEQ, DEPTH = 2048, 256, 2
DIFF_HEADS, DIFF_HD, DIFF_VD = 6, 64, 128
GLA_HEADS, GLA_DK, GLA_DV, GLA_RANK, GLA_TAU = 4, 64, 128, 16, 16.0
MLA_HEADS, MLA_Q_RANK, MLA_KV_RANK, MLA_NOPE, MLA_ROPE, MLA_VD = 6, 512, 256, 128, 64, 128
ROPE_THETA, D_FF, EPS = 10000.0, 5632, 1e-6

NT = SEQ // P
KT = D_MODEL // P
FT = D_FF // P
NCH = 512
FF_CHUNKS = D_FF // NCH
LEAD = 3

C_DV = 2 * DIFF_HEADS * 2 * DIFF_HD
C_GQ = C_DV + DIFF_HEADS * DIFF_VD
C_GK = C_GQ + GLA_HEADS * GLA_DK
C_GV = C_GK + GLA_HEADS * GLA_DK
C_GR = C_GV + GLA_HEADS * GLA_DV
C_GO = C_GR + GLA_RANK
C_QA = C_GO + GLA_HEADS * GLA_DV
C_KVA = C_QA + MLA_Q_RANK
C_KR = C_KVA + MLA_KV_RANK
IN_COLS = C_KR + MLA_ROPE
DIFF_QK = DIFF_HEADS * 2 * DIFF_HD
G3 = 3 * 2 * DIFF_HD

EARLY = [(C_QA, MLA_Q_RANK), (C_KVA, IN_COLS - C_KVA), (C_GQ, NCH), (C_GV, NCH), (C_GR, 272), (C_GR + 272, 256)]
LATE = [(part + g * G3, G3) for g in range(2) for part in (0, DIFF_QK)] + [(2 * DIFF_QK + g * G3, G3) for g in range(2)]

EARLY_UNITS = [(c, range(k, k + width)) for c, (_, cols) in enumerate(EARLY) for width in [8 if cols <= 256 else 4]
               for k in range(0, KT, width)]
U_MLA = len(EARLY_UNITS)
MLA_PAIRS = MLA_HEADS // 2
U_LATE = U_MLA + 2 * MLA_PAIRS
U_OUT = U_LATE + 4 * len(LATE)
U_FF = U_OUT + 4 * (D_MODEL // NCH)
U_DOWN = U_FF + 8 * FF_CHUNKS
DOWN_KT = [range(4 * u, 4 * u + 4) for u in range(8)] + [range(32 + 3 * u, 35 + 3 * u) for u in range(4)]
UNITS = U_DOWN + len(DOWN_KT) * (D_MODEL // NCH)
QUADS = UNITS // 4
R_MLA = len(EARLY) // 2
R_LATE = R_MLA + MLA_PAIRS
R_OUT = R_LATE + len(LATE) // 2
R_FF = R_OUT + 2
R_DOWN = R_FF + FF_CHUNKS

OUT_KT = [[6, 7, 8, 9], [10, 11, 12, 13], [14, 15, 0, 1], [2, 3, 4, 5]]

LEVELS = [64, 32, 16, 8, 4, 2, 1, 0]
N_LEVELS = 1 + len(LEVELS)
HEADS = MLA_HEADS + DIFF_HEADS

SCORES_AT = [U_LATE + n for n in (4, 5, 6, 7, 8, 9, 11, 13, 15, 18, 20, 22)]
TURN_AT = [n + 2 for n in SCORES_AT[:MLA_HEADS]] + [n + 3 for n in SCORES_AT[MLA_HEADS:]]
OUT_AT = [n + 3 for n in SCORES_AT[:MLA_HEADS]] + [U_LATE + n for n in (20, 21, 22, 24, 25, 26)]
PT_OF = [0] * MLA_HEADS + [j % 3 for j in range(DIFF_HEADS)]

MIX_AT = [(U_LATE + n, kt) for n, kt in ((14, 6), (17, 8), (19, 10), (24, 12), (25, 14), (26, 0), (28, 2), (28, 4))]
MIX_EARLY = [6, 8, 10]


def last_unit(c):
    if c < len(EARLY):
        return max(n for n, (chunk, _) in enumerate(EARLY_UNITS) if chunk == c)
    return U_LATE + 4 * (c - len(EARLY)) + 3


def mix_bank(kt):
    k = [first for _, first in MIX_AT].index(kt)
    return (5 if k % 2 == 0 else 4) if k < len(MIX_EARLY) else 6 + k % 2


def hooks():
    at = {}

    def put(n, *steps):
        at.setdefault(n, []).extend(steps)

    for c in range(len(EARLY)):
        put(last_unit(c), ("evac", c))
    for h in range(MLA_PAIRS):
        put(U_MLA + 2 * h, ("mla_q", h))
        put(U_MLA + 2 * h + 1, ("mla_kv", h))
    put(7, ("qa_rms", 0))
    put(8, ("qa_scale", 0))
    for b in range(3):
        put(10 + b, ("qa_turn", b))
    put(13, ("angles", 0))
    put(20, ("gla_turn", 0))
    put(21, ("gla_silu", 0), ("gla_logits", 0))
    put(22, ("gla_decay", 0))
    put(24, ("att_cleared", 0))
    put(25, ("level_mm", N_LEVELS - 1))
    for i, n in enumerate((23, 24, 25, 27, 28, 29, 30, 31)):
        put(n, ("level_prep", i))
        put(n + 1, ("level_exp", i))
        put(n + 3, ("level_mm", i))
    for c in range(len(LATE)):
        put(last_unit(len(EARLY) + c), ("evac", len(EARLY) + c))
    put(U_LATE - 1, ("rope", 0))
    put(U_LATE + 3, ("rope_turn", 0))
    put(U_LATE + 9, ("gla_out", 0))
    put(U_LATE + 10, ("gla_rms", 0), ("lambdas", 0))
    put(U_LATE + 11, ("gla_gated", 0))
    for n, kt in MIX_AT:
        put(n, ("mix_turn", kt))
    for i, n in enumerate((8, 10, 16, 17)):
        put(U_LATE + n, ("diff_turn", i))
    for j in range(HEADS):
        put(OUT_AT[j], ("head_out", j))
        put(TURN_AT[j], ("head_turn", j))
        put(SCORES_AT[j] + 2, ("head_norm", j))
        put(SCORES_AT[j] + 1, ("head_exp", j))
        put(SCORES_AT[j], ("head_scores", j))
    put(U_LATE + 22, ("diff_rms", 0))
    put(U_LATE + 24, ("diff_scale", 0))
    put(U_LATE + 26, ("diff_rms", 1))
    put(U_LATE + 27, ("diff_scale", 1))
    order = ["", "head_out", "head_turn", "head_norm", "head_exp", "head_scores", "diff_rms", "diff_scale"]
    for steps in at.values():
        steps.sort(key=lambda step: order.index(step[0]) if step[0] in order else 0)
    return at


HOOKS = hooks()
BANKS_OF = {"qa_turn": lambda b: [4 + b], "gla_turn": lambda _: [4, 5, 6], "gla_logits": lambda _: [7],
            "level_mm": lambda _: [6, 7], "rope_turn": lambda _: [4, 5],
            "head_scores": lambda j: [6] if j < MLA_HEADS else [6, 7], "head_turn": lambda _: [4],
            "head_out": lambda _: [5], "gla_out": lambda _: [6, 7], "diff_turn": lambda _: [6, 7],
            "mix_turn": lambda kt: [mix_bank(kt)]}


def chunk_round(c):
    return c % 2, c // 2 if c < len(EARLY) else R_LATE + (c - len(EARLY)) // 2


def bank_rounds():
    used = {b: 0 for b in (4, 5, 6, 7)}
    of = {}

    def take(key, banks):
        of[key] = {}
        for b in banks:
            of[key][b] = used[b]
            used[b] += 1

    for r in range(KT // 2):
        take(("norm1", r), [4 + r % 4])
    for n in sorted(HOOKS):
        for step in HOOKS[n]:
            if step[0] in BANKS_OF:
                take(step, BANKS_OF[step[0]](step[1]))
    for r in range(KT // 2):
        take(("norm2", r), [4 + r % 4])
    take(("ff_turn", 0), [4, 5])
    for b in (4, 5):
        used[b] += FF_CHUNKS - 1
    return of, used


ROUND, USES = bank_rounds()
POW = {"norm1": 0, "mla": 1, "gla": 2, "diff0": 3, "diff1": 4, "norm2": 5}

ARENA = 2 * FT * SEQ
A_PD = 0
A_P2 = A_PD + NT * C_GQ
P2 = IN_COLS - C_GQ
A_QNT = A_P2 + NT * P2
A_KNT = A_QNT + MLA_HEADS * SEQ
A_MV = A_KNT + MLA_HEADS * SEQ
A_QRT = A_MV + NT * MLA_HEADS * MLA_VD
A_QR = A_QRT + 4 * SEQ
A_GQT = A_QR + NT * 8 * MLA_ROPE
A_GKT = A_GQT + 2 * SEQ
A_B = A_GKT + 2 * SEQ
A_QL = A_B + 2 * SEQ
A_KL = A_QL + 2 * 2 * SEQ
A_ATT = A_KL + 2 * 2 * SEQ
A_CROSS = A_ATT + 2 * NT * 2 * P
A_E1 = A_CROSS + 2 * 2 * P
A_E2 = A_E1 + 3 * P
A_PT = A_E2 + 3 * P
A_END = A_PT + 3 * P
assert A_END <= ARENA

K_ID, K_INV, K_LAM, K_END = 0, P, P + MLA_ROPE // 2, P + MLA_ROPE // 2 + 2 * DEPTH
G_ATTN, G_FFN, G_QA, G_KVA, G_BIAS, G_END = 0, KT, 2 * KT, 2 * KT + 4, 2 * KT + 6, 2 * KT + 8
W_SUB, W_GLA, W_LAM, W_END = 0, P, 2 * P, 2 * P + 4 * DIFF_HD
NEG = -1e30
ACT_LINKS, VEC_LINKS = 1, 71
TWO_PI = [int(2 * np.pi * 2 ** n) / 2 ** n - int(2 * np.pi * 2 ** (n - 7)) / 2 ** (n - 7) for n in (4, 11, 18, 25, 32)]
ROUNDER = 12582912.0


def program(nc, x, positions, w_in, w_q_b, w_kv_b, w_out, w_gate, w_up, w_down, gate_w, gains, rows,
            final_norm, consts, levels, causal, out):
    with ExitStack() as ctx:
        def sem(name):
            return ctx.enter_context(nc.semaphore(name))

        def sb(name, shape, dt):
            return ctx.enter_context(nc.sbuf_tensor(name, shape, dt))

        arena_at = nc.sbuf_base + (-nc.sbuf_base) % 64
        xt_at = arena_at + 4 * ARENA
        g_at = xt_at + 4 * 2 * KT * SEQ
        stage_at = g_at + 4 * NT * NCH
        sb("slab", [P, (stage_at - arena_at) // 4 + 4 * 4 * NCH], F32)

        def place(name, shape, dt, offset):
            return nc.alloc_sbuf_tensor_at(name, shape, dt, offset=offset)

        def arena(name, shape, dt, word):
            return place(name, shape, dt, arena_at + 4 * word)

        pd = arena("pd", [P, NT, C_GQ], F32, A_PD)
        p2 = arena("p2", [P, NT, P2], F32, A_P2)
        qa_hi = arena("qa_hi", [P, 6, SEQ], F32R, A_PD)
        qa_lo = arena("qa_lo", [P, 6, SEQ], F32R, A_PD + 6 * SEQ)
        turn1, turn2, turn3, turn4 = (arena(f"rope_product{i}", [P, NT, 7, 32], F32, A_PD + 448 * i) for i in range(4))
        qnt = arena("qnt", [P, MLA_HEADS, SEQ], F32, A_QNT)
        knt = arena("knt", [P, MLA_HEADS, SEQ], F32, A_KNT)
        mv = arena("mv", [P, NT, MLA_HEADS, MLA_VD], F32, A_MV)
        mix_hi = arena("mix_hi", [P, 6, SEQ], F32R, A_QNT)
        mix_lo = arena("mix_lo", [P, 6, SEQ], F32R, A_KNT)
        levels_in = arena("levels_in", [P, len(LEVELS), P], F32, A_QNT)
        qrt = arena("qrt", [P, 4, SEQ], F32, A_QRT)
        qr = arena("qr", [P, NT, 8, MLA_ROPE], F32, A_QR)
        gqt = arena("gqt", [P, 2, SEQ], F32, A_GQT)
        gkt = arena("gkt", [P, 2, SEQ], F32, A_GKT)
        dqt = arena("dqt", [P, 3, SEQ], F32, A_QR)
        dkt = arena("dkt", [P, 3, SEQ], F32, A_QR + 3 * SEQ)
        logs = arena("logs", [P, 2, SEQ], F32, A_B)
        ql = arena("ql", [P, 2, 2, SEQ], F32, A_QL)
        kl = arena("kl", [P, 2, 2, SEQ], F32, A_KL)
        grt = arena("grt", [GLA_RANK, SEQ], F32, A_QL)
        squares = arena("squares", [P, NT, 4, P], F32, A_QL)
        att = arena("att", [P, 2, NT, 2, P], F32, A_ATT)
        cross = arena("cross", [P, 2, 2, P], F32, A_CROSS)
        gate_z = arena("gate_z", [P, 2, SEQ], F32, A_ATT)
        gate_e = arena("gate_e", [P, 2, SEQ], F32, A_ATT + 2 * SEQ)
        lam_prod = arena("lam_prod", [P, 2 * DIFF_HD], F32, A_CROSS)
        ones = arena("ones", [P, SEQ], F32, A_CROSS)
        e = [arena(f"e{i}", [P, 3 * P], F32, at) for i, at in enumerate((A_E1, A_E2, A_ATT, A_ATT + 3 * P))]
        pt = [arena(f"pt{i}", [P, 3 * P], F32, at) for i, at in enumerate((A_PT, A_KL, A_KL + 3 * P))]
        xn = arena("xn", [P, NT, D_MODEL], F32, 0)
        f_hi = arena("f_hi", [P, FT, SEQ], F32R, 0)
        f_lo = arena("f_lo", [P, FT, SEQ], F32R, FT * SEQ)
        xt_hi = place("xt_hi", [P, KT, SEQ], F32R, xt_at)
        xt_lo = place("xt_lo", [P, KT, SEQ], F32R, xt_at + 4 * KT * SEQ)
        last_gain = place("last_gain", [P, D_MODEL], F32, xt_at)
        row_sb = place("row_sb", [P, W_END], F32, g_at)
        gw_sb = place("gw_sb", [GLA_RANK, GLA_HEADS * GLA_DK], F32, g_at + 4 * W_END)
        small_at = g_at + 4 * (W_END + GLA_HEADS * GLA_DK)
        m_ss = place("m_ss", [P, 4], F32, small_at)
        rsum = place("rsum", [P, 4], F32, small_at + 32)
        held = place("held", [P, 2 * MLA_HEADS], F32, small_at + 64)
        lam2 = place("lam2", [P, 2], F32, small_at + 128)
        lam2e = place("lam2e", [P, 2], F32, small_at + 160)
        lam = place("lam", [P, 1], F32, small_at + 192)
        junk = place("junk", [P, NCH], F32, g_at)
        act_sb = place("act_sb", [P, NT, NCH], F32, g_at)

        resid = sb("resid", [P, NT, D_MODEL], F32)
        stage = [place(f"stage{i}", [P, 4 * NCH], F32, stage_at + 16 * NCH * i) for i in range(4)]
        w_lo = [place(f"w_lo{i}", [P, 4 * NCH], F32R, stage_at + 16 * NCH * i) for i in range(4)]
        w_hi = [sb(f"w_hi{i}", [P, 4 * NCH], F32R) for i in range(4)]
        k_sb = sb("k_sb", [P, K_END], F32)
        gain_sb = sb("gain_sb", [P, DEPTH, G_END], F32)
        lev_sb = sb("lev_sb", [P, len(LEVELS), P], U8)
        caus_sb = sb("caus_sb", [P, 2 * P], F32)
        cos_sb = sb("cos_sb", [P, NT, 1, 32], F32)
        sin_sb = sb("sin_sb", [P, NT, 1, 32], F32)
        pos_i = sb("pos_i", [P, NT], I32)
        pos_f = sb("pos_f", [P, NT], F32)
        ssq = sb("ssq", [P, NT, 4], F32)
        ms = sb("ms", [P, 8], F32)
        rstd = sb("rstd", [P, 8], F32)
        rstd_x = sb("rstd_x", [P, NT], F32)
        warm = sb("warm", [P, 1], F32)
        halves = sb("halves", [P, 8], F32)
        mx = sb("mx", [P, 8], F32)
        nmx = sb("nmx", [P, 8], F32)
        esum = sb("esum", [P, 8], F32)

        ident = k_sb[:, K_ID:K_ID + P]
        bank = [ctx.enter_context(nc.psum_tensor(f"bank{i}", [P, NCH], F32)) for i in range(8)]

        full = [sem(f"full{s}") for s in range(4)]
        hi_made = [sem(f"hi_made{s}") for s in range(4)]
        lo_made = [sem(f"lo_made{s}") for s in range(4)]
        used = [sem(f"used{s}") for s in range(4)]
        acc_out_act = [sem(f"acc_out_act{p}") for p in range(2)]
        acc_out_vec = [sem(f"acc_out_vec{p}") for p in range(2)]
        bank_full = {b: sem(f"bank_full{b}") for b in USES}
        bank_free = {b: sem(f"bank_free{b}") for b in USES}
        setup_in, rows_in, halves_made = sem("setup_in"), sem("rows_in"), sem("halves_made")
        consts_in, masks_in, masks_made = sem("consts_in"), sem("masks_in"), sem("masks_made")
        x_in = [sem(f"x_in{c}") for c in range(4)]
        squared = sem("squared")
        x_added = sem("x_added")
        ms_made, rstd_made = sem("ms_made"), sem("rstd_made")
        xn_act, xn_vec, gain_taken = sem("xn_act"), sem("xn_vec"), sem("gain_taken")
        xt_hi_made = sem("xt_hi_made")
        m_squared, qa_scaled = sem("m_squared"), sem("qa_scaled")
        qa_hi_made = sem("qa_hi_made")
        roped, rope_mul = sem("roped"), sem("rope_mul")
        kr_in = sem("kr_in")
        gate_neg, gate_ln, gate_silu = sem("gate_neg"), sem("gate_ln"), sem("gate_silu")
        span_made, decay_made, level_made = sem("span_made"), sem("decay_made"), sem("level_made")
        gla_mixed, diff_mixed = sem("gla_mixed"), sem("diff_mixed")
        masked, exped, probs_made = sem("masked"), sem("exped"), sem("probs_made")
        sums_inverted = sem("sums_inverted")
        lam_dot, lam_exp = sem("lam_dot"), sem("lam_exp")
        silu_made, act_made, ft_hi_made = sem("silu_made"), sem("act_made"), sem("ft_hi_made")
        positions_made, angles, waves = sem("positions_made"), sem("angles"), sem("waves")
        act_chain, vec_chain = sem("act_chain"), sem("vec_chain")
        stored = sem("stored")

        def e_of(j):
            return (e[j % 2],) if j < MLA_HEADS else e[2 * (j % 2):2 * (j % 2) + 2]

        def mixed(kt):
            if kt - kt % 2 in MIX_EARLY:
                return mix_hi, mix_lo, kt - MIX_EARLY[0]
            return xt_hi, xt_lo, kt

        def later_halves(x, size):
            return x.rearrange("p (n h w) -> p n h w", h=2, w=size)[:, :, 1, :]

        def decay_of(i):
            return p2[:, :, SEQ * (i % 2):SEQ * (i % 2) + SEQ]

        def p2c(t, col, n):
            return p2[:, t, col - C_GQ:col - C_GQ + n]

        def projected(t, col, n):
            return pd[:, t, col:col + n] if col < C_GQ else p2c(t, col, n)

        def unit_shape(n):
            n %= UNITS
            if n < U_MLA:
                c, kts = EARLY_UNITS[n]
                return len(kts), EARLY[c][1]
            if n < U_LATE:
                return (4, 2 * (MLA_NOPE + MLA_ROPE)) if (n - U_MLA) % 2 == 0 else (2, 2 * (MLA_NOPE + MLA_VD))
            if n < U_OUT:
                return 4, LATE[(n - U_LATE) // 4][1]
            if n < U_DOWN:
                return 4, NCH
            return len(DOWN_KT[(n - U_DOWN) % len(DOWN_KT)]), NCH

        block = ctx.enter_context(nc.Block())

        @block.sync
        def _(sp):
            sp.dma_start(k_sb[:, :], consts).then_inc(consts_in, 16)
            for c in range(4):
                part = slice(c * NCH, (c + 1) * NCH)
                sp.dma_start(resid[:, :, part], x[:, part].rearrange("(t p) d -> p t d", p=P)).then_inc(x_in[c], 16)
            sp.dma_start(gain_sb[:, :, :], gains).then_inc(setup_in, 16)
            sp.dma_start(pos_i[:, :], positions).then_inc(setup_in, 16)

            def load(quad, n, sources, second_first=False):
                s = n % 4
                kts, cols = unit_shape(n)
                view = stage[s][:, 0:kts * cols].rearrange("p (k n) -> p k n", k=kts)
                sp.wait_ge(used[s], quad + 1)
                parts = []
                for src in sources:
                    at, m = sum(n_rows for _, n_rows, _ in parts), src.shape[0] // P
                    parts.append((at, m, src))
                for at, m, src in reversed(parts) if second_first else parts:
                    sp.dma_start(view[:, at:at + m, :], src.rearrange("(k p) n -> p k n", p=P)).then_inc(full[s], 16)

            def halves_of(w, layer, kts, col, cols):
                kts = list(kts)
                cut = (len(kts) + 1) // 2
                return [w[layer, part[0] * P:(part[-1] + 1) * P, bass.ds(col, cols)] for part in (kts[:cut], kts[cut:])]

            with sp.Fori(0, DEPTH) as layer:
                def quad(n):
                    return layer * QUADS + n // 4

                for n, (c, kts) in enumerate(EARLY_UNITS):
                    load(quad(n), n, halves_of(w_in, layer, kts, *EARLY[c]))
                    if n == 7:
                        sp.wait_ge(squared, layer * 16 + 8)
                        sp.dma_start(row_sb[:, :], rows[layer].to_broadcast([P, W_END])).then_inc(rows_in, 16)
                        sp.dma_start(gw_sb[:, :], gate_w[layer]).then_inc(rows_in, 16)
                for h in range(MLA_PAIRS):
                    n = U_MLA + 2 * h
                    for k, (w, tiles) in enumerate(((w_q_b, 4), (w_kv_b, 2))):
                        cols = unit_shape(n + k)[1]
                        load(quad(n + k), n + k, halves_of(w, layer, range(tiles), cols * h, cols))
                for n in range(U_LATE, U_OUT):
                    i = n - U_LATE
                    col, cols = LATE[i // 4]
                    load(quad(n), n, halves_of(w_in, layer, range(4 * (i % 4), 4 * (i % 4) + 4), col, cols), i == 0)
                for pair in range(2):
                    for i in range(8):
                        n = U_OUT + 8 * pair + i
                        load(quad(n), n, [part for kts in (OUT_KT[i // 2][:2], OUT_KT[i // 2][2:])
                                          for part in [w_out[layer, kts[0] * P:(kts[1] + 1) * P,
                                                             bass.ds((2 * pair + i % 2) * NCH, NCH)]]])
                with sp.Fori(0, FF_CHUNKS) as f:
                    for i in range(8):
                        w = w_gate if i < 4 else w_up
                        load(quad(U_FF + i) + 2 * f, U_FF + i,
                             halves_of(w, layer, range(4 * (i % 4), 4 * (i % 4) + 4), f * NCH, NCH))
                for c in range(4):
                    for i, kts in enumerate(DOWN_KT):
                        n = U_DOWN + len(DOWN_KT) * c + i
                        load(quad(n), n, halves_of(w_down, layer, kts, c * NCH, NCH))
            load(DEPTH * QUADS, 0, halves_of(w_in, 0, EARLY_UNITS[0][1], *EARLY[0]))
            sp.wait_ge(act_made, DEPTH * FF_CHUNKS * NT)
            sp.dma_start(last_gain[:, :], final_norm.to_broadcast([P, D_MODEL])).then_inc(setup_in, 16)
            for half in range(2):
                part = slice(half * D_MODEL // 2, (half + 1) * D_MODEL // 2)
                for t, made in ((1, xn_act), (0, xn_vec)):
                    sp.wait_ge(made, half + 1)
                    sp.dma_start(out[t * P:(t + 1) * P, part], xn[:, t, part]).then_inc(stored, 16)
            sp.wait_ge(stored, 16 * 2 * NT)

        @block.tensor
        def _(pe):
            pe.wait_ge(consts_in, 16)
            with pe.Fori(0, DEPTH) as layer:
                def need(s, per_layer, k):
                    pe.wait_ge(s, layer * per_layer + k)

                def bank_taken(key, b):
                    need(bank_free[b], USES[b], ROUND[key][b] + 1)
                    return bank[b]

                def copied(key, b):
                    need(bank_free[b], USES[b], ROUND[key][b] + 2)

                def projected_by_now(chunks):
                    parity, r = chunk_round(chunks - 1)
                    need(acc_out_act[parity], R_OUT, r + 1)
                    need(acc_out_vec[parity], R_OUT, r + 1)

                def transpose(dst, src):
                    return pe.transpose(dst, src, ident)

                def unit(n, kts, parity, operand, first, last, turn=0, norm=None):
                    s = n % 4
                    _, cols = unit_shape(n)
                    pe.wait_ge(lo_made[s], layer * QUADS + n // 4 + 1 + turn)
                    wh = w_hi[s][:, 0:len(kts) * cols].rearrange("p (k n) -> p k n", n=cols)
                    wl = w_lo[s][:, 0:len(kts) * cols].rearrange("p (k n) -> p k n", n=cols)
                    for i, kt in enumerate(kts):
                        hi, lo, at = operand(kt)
                        if norm and kt % 2 == 0:
                            copied((norm, kt // 2), 4 + kt // 2 % 4)
                        for t in range(NT):
                            acc = bank[2 * parity + t][:, 0:cols]
                            a = hi[:, at, t * P:(t + 1) * P]
                            b = lo[:, at, t * P:(t + 1) * P]
                            pe.matmul(acc, a, wh[:, i, :], start=first and i == 0, stop=False)
                            pe.matmul(acc, a, wl[:, i, :], start=False, stop=False)
                            mm = pe.matmul(acc, b, wh[:, i, :], start=False, stop=last and i == len(kts) - 1)
                    mm.then_inc(used[s], 1)

                def normed(kt):
                    return xt_hi, xt_lo, kt

                def hidden(kt):
                    return f_hi, f_lo, kt

                def acc_taken(parity, r, in_loop=False, f=0):
                    if r == 0:
                        need(x_added, 16, NT * (3 + parity))
                        return
                    if r <= R_OUT:
                        need(acc_out_act[parity], R_OUT, r)
                        need(acc_out_vec[parity], R_OUT, r)
                    elif r < R_FF or r == R_FF and not in_loop:
                        need(x_added, 16, 8 + NT * (2 * (r - 1 - R_OUT) + parity + 1))
                    elif r == R_FF:
                        need((silu_made, act_made)[parity], FF_CHUNKS * NT, NT * f)
                    elif r == R_DOWN:
                        need((silu_made, act_made)[parity], FF_CHUNKS * NT, NT * FF_CHUNKS)
                    else:
                        need(x_added, 16, 16 + NT * (parity + 1))

                def norm_turn(which, rounds):
                    for r in rounds:
                        need(x_added, 16, (0 if which == "norm1" else 8) + NT * (r // 2 + 1))
                        b = 4 + r % 4
                        ps = bank_taken((which, r), b)
                        for i in range(2):
                            for t in range(NT):
                                kt = 2 * r + i
                                mm = transpose(ps[:, i * SEQ + t * P:i * SEQ + (t + 1) * P],
                                               resid[:, t, kt * P:(kt + 1) * P])
                        mm.then_inc(bank_full[b], 1)

                def qa_turn(b):
                    need(qa_scaled, 1, 1)
                    ps = bank_taken(("qa_turn", b), 4 + b)
                    for i in range(2):
                        for t in range(NT):
                            mm = transpose(ps[:, i * SEQ + t * P:i * SEQ + (t + 1) * P],
                                           p2c(t, C_QA + (2 * b + i) * P, P))
                    mm.then_inc(bank_full[4 + b], 1)

                def mla_unit(h, kv):
                    n = U_MLA + 2 * h + kv
                    s, (kts, cols) = n % 4, unit_shape(n)
                    if h == 0 and kv == 0:
                        for b in range(3):
                            copied(("qa_turn", b), 4 + b)
                    pe.wait_ge(lo_made[s], layer * QUADS + n // 4 + 1)
                    acc_taken(kv, R_MLA + h)
                    wh = w_hi[s][:, 0:kts * cols].rearrange("p (k h n) -> p k h n", k=kts, h=2)
                    wl = w_lo[s][:, 0:kts * cols].rearrange("p (k h n) -> p k h n", k=kts, h=2)
                    ps, k0 = bank[2 * kv], 4 * kv
                    for head in range(2):
                        dst = ps[:, head * SEQ:(head + 1) * SEQ]
                        for k in range(kts):
                            a, b = wh[:, k, head, 0:P], wl[:, k, head, 0:P]
                            pe.matmul(dst, a, qa_hi[:, k0 + k, :], start=k == 0, stop=False)
                            pe.matmul(dst, a, qa_lo[:, k0 + k, :], start=False, stop=False)
                            pe.matmul(dst, b, qa_hi[:, k0 + k, :], start=False, stop=k == kts - 1)
                    ps, w = bank[2 * kv + 1], cols // 2 - P
                    for t in range(NT):
                        dst = ps[:, t * 2 * w:(t + 1) * 2 * w].rearrange("p (h n) -> p h n", h=2)
                        for k in range(kts):
                            a = qa_hi[:, k0 + k, t * P:(t + 1) * P]
                            b = qa_lo[:, k0 + k, t * P:(t + 1) * P]
                            pe.matmul(dst, a, wh[:, k, :, P:], start=k == 0, stop=False)
                            pe.matmul(dst, a, wl[:, k, :, P:], start=False, stop=False)
                            mm = pe.matmul(dst, b, wh[:, k, :, P:], start=False, stop=k == kts - 1)
                    mm.then_inc(used[s], 1)

                def gla_turn(_):
                    projected_by_now(5)
                    for b, col in ((4, C_GQ), (5, C_GK)):
                        ps = bank_taken(("gla_turn", 0), b)
                        for g in range(2):
                            for t in range(NT):
                                mm = transpose(ps[:, g * SEQ + t * P:g * SEQ + (t + 1) * P], p2c(t, col + g * P, P))
                        mm.then_inc(bank_full[b], 1)
                    ps = bank_taken(("gla_turn", 0), 6)
                    for t in range(NT):
                        mm = transpose(ps[:, t * P:(t + 1) * P], p2c(t, C_GR, P))
                    mm.then_inc(bank_full[6], 1)

                def gla_logits(_):
                    copied(("gla_turn", 0), 6)
                    need(rows_in, 32, 32)
                    ps = bank_taken(("gla_logits", 0), 7)
                    for g in range(2):
                        mm = pe.matmul(ps[:, g * SEQ:(g + 1) * SEQ], gw_sb[:, g * P:(g + 1) * P], grt[:, :],
                                       start=True, stop=True)
                    mm.then_inc(bank_full[7], 1)

                def level_mm(i):
                    if i == N_LEVELS - 1:
                        copied(("gla_turn", 0), 4)
                        copied(("gla_turn", 0), 5)
                    if i < N_LEVELS - 1:
                        need(level_made, N_LEVELS - 1, i + 1)
                    q, k = (gqt, gkt) if i == N_LEVELS - 1 else (ql[:, i % 2], kl[:, i % 2])
                    for par in range(2):
                        ps = bank_taken(("level_mm", i), 6 + par)
                        rows_ = slice(par * 64, par * 64 + 64)
                        for g in range(2):
                            if i == 0:
                                mm = pe.matmul(ps[:, g * P:(g + 1) * P], k[rows_, g, 0:P], q[rows_, g, P:SEQ],
                                               start=True, stop=True)
                                continue
                            for t in range(NT):
                                at = (t * 2 + g) * P
                                dst, moving = ps[:, at:at + P], q[rows_, g, t * P:(t + 1) * P]
                                if LEVELS[i - 1]:
                                    dst, moving = (later_halves(x, LEVELS[i - 1]) for x in (dst, moving))
                                mm = pe.matmul(dst, k[rows_, g, t * P:(t + 1) * P], moving, start=True, stop=True)
                        mm.then_inc(bank_full[6 + par], 1)

                def gla_out(_):
                    copied(("level_mm", N_LEVELS - 2), 7)
                    for t in range(NT):
                        ps = bank_taken(("gla_out", 0), 6 + t)
                        for h in range(GLA_HEADS):
                            dst, par, g = ps[:, h * P:(h + 1) * P], h % 2, h // 2
                            if t == 1:
                                pe.matmul(dst, cross[:, par, g, :], p2c(0, C_GV + h * P, P), start=True, stop=False)
                            mm = pe.matmul(dst, att[:, par, t, g, :], p2c(t, C_GV + h * P, P), start=t == 0, stop=True)
                        mm.then_inc(bank_full[6 + t], 1)

                def rope_turn(_):
                    need(roped, 1, 1)
                    for b in range(2):
                        ps = bank_taken(("rope_turn", 0), 4 + b)
                        for i in range(2):
                            for t in range(NT):
                                pair = 2 * b + i
                                mm = transpose(ps[:, i * SEQ + t * P:i * SEQ + (t + 1) * P],
                                               qr[:, t, 2 * pair:2 * pair + 2, :].rearrange("p a b -> p (a b)"))
                        mm.then_inc(bank_full[4 + b], 1)

                def diff_turn(i):
                    g, part = i // 2, i % 2
                    projected_by_now(7 + i)
                    for b, heads in ((6, (0, 1)), (7, (2,))):
                        ps = bank_taken(("diff_turn", i), b)
                        for k, h in enumerate(heads):
                            for t in range(NT):
                                col = part * DIFF_QK + (3 * g + h) * P
                                mm = transpose(ps[:, k * SEQ + t * P:k * SEQ + (t + 1) * P], pd[:, t, col:col + P])
                        mm.then_inc(bank_full[b], 1)

                def head_scores(j):
                    key = ("head_scores", j)
                    if j < MLA_HEADS:
                        if j == 0:
                            copied(("rope_turn", 0), 4)
                            copied(("rope_turn", 0), 5)
                            for parity in range(2):
                                need(acc_out_act[parity], R_OUT, R_LATE)
                        ps = bank_taken(key, 6)
                        r = slice(64 * (j % 2), 64 * (j % 2) + 64)
                        for t in range(NT):
                            dst = ps[:, t * P:t * P + (t + 1) * P]
                            n = (t + 1) * P
                            pe.matmul(dst, qnt[:, j, t * P:n], knt[:, j, 0:n], start=True, stop=False)
                            mm = pe.matmul(dst, qrt[r, j // 2, t * P:n], qrt[r, 3, 0:n], start=False, stop=True)
                        mm.then_inc(bank_full[6], 1)
                        return
                    h = j - MLA_HEADS
                    copied(("diff_turn", 2 * (h // 3) + 1), 7)
                    for branch in range(2):
                        ps = bank_taken(key, 6 + branch)
                        r = slice(64 * branch, 64 * branch + 64)
                        for t in range(NT):
                            n = (t + 1) * P
                            mm = pe.matmul(ps[:, t * P:t * P + n], dqt[r, h % 3, t * P:n], dkt[r, h % 3, 0:n],
                                           start=True, stop=True)
                        mm.then_inc(bank_full[6 + branch], 1)

                def head_turn(j):
                    if j < MLA_HEADS:
                        need(exped, HEADS, j + 1)
                    else:
                        need(probs_made, DIFF_HEADS, j - MLA_HEADS + 1)
                    ps = bank_taken(("head_turn", j), 4)
                    for i in range(3):
                        mm = transpose(ps[:, i * P:(i + 1) * P], e_of(j)[0][:, i * P:(i + 1) * P])
                    mm.then_inc(bank_full[4], 1)

                def head_out(j):
                    copied(("head_turn", j), 4)
                    if j == 0:
                        need(acc_out_vec[1], R_OUT, R_LATE)
                    if j in (MLA_HEADS, MLA_HEADS + 3):
                        projected_by_now(11 + (j - MLA_HEADS) // 3)

                    def v(t):
                        if j < MLA_HEADS:
                            return mv[:, t, j, :]
                        return pd[:, t, C_DV + (j - MLA_HEADS) * P:C_DV + (j - MLA_HEADS + 1) * P]

                    ps, p = bank_taken(("head_out", j), 5), pt[PT_OF[j]]
                    pe.matmul(ps[:, 0:P], p[:, 0:P], v(0), start=True, stop=True)
                    pe.matmul(ps[:, P:2 * P], p[:, P:2 * P], v(0), start=True, stop=False)
                    pe.matmul(ps[:, P:2 * P], p[:, 2 * P:3 * P], v(1), start=False, stop=True).then_inc(bank_full[5], 1)

                def mix_turn(kt0):
                    b = mix_bank(kt0)
                    if kt0 in (6, 8):
                        need(gla_mixed, 1, 1)
                    elif kt0 >= 10:
                        if b != 5:
                            copied(("head_out", kt0 - 10 + 1), 5)
                    else:
                        need(diff_mixed, 2, 2 if kt0 else 1)
                    ps = bank_taken(("mix_turn", kt0), b)
                    for i in range(2):
                        for t in range(NT):
                            kt = kt0 + i
                            src = (pd[:, t, C_DV + kt * P:C_DV + (kt + 1) * P] if kt < 6 else
                                   p2c(t, C_GV + (kt - 6) * P, P) if kt < 10 else mv[:, t, kt - 10, :])
                            mm = transpose(ps[:, i * SEQ + t * P:i * SEQ + (t + 1) * P], src)
                    mm.then_inc(bank_full[b], 1)

                steps = {"qa_turn": qa_turn, "gla_turn": gla_turn, "gla_logits": gla_logits, "level_mm": level_mm,
                         "gla_out": gla_out, "rope_turn": rope_turn, "diff_turn": diff_turn, "head_scores": head_scores,
                         "head_turn": head_turn, "head_out": head_out, "mix_turn": mix_turn}

                def hook(n):
                    for name, arg in HOOKS.get(n, []):
                        if name in steps:
                            steps[name](arg)

                norm_turn("norm1", range(KT // 4))
                for n, (c, kts) in enumerate(EARLY_UNITS):
                    if kts[0] == 0:
                        acc_taken(c % 2, c // 2)
                    unit(n, kts, c % 2, normed, kts[0] == 0, kts[-1] == KT - 1, norm=None if c else "norm1")
                    if n == 0:
                        norm_turn("norm1", range(KT // 4, KT // 2))
                    hook(n)
                for h in range(MLA_PAIRS):
                    for kv in range(2):
                        mla_unit(h, kv)
                        hook(U_MLA + 2 * h + kv)
                for c in range(len(LATE)):
                    acc_taken(c % 2, R_LATE + c // 2)
                    for u in range(4):
                        n = U_LATE + 4 * c + u
                        unit(n, range(4 * u, 4 * u + 4), c % 2, normed, u == 0, u == 3)
                        hook(n)
                for pair in range(2):
                    for i in range(8):
                        if i < 2:
                            acc_taken(i, R_OUT + pair)
                        if pair == 0 and i % 2 == 0:
                            for kt0 in {kt - kt % 2 for kt in OUT_KT[i // 2]}:
                                copied(("mix_turn", kt0), mix_bank(kt0))
                        n = U_OUT + 8 * pair + i
                        unit(n, OUT_KT[i // 2], i % 2, mixed, i < 2, i >= 6)
                        hook(n)
                norm_turn("norm2", range(KT // 4))

                def ff_turn(f):
                    pe.wait_ge(act_made, layer * (FF_CHUNKS * NT) + NT * f + NT)
                    for b in (4, 5):
                        pe.wait_ge(bank_free[b], layer * USES[b] + ROUND[("ff_turn", 0)][b] + f + 1)
                        for i in range(2):
                            for t in range(NT):
                                j = 2 * (b - 4) + i
                                mm = transpose(bank[b][:, i * SEQ + t * P:i * SEQ + (t + 1) * P],
                                               act_sb[:, t, j * P:(j + 1) * P])
                        mm.then_inc(bank_full[b], 1)

                def ff_chunk(f, first):
                    for half in range(2):
                        acc_taken(half, R_FF, not first, f)
                        for u in range(4):
                            unit(U_FF + 4 * half + u, range(4 * u, 4 * u + 4), half, normed, u == 0, u == 3,
                                 turn=2 * f, norm="norm2" if first and half == 0 else None)
                            if first and half == 0 and u == 0:
                                norm_turn("norm2", range(KT // 4, KT // 2))
                            if half == 0 and u == 1 and not first:
                                ff_turn(f - 1)

                ff_chunk(0, True)
                with pe.Fori(1, FF_CHUNKS) as f:
                    ff_chunk(f, False)
                for c in range(4):
                    acc_taken(c % 2, R_DOWN + c // 2)
                    for i, kts in enumerate(DOWN_KT):
                        if c == 0 and i in (0, 10):
                            for b in (4, 5):
                                need(bank_free[b], USES[b], USES[b] + (i != 0))
                        unit(U_DOWN + len(DOWN_KT) * c + i, kts, c % 2, hidden, i == 0, i == len(DOWN_KT) - 1)
                        if c == 0 and i == 1:
                            ff_turn(FF_CHUNKS - 1)

        @block.scalar
        def _(act):
            count = [0]

            def link(ins):
                count[0] += 1
                ins.then_inc(act_chain, 1)
                return count[0]

            act.wait_ge(consts_in, 16)
            for c in range(3):
                act.wait_ge(x_in[c], 16)
                for t in range(NT):
                    if t + c:
                        act.wait_ge(squared, NT * c + t)
                    act.activation(junk[:, :], resid[:, t, c * NCH:(c + 1) * NCH], ACT.Square,
                                   accum_out=ssq[:, t, c:c + 1]).then_inc(squared, 1)
            def round_unit(quad, n):
                s = n % 4
                kts, cols = unit_shape(n)
                act.wait_ge(full[s], (quad + 1) * 32)
                act.activation(w_hi[s][:, 0:kts * cols], stage[s][:, 0:kts * cols], ACT.Copy).then_inc(hi_made[s], 1)

            round_unit(0, 0)
            act.dma_start(levels_in[:, :, :], levels).then_inc(masks_in, 16)
            act.dma_start(caus_sb[:, :], causal).then_inc(masks_in, 16)
            act.wait_ge(setup_in, 32)

            with act.Fori(0, DEPTH) as layer:
                def need(s, per_layer, k):
                    act.wait_ge(s, layer * per_layer + k)

                def bank_in(key, b):
                    need(bank_full[b], USES[b], ROUND[key][b] + 1)
                    return bank[b]

                def complete(n):
                    need(used[n % 4], QUADS, n // 4 + 2)

                def gain(i):
                    return gain_sb[:, bass.ds(layer, 1), i:i + 1].rearrange("p a b -> p (a b)")

                def squares_of(c, done):
                    for t in range(NT):
                        need(x_added, 16, done + NT * c + t + 1)
                        need(squared, 16, done + NT * c + t)
                        act.activation(junk[:, :], resid[:, t, c * NCH:(c + 1) * NCH], ACT.Square,
                                       accum_out=ssq[:, t, c:c + 1]).then_inc(squared, 1)

                def norm(which, seen):
                    g0 = G_ATTN if which == "norm1" else G_FFN
                    for r in range(KT // 2):
                        if r in (KT // 4, KT // 4 + 2):
                            n = (U_FF if seen else 0) + (r - KT // 4) // 2 + 1
                            round_unit(layer * QUADS + n // 4, n)
                        ps = bank_in((which, r), 4 + r % 4)
                        for i in range(2):
                            act.activation(xt_hi[:, 2 * r + i, :], ps[:, i * SEQ:(i + 1) * SEQ], ACT.Copy,
                                           scale=gain(g0 + 2 * r + i)).then_inc(xt_hi_made, 1)
                    squares_of(3, 8 * seen)

                def evac(c):
                    if c == 0:
                        need(rstd_made, len(POW), POW["norm1"] + 1)
                    col, cols = (EARLY + LATE)[c]
                    complete(last_unit(c))
                    act.activation(projected(0, col, cols), bank[2 * (c % 2)][:, 0:cols], ACT.Copy, scale=rstd_x[:, 0:1])\
                       .then_inc(acc_out_act[c % 2], 1)

                def angles_made(_):
                    need(angles, NT, NT)
                    act.activation(sin_sb[:, :, 0, :], sin_sb[:, :, 0, :], ACT.Sin)
                    act.activation(cos_sb[:, :, 0, :], cos_sb[:, :, 0, :], ACT.Sin).then_inc(waves, 1)

                def qa_rms(_):
                    need(acc_out_vec[1], R_OUT, 1)
                    need(acc_out_act[1], R_OUT, 1)
                    for t in range(NT):
                        for i, (col, n) in enumerate(((C_QA, MLA_Q_RANK), (C_KVA, MLA_KV_RANK))):
                            at, m = 4 * i + t * n // SEQ, n // SEQ
                            act.activation(qnt[:, at:at + m, :].rearrange("p a b -> p (a b)"), p2c(t, col, n), ACT.Square,
                                           accum_out=m_ss[:, 2 * i + t:2 * i + t + 1]).then_inc(m_squared, 1)

                def qa_turn(b):
                    ps = bank_in(("qa_turn", b), 4 + b)
                    for i in range(2):
                        act.activation(qa_hi[:, 2 * b + i, :], ps[:, i * SEQ:(i + 1) * SEQ], ACT.Copy,
                                       scale=gain(G_QA + 2 * b + i)).then_inc(qa_hi_made, 1)

                def mla_q(h):
                    complete(U_MLA + 2 * h)
                    act.activation(qnt[:, 2 * h:2 * h + 2, :].rearrange("p a b -> p (a b)"), bank[0][:, :], ACT.Copy)\
                       .then_inc(acc_out_act[0], 1)

                def mla_kv(h):
                    complete(U_MLA + 2 * h + 1)
                    act.activation(knt[:, 2 * h:2 * h + 2, :].rearrange("p a b -> p (a b)"), bank[2][:, :], ACT.Copy)\
                       .then_inc(acc_out_act[1], 1)

                def gla_turn(_):
                    ps = bank_in(("gla_turn", 0), 6)
                    act.activation(grt[:, :], ps[0:GLA_RANK, 0:SEQ], ACT.Copy).then_inc(bank_free[6], 1)
                    ps = bank_in(("gla_turn", 0), 4)
                    act.activation(gqt[:, :, :].rearrange("p a b -> p (a b)"), ps[:, :], ACT.Copy,
                                   scale=GLA_DK ** -0.5).then_inc(bank_free[4], 1)

                def gla_decay(_):
                    need(gate_neg, 1, 1)
                    link(act.activation(gate_e[:, :, :], gate_e[:, :, :], ACT.Exp))
                    need(act_chain, ACT_LINKS, count[0])
                    act.activation(gate_e[:, :, :], gate_e[:, :, :], ACT.Ln, bias=1.0).then_inc(gate_ln, 1)

                def gla_silu(_):
                    need(acc_out_vec[1], R_OUT, 3)
                    need(acc_out_act[1], R_OUT, 3)
                    for t in range(NT):
                        act.activation(p2c(t, C_GO, NCH), p2c(t, C_GO, NCH), ACT.Silu).then_inc(gate_silu, 1)

                def level_exp(i):
                    need(span_made, N_LEVELS - 1, i + 1)
                    act.activation(decay_of(i), decay_of(i), ACT.Exp, scale=1.0 / GLA_TAU).then_inc(decay_made, 1)

                def rope_turn(_):
                    ps = bank_in(("rope_turn", 0), 4)
                    act.activation(qrt[:, 0:2, :].rearrange("p a b -> p (a b)"), ps[:, :], ACT.Copy)\
                       .then_inc(bank_free[4], 1)

                def diff_turn(i):
                    dst = dkt if i % 2 else dqt
                    ps = bank_in(("diff_turn", i), 6)
                    act.activation(dst[:, 0:2, :].rearrange("p a b -> p (a b)"), ps[:, :], ACT.Copy)\
                       .then_inc(bank_free[6], 1)

                def head_exp(j):
                    scale = (MLA_NOPE + MLA_ROPE) ** -0.5 if j < MLA_HEADS else DIFF_HD ** -0.5
                    if j == MLA_HEADS:
                        need(lam_dot, 1, 1)
                        act.activation(lam2e[:, :], lam2[:, :], ACT.Exp).then_inc(lam_exp, 1)
                    need(masked, HEADS, j + 1)
                    for branch in range(1 if j < MLA_HEADS else 2):
                        for t in range(NT):
                            k = 4 * (j % 2) + 2 * branch + t
                            part = e_of(j)[branch][:, t * P:t * P + (t + 1) * P]
                            last = act.activation(part, part, ACT.Exp, bias=nmx[:, k:k + 1], scale=scale,
                                                  accum_out=esum[:, k:k + 1])
                    last.then_inc(exped, 1)

                def head_turn(j):
                    ps = bank_in(("head_turn", j), 4)
                    act.activation(pt[PT_OF[j]][:, :], ps[:, 0:3 * P], ACT.Copy).then_inc(bank_free[4], 1)

                def mix_turn(kt0):
                    ps = bank_in(("mix_turn", kt0), mix_bank(kt0))
                    hi, _, at = mixed(kt0)
                    act.activation(hi[:, at:at + 2, :].rearrange("p a b -> p (a b)"), ps[:, :], ACT.Copy)\
                       .then_inc(xt_hi_made, 2)

                steps = {"evac": evac, "angles": angles_made, "qa_rms": qa_rms, "qa_turn": qa_turn,
                         "mla_q": mla_q, "mla_kv": mla_kv,
                         "gla_turn": gla_turn, "gla_decay": gla_decay, "gla_silu": gla_silu, "level_exp": level_exp,
                         "rope_turn": rope_turn, "diff_turn": diff_turn, "head_exp": head_exp,
                         "head_turn": head_turn, "mix_turn": mix_turn}

                act.activation(warm[:, :], k_sb[:, 0:1], ACT.Copy)
                norm("norm1", 0)
                for n in range(U_FF):
                    for name, arg in HOOKS.get(n, []):
                        if name in steps:
                            steps[name](arg)
                    if n < U_FF - LEAD + 1:
                        round_unit(layer * QUADS + (n + LEAD) // 4, n + LEAD)
                    if n >= U_OUT and (n - U_OUT) % 8 >= 6 and n < U_FF - 1:
                        squares_of(2 * ((n - U_OUT) // 8) + (n - U_OUT) % 2, 8)
                norm("norm2", 1)

                def ff_turn(f):
                    for b in (4, 5):
                        act.wait_ge(bank_full[b], layer * USES[b] + ROUND[("ff_turn", 0)][b] + f + 1)
                        dst = f_hi[:, bass.ds(f * 4 + 2 * (b - 4), 2), :].rearrange("p a b -> p (a b)")
                        act.activation(dst, bank[b][:, :], ACT.Copy).then_inc(ft_hi_made, 1)

                def ff_chunk(f, first):
                    for i in range(8):
                        round_unit(layer * QUADS + (U_FF + i + LEAD) // 4 + 2 * f, U_FF + i + LEAD)
                        if i == 1 and not first:
                            ff_turn(f - 1)
                        if i == 3:
                            if first:
                                need(rstd_made, len(POW), POW["norm2"] + 1)
                            act.wait_ge(used[3], layer * QUADS + (U_FF + 3) // 4 + 2 + 2 * f)
                            for t in range(NT):
                                act.activation(act_sb[:, t, :], bank[t][:, :], ACT.Silu, scale=rstd_x[:, t:t + 1])\
                                   .then_inc(silu_made, 1)

                ff_chunk(0, True)
                with act.Fori(1, FF_CHUNKS) as f:
                    ff_chunk(f, False)
                for n in range(U_DOWN, UNITS):
                    i = n - U_DOWN
                    if n < UNITS - LEAD + 1:
                        round_unit(layer * QUADS + (n + LEAD) // 4, n + LEAD)
                    if i == 1:
                        ff_turn(FF_CHUNKS - 1)
                    if i % len(DOWN_KT) == len(DOWN_KT) - 1 and n < UNITS - 1:
                        squares_of(i // len(DOWN_KT), 16)
            for t in range(NT):
                act.wait_ge(x_added, 16 * DEPTH + 7 + t)
                act.wait_ge(squared, 16 * DEPTH + 6 + t)
                act.activation(junk[:, :], resid[:, t, 3 * NCH:4 * NCH], ACT.Square, accum_out=ssq[:, t, 3:4])\
                   .then_inc(squared, 1)
            act.wait_ge(rstd_made, DEPTH * len(POW) + 1)
            for i, half in enumerate((slice(0, D_MODEL // 2), slice(D_MODEL // 2, D_MODEL))):
                act.wait_ge(gain_taken, i + 1)
                act.activation(xn[:, 1, half], xn[:, 1, half], ACT.Copy, scale=rstd_x[:, 1:2]).then_inc(xn_act, 1)
            assert count[0] == ACT_LINKS, count[0]

        @block.gpsimd
        def _(pool):
            pool.memset(halves[:, :], -0.5).then_inc(halves_made, 1)
            pool.wait_ge(halves_made, 1)
            pool.wait_ge(masks_in, 32)
            pool.tensor_copy(lev_sb[:, :, :], levels_in[:, :, :]).then_inc(masks_made, 1)
            with pool.Fori(0, DEPTH) as layer:
                def need(s, per_layer, k):
                    pool.wait_ge(s, layer * per_layer + k)

                def power(name, n, to=rstd):
                    need(ms_made, len(POW), POW[name] + 1)
                    pool.tensor_tensor(to[:, 0:n], ms[:, 0:n], halves[:, 0:n], ALU.pow).then_inc(rstd_made, 1)

                power("norm1", NT, rstd_x)
                for n in range(U_FF):
                    for name, arg in HOOKS.get(n, []):
                        if name == "qa_rms":
                            power("mla", 4)
                        if name == "gla_rms":
                            power("gla", 8)
                        if name == "diff_rms":
                            power(f"diff{arg}", 6)
                        if name == "level_exp":
                            need(decay_made, N_LEVELS - 1, arg + 1)
                            if arg == 0:
                                for b in (4, 5):
                                    need(bank_free[b], USES[b], ROUND[("gla_turn", 0)][b] + 2)
                            if arg >= 2:
                                need(bank_full[7], USES[7], ROUND[("level_mm", arg - 2)][7] + 1)
                            pool.tensor_tensor(ql[:, arg % 2], gqt[:, :, :], decay_of(arg), ALU.mult)
                            pool.tensor_tensor(kl[:, arg % 2], gkt[:, :, :], decay_of(arg), ALU.mult)\
                                .then_inc(level_made, 1)
                        if name == "rope":
                            need(kr_in, 1, 1)
                            need(waves, 1, 1)
                            cos = cos_sb[:, :, :, :].to_broadcast([P, NT, 7, 32])
                            sin = sin_sb[:, :, :, :].to_broadcast([P, NT, 7, 32])
                            a, b = qr[:, :, 0:7, 0:32], qr[:, :, 0:7, 32:64]
                            pool.tensor_tensor(turn1[:, :, :, :], a, cos, ALU.mult)
                            pool.tensor_tensor(turn2[:, :, :, :], b, sin, ALU.mult)
                            pool.tensor_tensor(turn3[:, :, :, :], a, sin, ALU.mult)
                            pool.tensor_tensor(turn4[:, :, :, :], b, cos, ALU.mult).then_inc(rope_mul, 1)
                power("norm2", NT, rstd_x)
            pool.wait_ge(ms_made, DEPTH * len(POW) + 1)
            pool.tensor_tensor(rstd_x[:, :], ms[:, 0:NT], halves[:, 0:NT], ALU.pow).then_inc(rstd_made, 1)

        @block.vector
        def _(vec):
            count = [0]

            def rest_of_unit(quad, n):
                s = n % 4
                kts, cols = unit_shape(n)
                vec.wait_ge(hi_made[s], quad + 1)
                vec.tensor_tensor(w_lo[s][:, 0:kts * cols], stage[s][:, 0:kts * cols],
                                  w_hi[s][:, 0:kts * cols].bitcast(F32), ALU.subtract).then_inc(lo_made[s], 1)

            for i, free in enumerate([*used, *bank_free.values()]):
                vec.memset(mx[:, i:i + 1], 0.0).then_inc(free, 1)

            for c in range(4):
                vec.wait_ge(x_in[c], 16)
                vec.memset(esum[:, c:c + 1], 1.0).then_inc(x_added, NT)

            vec.wait_ge(consts_in, 16)
            vec.wait_ge(setup_in, 32)
            vec.tensor_copy(pos_f[:, :], pos_i[:, :]).then_inc(positions_made, 1)
            vec.wait_ge(positions_made, 1)
            rest_of_unit(0, 0)

            with vec.Fori(0, DEPTH) as layer:
                def need(s, per_layer, k):
                    vec.wait_ge(s, layer * per_layer + k)

                def link(ins):
                    count[0] += 1
                    ins.then_inc(vec_chain, 1)
                    need(vec_chain, VEC_LINKS, count[0])

                def bank_in(key, b):
                    need(bank_full[b], USES[b], ROUND[key][b] + 1)
                    return bank[b]

                def masked_bank_in(key, b):
                    turn = vec.to_reg(layer * USES[b] + (ROUND[key][b] + 1))
                    vec.wait_ge(masks_made, 1)
                    vec.wait_ge(bank_full[b], turn)
                    return bank[b]

                def complete(n):
                    need(used[n % 4], QUADS, n // 4 + 2)

                def copied(key, b):
                    need(bank_free[b], USES[b], ROUND[key][b] + 2)

                def gain(i):
                    return gain_sb[:, bass.ds(layer, 1), i:i + 1].rearrange("p a b -> p (a b)")

                def scaled(n, width, of):
                    vec.tensor_scalar(ms[:, 0:n], of, 1.0 / width, EPS, ALU.mult, ALU.add).then_inc(ms_made, 1)

                def norm(which, seen):
                    g0 = G_ATTN if which == "norm1" else G_FFN
                    for r in range(KT // 2):
                        if r in (KT // 4, KT // 4 + 2):
                            n = (U_FF if seen else 0) + (r - KT // 4) // 2 + 1
                            rest_of_unit(layer * QUADS + n // 4, n)
                        ps = bank_in((which, r), 4 + r % 4)
                        need(xt_hi_made, 48, 32 * seen + 2 * r + 2)
                        for i in range(2):
                            kt = 2 * r + i
                            ins = vec.scalar_tensor_tensor(xt_lo[:, kt, :], ps[:, i * SEQ:(i + 1) * SEQ], gain(g0 + kt),
                                                           xt_hi[:, kt, :].bitcast(F32), ALU.mult, ALU.subtract)
                        ins.then_inc(bank_free[4 + r % 4], 1)
                    vec.wait_ge(squared, layer * 16 + 8 * seen + 8)
                    link(vec.tensor_reduce(ms[:, 0:NT], ssq[:, :, :], AX.X, ALU.add))
                    scaled(NT, D_MODEL, ms[:, 0:NT])

                def evac(c):
                    if c == 0:
                        need(rstd_made, len(POW), POW["norm1"] + 1)
                    col, cols = (EARLY + LATE)[c]
                    complete(last_unit(c))
                    vec.tensor_scalar(projected(1, col, cols), bank[2 * (c % 2) + 1][:, 0:cols], rstd_x[:, 1:2], None,
                                      ALU.mult)\
                       .then_inc(acc_out_vec[c % 2], 1)

                def angles_made(_):
                    inv = k_sb[:, K_INV:K_INV + 32]
                    for t in range(NT):
                        ang, turns = sin_sb[:, t, 0, :], cos_sb[:, t, 0, :]
                        link(vec.tensor_scalar(ang, inv, pos_f[:, t:t + 1], None, ALU.mult))
                        link(vec.tensor_scalar(turns, ang, 1.0 / (2 * np.pi), ROUNDER, ALU.mult, ALU.add))
                        link(vec.tensor_scalar(turns, turns, ROUNDER, None, ALU.subtract))
                        for part in TWO_PI:
                            link(vec.scalar_tensor_tensor(ang, turns, -part, ang, ALU.mult, ALU.add))
                        link(vec.tensor_scalar(ang, ang, 3.1415925, -3.1415925, ALU.min, ALU.max))
                        link(vec.scalar_tensor_tensor(turns, ang, -1.0, ang, ALU.mult, ALU.min))
                        vec.tensor_scalar(turns, turns, float(np.pi / 2), None, ALU.add).then_inc(angles, 1)

                def qa_rms(_):
                    need(m_squared, 4, 4)
                    vec.tensor_scalar(ms[:, 0:2], m_ss[:, 0:2], 1.0 / MLA_Q_RANK, EPS, ALU.mult, ALU.add)
                    vec.tensor_scalar(ms[:, 2:4], m_ss[:, 2:4], 1.0 / MLA_KV_RANK, EPS, ALU.mult, ALU.add)\
                       .then_inc(ms_made, 1)

                def qa_scale(_):
                    need(rstd_made, len(POW), POW["mla"] + 1)
                    need(acc_out_act[1], R_OUT, 1)
                    need(acc_out_vec[1], R_OUT, 1)
                    for t in range(NT):
                        for i, (col, n) in enumerate(((C_QA, MLA_Q_RANK), (C_KVA, MLA_KV_RANK))):
                            ins = vec.tensor_scalar(p2c(t, col, n), p2c(t, col, n), rstd[:, 2 * i + t:2 * i + t + 1], None,
                                                    ALU.mult)
                    ins.then_inc(qa_scaled, 1)

                def qa_turn(b):
                    ps = bank_in(("qa_turn", b), 4 + b)
                    need(qa_hi_made, 6, 2 * b + 2)
                    for i in range(2):
                        k = 2 * b + i
                        ins = vec.scalar_tensor_tensor(qa_lo[:, k, :], ps[:, i * SEQ:(i + 1) * SEQ], gain(G_QA + k),
                                                       qa_hi[:, k, :].bitcast(F32), ALU.mult, ALU.subtract)
                    ins.then_inc(bank_free[4 + b], 1)

                def mla_q(h):
                    complete(U_MLA + 2 * h)
                    ps = bank[1][:, 0:4 * MLA_ROPE].rearrange("p (t h d) -> p t h d", t=NT, h=2)
                    vec.tensor_copy(qr[:, :, 2 * h:2 * h + 2, :], ps).then_inc(acc_out_vec[0], 1)

                def mla_kv(h):
                    complete(U_MLA + 2 * h + 1)
                    ps = bank[3][:, :].rearrange("p (t h d) -> p t h d", t=NT, h=2)
                    vec.tensor_copy(mv[:, :, 2 * h:2 * h + 2, :], ps).then_inc(acc_out_vec[1], 1)

                def gla_turn(_):
                    ps = bank_in(("gla_turn", 0), 5)
                    vec.tensor_copy(gkt[:, :, :].rearrange("p a b -> p (a b)"), ps[:, :]).then_inc(bank_free[5], 1)

                def gla_logits(_):
                    ps = bank_in(("gla_logits", 0), 7)
                    for g in range(2):
                        ins = vec.tensor_scalar(gate_z[:, g, :], ps[:, g * SEQ:(g + 1) * SEQ], gain(G_BIAS + g), None, ALU.add)
                    ins.then_inc(bank_free[7], 1)
                    copied(("gla_logits", 0), 7)
                    vec.scalar_tensor_tensor(gate_e[:, :, :], gate_z[:, :, :], -1.0, gate_z[:, :, :], ALU.mult, ALU.min)\
                       .then_inc(gate_neg, 1)
                    link(vec.memset(ones[:, :], 1.0))

                def gla_decay(_):
                    need(gate_ln, 1, 1)
                    link(vec.scalar_tensor_tensor(gate_z[:, :, :], gate_z[:, :, :], 0.0, gate_e[:, :, :], ALU.min,
                                                  ALU.subtract))
                    for g in range(2):
                        ins = vec.tensor_tensor_scan(logs[:, g, :], ones[:, :], gate_z[:, g, :], 0.0, ALU.mult, ALU.add)
                    link(ins)

                def att_cleared(_):
                    link(vec.memset(att[:, :, :, :, :].rearrange("p a b c d -> p (a b c d)"), 0.0))

                def level_prep(i):
                    size = SEQ // 2 if i == 0 else LEVELS[i - 1]
                    b = logs[:, :, :].rearrange("p g (n w) -> p g n w", w=2 * size)
                    o = decay_of(i).rearrange("p g (n w) -> p g n w", w=2 * size)
                    if i > 1:
                        need(level_made, N_LEVELS - 1, i - 1)
                    nb = SEQ // (2 * size)
                    mid = b[:, :, :, size - 1:size].to_broadcast([P, 2, nb, 2 * size])
                    link(vec.tensor_tensor(o, b, mid, ALU.subtract))
                    vec.scalar_tensor_tensor(decay_of(i), decay_of(i), -1.0, decay_of(i), ALU.mult, ALU.min)\
                       .then_inc(span_made, 1)

                def level_mm(i):
                    for par in range(2):
                        ps = masked_bank_in(("level_mm", i), 6 + par)
                        if i == 0:
                            ins = vec.tensor_copy(cross[:, par, :, :].rearrange("p g n -> p (g n)"), ps[:, 0:2 * P])
                        else:
                            mask, size = lev_sb[:, i - 1, :], LEVELS[i - 1]
                            dst = att[:, par, :, :, :].rearrange("p t g n -> p (t g n)")
                            if size:
                                dst, new, mask = (later_halves(x, size) for x in (dst, ps[:, :], mask))
                                nb = P // (2 * size)
                                dst, new = (x.rearrange("p (a n) w -> p a n w", a=4) for x in (dst, new))
                                mask = mask.rearrange("p (o n) w -> p o n w", o=1).to_broadcast([P, 4, nb, size])
                            else:
                                dst, new = (x.rearrange("p (a n) -> p a n", a=4) for x in (dst, ps[:, :]))
                                mask = mask.rearrange("p (o n) -> p o n", o=1).to_broadcast([P, 4, P])
                            ins = vec.copy_predicated(dst, mask, new)
                        ins.then_inc(bank_free[6 + par], 1)

                def gla_out(_):
                    bank_in(("gla_out", 0), 7)
                    for t in range(NT):
                        ps = bank_in(("gla_out", 0), 6 + t)
                        ins = vec.tensor_copy(p2c(t, C_GV, NCH), ps[:, :])
                        ins.then_inc(bank_free[6 + t], 1)
                    copied(("gla_out", 0), 7)

                def gla_rms(_):
                    o = p2[:, :, C_GV - C_GQ:C_GV - C_GQ + NCH]
                    link(vec.tensor_tensor(squares[:, :, :, :].rearrange("p t h d -> p t (h d)"), o, o, ALU.mult))
                    link(vec.tensor_reduce(ms[:, 0:8], squares[:, :, :, :].rearrange("p t h d -> p (t h) d"), AX.X, ALU.add))
                    scaled(8, GLA_DV, ms[:, 0:8])

                def gla_gated(_):
                    need(rstd_made, len(POW), POW["gla"] + 1)
                    need(gate_silu, 2, 2)
                    need(rows_in, 32, 32)
                    for t in range(NT):
                        o = p2c(t, C_GV, NCH).rearrange("p (h d) -> p h d", h=4)
                        r = rstd[:, 4 * t:4 * t + 4].rearrange("p (h o) -> p h o", o=1).to_broadcast([P, 4, P])
                        w = row_sb[:, W_GLA:W_GLA + P].rearrange("p (o d) -> p o d", o=1).to_broadcast([P, 4, P])
                        link(vec.tensor_tensor(o, o, r, ALU.mult))
                        link(vec.tensor_tensor(o, o, w, ALU.mult))
                        ins = vec.tensor_tensor(p2c(t, C_GV, NCH), p2c(t, C_GV, NCH), p2c(t, C_GO, NCH), ALU.mult)
                    ins.then_inc(gla_mixed, 1)

                def rope(_):
                    need(acc_out_vec[0], R_OUT, R_LATE)
                    vec.tensor_copy(qr[:, :, 6, :], p2[:, :, C_KR - C_GQ:C_KR - C_GQ + 64]).then_inc(kr_in, 1)
                    need(rope_mul, 1, 1)
                    vec.tensor_tensor(qr[:, :, 0:7, 0:32], turn1[:, :, :, :], turn2[:, :, :, :], ALU.subtract)
                    link(vec.tensor_tensor(qr[:, :, 0:7, 32:64], turn3[:, :, :, :], turn4[:, :, :, :], ALU.add))
                    vec.tensor_copy(qr[:, :, 7, :], qr[:, :, 6, :]).then_inc(roped, 1)

                def rope_turn(_):
                    ps = bank_in(("rope_turn", 0), 5)
                    vec.tensor_copy(qrt[:, 2:4, :].rearrange("p a b -> p (a b)"), ps[:, :])\
                       .then_inc(bank_free[5], 1)

                def lambdas(_):
                    need(rows_in, 32, 32)
                    link(vec.tensor_tensor(lam_prod[:, :], row_sb[:, W_LAM:W_LAM + P], row_sb[:, W_LAM + P:W_LAM + 2 * P],
                                           ALU.mult))
                    vec.tensor_reduce(lam2[:, :], lam_prod[:, :].rearrange("p (a b) -> p a b", a=2), AX.X, ALU.add)\
                       .then_inc(lam_dot, 1)

                def diff_turn(i):
                    ps = bank_in(("diff_turn", i), 7)
                    vec.tensor_copy((dkt if i % 2 else dqt)[:, 2, :], ps[:, 0:SEQ]).then_inc(bank_free[7], 1)

                def head_scores(j):
                    mla = j < MLA_HEADS
                    for branch in range(1 if mla else 2):
                        ps = masked_bank_in(("head_scores", j), 6 + branch)
                        for t in range(NT):
                            k, n = 4 * (j % 2) + 2 * branch + t, (t + 1) * P
                            ins = vec.tensor_tensor_reduce(e_of(j)[branch][:, t * P:t * P + n], ps[:, t * P:t * P + n],
                                                           caus_sb[:, 2 * P - n:2 * P], 1.0, NEG * 4, ALU.add, ALU.max,
                                                           mx[:, k:k + 1])
                        ins.then_inc(bank_free[6 + branch], 1)
                    for b in (6,) if mla else (6, 7):
                        copied(("head_scores", j), b)
                    scale = (MLA_NOPE + MLA_ROPE) ** -0.5 if mla else DIFF_HD ** -0.5
                    k = slice(4 * (j % 2), 4 * (j % 2) + (2 if mla else 4))
                    vec.tensor_scalar(nmx[:, k], mx[:, k], -scale, None, ALU.mult).then_inc(masked, 1)

                def head_norm(j):
                    mla = j < MLA_HEADS
                    k = slice(4 * (j % 2), 4 * (j % 2) + (2 if mla else 4))
                    need(exped, HEADS, j + 1)
                    if mla:
                        vec.reciprocal(held[:, 2 * j:2 * j + 2], esum[:, k]).then_inc(sums_inverted, 1)
                        return
                    if j == MLA_HEADS:
                        need(lam_exp, 1, 1)
                        link(vec.tensor_tensor(lam[:, :], lam2e[:, 0:1], lam2e[:, 1:2], ALU.subtract))
                        l0 = k_sb[:, bass.ds(K_LAM + 2 * layer, 1)]
                        link(vec.tensor_tensor(lam[:, :], lam[:, :], l0, ALU.add))
                    link(vec.reciprocal(rsum[:, :], esum[:, k]))
                    link(vec.tensor_scalar(rsum[:, 2:4], rsum[:, 2:4], lam[:, 0:1], None, ALU.mult))
                    for t in range(NT):
                        b = e_of(j)[1][:, t * P:t * P + (t + 1) * P]
                        ins = vec.tensor_scalar(b, b, rsum[:, 2 + t:3 + t], None, ALU.mult)
                    link(ins)
                    for t in range(NT):
                        a, b = (x[:, t * P:t * P + (t + 1) * P] for x in e_of(j))
                        ins = vec.scalar_tensor_tensor(a, a, rsum[:, t:t + 1], b, ALU.mult, ALU.subtract)
                    ins.then_inc(probs_made, 1)

                def head_out(j):
                    ps = bank_in(("head_out", j), 5)
                    if j < MLA_HEADS:
                        need(sums_inverted, MLA_HEADS, j + 1)
                        for t in range(NT):
                            ins = vec.tensor_scalar(mv[:, t, j, :], ps[:, t * P:(t + 1) * P], held[:, 2 * j + t:2 * j + t + 1],
                                                    None, ALU.mult)
                        ins.then_inc(bank_free[5], 1)
                        return
                    col = C_DV + (j - MLA_HEADS) * P
                    ins = vec.tensor_copy(pd[:, :, col:col + P], ps[:, 0:2 * P].rearrange("p (t d) -> p t d", t=NT))
                    ins.then_inc(bank_free[5], 1)

                def diff_rms(g):
                    copied(("head_out", MLA_HEADS + 3 * g + 2), 5)
                    o = pd[:, :, C_DV + g * G3:C_DV + (g + 1) * G3].rearrange("p t (h d) -> p t h d", h=3)
                    link(vec.tensor_tensor(squares[:, :, 0:3, :], o, o, ALU.mult))
                    link(vec.tensor_reduce(ms[:, 0:6].rearrange("p (t h) -> p t h", t=NT), squares[:, :, 0:3, :], AX.X, ALU.add))
                    scaled(6, DIFF_VD, ms[:, 0:6])
                    if g == 0:
                        w = row_sb[:, W_SUB:W_SUB + P]
                        link(vec.tensor_scalar(w, w, k_sb[:, bass.ds(K_LAM + 2 * layer + 1, 1)], None, ALU.mult))

                def diff_scale(g):
                    need(rstd_made, len(POW), POW[f"diff{g}"] + 1)
                    for t in range(NT):
                        o = pd[:, t, C_DV + g * G3:C_DV + (g + 1) * G3].rearrange("p (h d) -> p h d", h=3)
                        r = rstd[:, 3 * t:3 * t + 3].rearrange("p (h o) -> p h o", o=1).to_broadcast([P, 3, P])
                        w = row_sb[:, W_SUB:W_SUB + P].rearrange("p (o d) -> p o d", o=1).to_broadcast([P, 3, P])
                        link(vec.tensor_tensor(o, o, r, ALU.mult))
                        ins = vec.tensor_tensor(o, o, w, ALU.mult)
                    ins.then_inc(diff_mixed, 1)

                def mix_turn(kt0):
                    b = mix_bank(kt0)
                    ps = bank_in(("mix_turn", kt0), b)
                    order = [kt for _, kt in MIX_AT].index(kt0)
                    hi, lo, at = mixed(kt0)
                    need(xt_hi_made, 48, 16 + 2 * order + 2)
                    vec.tensor_tensor(lo[:, at:at + 2, :].rearrange("p a b -> p (a b)"), ps[:, :],
                                      hi[:, at:at + 2, :].rearrange("p a b -> p (a b)").bitcast(F32), ALU.subtract)\
                       .then_inc(bank_free[b], 1)

                steps = {"evac": evac, "angles": angles_made, "qa_rms": qa_rms, "qa_scale": qa_scale,
                         "att_cleared": att_cleared,
                         "qa_turn": qa_turn, "mla_q": mla_q,
                         "mla_kv": mla_kv, "gla_turn": gla_turn, "gla_logits": gla_logits, "gla_decay": gla_decay,
                         "level_prep": level_prep, "level_mm": level_mm, "gla_out": gla_out, "gla_rms": gla_rms,
                         "gla_gated": gla_gated, "rope": rope, "rope_turn": rope_turn, "diff_turn": diff_turn,
                         "head_norm": head_norm, "lambdas": lambdas, "head_scores": head_scores,
                         "head_out": head_out, "diff_rms": diff_rms,
                         "diff_scale": diff_scale, "mix_turn": mix_turn}

                def add_to_resid(c, parity, n):
                    complete(n)
                    for t in range(NT):
                        part = resid[:, t, c * NCH:(c + 1) * NCH]
                        vec.tensor_tensor(part, bank[2 * parity + t][:, :], part, ALU.add)\
                           .then_inc(x_added, 1)

                norm("norm1", 0)
                for n in range(U_FF):
                    if n >= U_OUT and (n - U_OUT) % 8 >= 6:
                        pair, c = (n - U_OUT) // 8, (n - U_OUT) % 2
                        add_to_resid(2 * pair + c, c, n)
                    for name, arg in HOOKS.get(n, []):
                        if name in steps:
                            steps[name](arg)
                    if n < U_FF - LEAD + 1:
                        rest_of_unit(layer * QUADS + (n + LEAD) // 4, n + LEAD)
                norm("norm2", 1)

                def ff_turn(f):
                    for b in (4, 5):
                        vec.wait_ge(bank_full[b], layer * USES[b] + ROUND[("ff_turn", 0)][b] + f + 1)
                        vec.wait_ge(ft_hi_made, layer * (2 * FF_CHUNKS) + 2 * f + b - 3)
                        at = bass.ds(f * 4 + 2 * (b - 4), 2)
                        vec.tensor_tensor(f_lo[:, at, :].rearrange("p a b -> p (a b)"), bank[b][:, :],
                                          f_hi[:, at, :].rearrange("p a b -> p (a b)").bitcast(F32), ALU.subtract)\
                           .then_inc(bank_free[b], 1)

                def ff_chunk(f, first):
                    for i in range(8):
                        rest_of_unit(layer * QUADS + (U_FF + i + LEAD) // 4 + 2 * f, U_FF + i + LEAD)
                        if i == 1 and not first:
                            ff_turn(f - 1)
                        if i == 7:
                            if first:
                                need(rstd_made, len(POW), POW["norm2"] + 1)
                            vec.wait_ge(used[3], layer * QUADS + (U_FF + 7) // 4 + 2 + 2 * f)
                            for t in range(NT):
                                vec.wait_ge(silu_made, layer * (FF_CHUNKS * NT) + f * NT + t + 1)
                                vec.scalar_tensor_tensor(act_sb[:, t, :], bank[2 + t][:, :], rstd_x[:, t:t + 1],
                                                         act_sb[:, t, :], ALU.mult, ALU.mult)\
                                   .then_inc(act_made, 1)

                ff_chunk(0, True)
                with vec.Fori(1, FF_CHUNKS) as f:
                    ff_chunk(f, False)
                for n in range(U_DOWN, UNITS):
                    i = n - U_DOWN
                    if i % len(DOWN_KT) == len(DOWN_KT) - 1:
                        c = i // len(DOWN_KT)
                        add_to_resid(c, c % 2, n)
                    if n < UNITS - LEAD + 1:
                        rest_of_unit(layer * QUADS + (n + LEAD) // 4, n + LEAD)
                    if i == 1:
                        ff_turn(FF_CHUNKS - 1)
                assert count[0] == VEC_LINKS, count[0]

            vec.wait_ge(setup_in, 48)
            vec.wait_ge(x_added, 16 * DEPTH + 8)
            halves_of_row = slice(0, D_MODEL // 2), slice(D_MODEL // 2, D_MODEL)
            vec.tensor_tensor(xn[:, 1, halves_of_row[0]], resid[:, 1, halves_of_row[0]], last_gain[:, halves_of_row[0]],
                              ALU.mult).then_inc(gain_taken, 1)
            vec.wait_ge(squared, 16 * DEPTH + 8)
            vec.tensor_reduce(ms[:, 0:NT], ssq[:, :, :], AX.X, ALU.add).then_inc(vec_chain, 1)
            vec.wait_ge(vec_chain, DEPTH * VEC_LINKS + 1)
            vec.tensor_scalar(ms[:, 0:NT], ms[:, 0:NT], 1.0 / D_MODEL, EPS, ALU.mult, ALU.add).then_inc(ms_made, 1)
            vec.tensor_tensor(xn[:, 1, halves_of_row[1]], resid[:, 1, halves_of_row[1]], last_gain[:, halves_of_row[1]],
                              ALU.mult).then_inc(gain_taken, 1)
            vec.wait_ge(rstd_made, DEPTH * len(POW) + 1)
            for half in halves_of_row:
                vec.scalar_tensor_tensor(xn[:, 0, half], resid[:, 0, half], rstd_x[:, 0:1], last_gain[:, half],
                                         ALU.mult, ALU.mult).then_inc(xn_vec, 1)


def build(nc, shapes):
    aps = {name: nc.dram_tensor(f"in_{name}", shape, dt, kind="ExternalInput").ap() for name, (shape, dt) in shapes.items()}
    out = nc.dram_tensor("out_0_dram", (SEQ, D_MODEL), F32, kind="ExternalOutput").ap()
    program(nc, out=out, **aps)


def kernel(**inputs):
    import concourse.bacc as bacc
    from concourse.bass_utils import run_bass_kernel_spmd

    a = {k: np.ascontiguousarray(v) for k, v in inputs.items()}

    def columns(v, n):
        return v.reshape(DEPTH, n, P).transpose(2, 0, 1)

    consts = np.zeros((P, K_END), np.float32)
    consts[:, K_ID:K_ID + P] = np.eye(P)
    consts[:, K_INV:K_INV + 32] = 1.0 / ROPE_THETA ** (np.arange(0, MLA_ROPE, 2, dtype=np.float32) / MLA_ROPE)
    for layer in range(DEPTH):
        first = 0.8 - 0.6 * np.exp(-0.3 * layer)
        consts[:, K_LAM + 2 * layer:K_LAM + 2 * layer + 2] = first, 1.0 - first
    key, query = np.arange(P)[:, None], np.arange(P)[None, :]
    levels = np.zeros((P, len(LEVELS), P), np.float32)
    for i, size in enumerate(LEVELS):
        if size:
            levels[:, i] = (key // (2 * size) == query // (2 * size)) & (key % (2 * size) < size) & (query % (2 * size) >= size)
        else:
            levels[:, i] = key == query
    causal = np.zeros((P, 2 * P), np.float32)
    causal[:, P:] = np.where(query <= key, 0.0, NEG)

    arrays = {
        "x": a["x"].reshape(SEQ, D_MODEL),
        "positions": a["positions"].reshape(NT, P).T,
        "w_in": a["w_in"], "w_q_b": a["mla_w_q_b"], "w_kv_b": a["mla_w_kv_b"], "w_out": a["w_out"],
        "w_gate": a["w_gate"], "w_up": a["w_up"], "w_down": a["w_down"], "gate_w": a["gla_gate_w"],
        "gains": np.concatenate([columns(a["attn_norm"], KT), columns(a["ffn_norm"], KT), columns(a["mla_q_norm"], 4),
                                 columns(a["mla_kv_norm"], 2), columns(a["gla_gate_b"], 2)], axis=2),
        "rows": np.concatenate([a["diff_subln"], a["gla_norm"], a["diff_lambda_q1"], a["diff_lambda_q2"],
                                a["diff_lambda_k1"], a["diff_lambda_k2"]], axis=1).reshape(DEPTH, 1, W_END),
        "final_norm": a["final_norm"].reshape(1, D_MODEL),
        "consts": consts, "levels": levels, "causal": causal,
    }
    arrays = {k: np.ascontiguousarray(v) for k, v in arrays.items()}
    nc = bacc.Bacc("TRN2", target_bir_lowering=False, num_devices=1)
    build(nc, {k: (v.shape, mybir.dt.from_np(v.dtype)) for k, v in arrays.items()})
    r = run_bass_kernel_spmd(nc, [{f"in_{k}": v for k, v in arrays.items()}], core_ids=[0])
    return r.results[0]["out_0_dram"].reshape(1, SEQ, D_MODEL)
```
